# Optimizing a Trainium2 kernel written in Bass

```python
import math
import jax, jax.numpy as jnp
from jax import lax
import numpy as np

D_MODEL = 1024
BATCH = 1
SEQ = 512
DEPTH = 2

RMS_EPS = 1e-6
LN_EPS = 1e-5
N_EVEN = (DEPTH + 1) // 2
N_ODD = DEPTH // 2
CONV_CH = D_MODEL // 2
CONV_WIDTH = 31
GDN_HEADS = 4
GDN_DK = 128
GDN_DV = 128
GDN_KEY = GDN_HEADS * GDN_DK
GDN_VAL = GDN_HEADS * GDN_DV
SHORT_CONV = 4
CHUNK = 64
IN0_COLS = 2 * CONV_CH + 2 * GDN_KEY + 2 * GDN_VAL + 2 * GDN_HEADS
SB_HEADS = 16
SB_HD = D_MODEL // SB_HEADS
SB_BLOCK = 128
D_FF = 2816
FFN_CONV = 3

kernel_name = 'hybrid_conformer_gdn_stickbreak_convffn'

def rmsnorm(x, w):
    xf = x.astype(jnp.float32)
    y = xf * lax.rsqrt(jnp.mean(xf * xf, axis=-1, keepdims=True) + RMS_EPS)
    return (y * w.astype(jnp.float32)).astype(x.dtype)

def layernorm(x, w, b):
    xf = x.astype(jnp.float32)
    mu = jnp.mean(xf, axis=-1, keepdims=True)
    xc = xf - mu
    y = xc * lax.rsqrt(jnp.mean(xc * xc, axis=-1, keepdims=True) + LN_EPS)
    return (y * w.astype(jnp.float32) + b.astype(jnp.float32)).astype(x.dtype)

def l2norm(x):
    return x * lax.rsqrt(jnp.sum(x * x, axis=-1, keepdims=True) + RMS_EPS)

def causal_dwconv(x, w):
    K, C = w.shape
    return lax.conv_general_dilated(
        x, w[:, None, :], window_strides=(1,), padding=[(K - 1, 0)],
        dimension_numbers=('NWC', 'WIO', 'NWC'), feature_group_count=C)

def conformer_conv(a_val, a_gate, dw_w, dw_b, ln_w, ln_b):
    h = a_val * jax.nn.sigmoid(a_gate)
    h = causal_dwconv(h, dw_w) + dw_b
    h = layernorm(h, ln_w, ln_b)
    return jax.nn.silu(h)

def chunk_gated_delta_rule(q, k, v, g, beta):
    B, L, H, DK = q.shape
    DV = v.shape[-1]
    N = L // CHUNK

    def to_chunks(t):
        return t.reshape(B, N, CHUNK, H, -1).transpose(1, 0, 3, 2, 4)

    q_c, k_c, v_c = to_chunks(q), to_chunks(k), to_chunks(v)
    g_c = g.reshape(B, N, CHUNK, H).transpose(1, 0, 3, 2)
    b_c = beta.reshape(B, N, CHUNK, H).transpose(1, 0, 3, 2)
    g_cum = jnp.cumsum(g_c, axis=-1)
    idx = jnp.arange(CHUNK)
    incl = idx[:, None] >= idx[None, :]
    strict = idx[:, None] > idx[None, :]
    decay = jnp.exp(jnp.where(incl, g_cum[..., :, None] - g_cum[..., None, :], -jnp.inf))
    k_beta = k_c * b_c[..., None]
    v_beta = v_c * b_c[..., None]
    kk = jnp.einsum('nbhid,nbhjd->nbhij', k_beta, k_c) * decay
    lower = jnp.where(strict, kk, 0.0)
    u = lax.linalg.triangular_solve(lower, v_beta, left_side=True, lower=True, unit_diagonal=True)
    w = lax.linalg.triangular_solve(lower, k_beta * jnp.exp(g_cum)[..., None],
                                    left_side=True, lower=True, unit_diagonal=True)
    qk = jnp.einsum('nbhid,nbhjd->nbhij', q_c, k_c) * decay
    g_last = g_cum[..., -1]
    k_tail = k_c * jnp.exp(g_last[..., None] - g_cum)[..., None]
    q_dec = q_c * jnp.exp(g_cum)[..., None]

    def step(S, inp):
        qd, qk_i, u_i, w_i, kt, gl = inp
        v_new = u_i - jnp.einsum('bhcd,bhde->bhce', w_i, S)
        o = jnp.einsum('bhcd,bhde->bhce', qd, S) + jnp.einsum('bhij,bhje->bhie', qk_i, v_new)
        S = S * jnp.exp(gl)[..., None, None] + jnp.einsum('bhcd,bhce->bhde', kt, v_new)
        return S, o

    S0 = jnp.zeros((B, H, DK, DV), jnp.float32)
    _, o = lax.scan(step, S0, (q_dec, qk, u, w, k_tail, g_last))
    return o.transpose(1, 0, 3, 2, 4).reshape(B, L, H, DV)

def gated_deltanet(q, k, v, z, a, b, conv_w, a_log, dt_bias, onorm_w):
    Bsz, L, _ = q.shape
    dtype = q.dtype
    qkv = jax.nn.silu(causal_dwconv(jnp.concatenate([q, k, v], axis=-1), conv_w))
    qkv = qkv.astype(jnp.float32)
    qf = qkv[..., :GDN_KEY].reshape(Bsz, L, GDN_HEADS, GDN_DK)
    kf = qkv[..., GDN_KEY:2 * GDN_KEY].reshape(Bsz, L, GDN_HEADS, GDN_DK)
    vf = qkv[..., 2 * GDN_KEY:].reshape(Bsz, L, GDN_HEADS, GDN_DV)
    qf = l2norm(qf) * (GDN_DK ** -0.5)
    kf = l2norm(kf)
    beta = jax.nn.sigmoid(b.astype(jnp.float32))
    g = -jnp.exp(a_log.astype(jnp.float32)) * jax.nn.softplus(
        a.astype(jnp.float32) + dt_bias.astype(jnp.float32))
    o = chunk_gated_delta_rule(qf, kf, vf, g, beta)
    o = rmsnorm(o, onorm_w) * jax.nn.silu(z.astype(jnp.float32).reshape(Bsz, L, GDN_HEADS, GDN_DV))
    return o.reshape(Bsz, L, GDN_VAL).astype(dtype)

def conv_deltanet_mixer(h, w_in, a_dw_w, a_dw_b, a_ln_w, a_ln_b,
                        gdn_conv_w, gdn_a_log, gdn_dt_bias, gdn_onorm_w, w_out):
    p = h @ w_in
    c0 = CONV_CH
    c1 = c0 + CONV_CH
    c2 = c1 + GDN_KEY
    c3 = c2 + GDN_KEY
    c4 = c3 + GDN_VAL
    c5 = c4 + GDN_VAL
    c6 = c5 + GDN_HEADS
    a_val, a_gate, q, k, v, z, a, b = jnp.split(p, [c0, c1, c2, c3, c4, c5, c6], axis=-1)
    y_a = conformer_conv(a_val, a_gate, a_dw_w, a_dw_b, a_ln_w, a_ln_b)
    y_b = gated_deltanet(q, k, v, z, a, b, gdn_conv_w, gdn_a_log, gdn_dt_bias, gdn_onorm_w)
    return jnp.concatenate([y_a, y_b], axis=-1) @ w_out

def stick_breaking_attention(q, k, v):
    B, L, H, D = q.shape
    dtype = q.dtype
    nb = L // SB_BLOCK
    qf = q.astype(jnp.float32) * (D ** -0.5)
    kf = k.astype(jnp.float32)
    vf = v.astype(jnp.float32)
    qb = qf.reshape(B, nb, SB_BLOCK, H, D).transpose(1, 0, 3, 2, 4)
    kpos = jnp.arange(L)

    def block(args):
        qi, i = args
        z = jnp.einsum('bhqd,bkhd->bhqk', qi, kf)
        qpos = i * SB_BLOCK + jnp.arange(SB_BLOCK)
        causal = kpos[None, :] < qpos[:, None]
        neg_log_1mb = jnp.where(causal, jax.nn.softplus(z), 0.0)
        tail = lax.cumsum(neg_log_1mb, axis=3, reverse=True) - neg_log_1mb
        log_a = -jax.nn.softplus(-z) - tail
        att = jnp.where(causal, jnp.exp(log_a), 0.0)
        return jnp.einsum('bhqk,bkhd->bqhd', att, vf)

    o = lax.map(block, (qb, jnp.arange(nb)))
    return o.transpose(1, 0, 2, 3, 4).reshape(B, L, H * D).astype(dtype)

def stick_breaking_mixer(h, w_qkv, w_out):
    B, L, _ = h.shape
    qkv = (h @ w_qkv).reshape(B, L, 3, SB_HEADS, SB_HD)
    o = stick_breaking_attention(qkv[:, :, 0], qkv[:, :, 1], qkv[:, :, 2])
    return o @ w_out

def conv_ffn(h, w_up, conv_w, w_down):
    u = causal_dwconv(h @ w_up, conv_w)
    gate, val = jnp.split(u, 2, axis=-1)
    return (jax.nn.silu(gate) * val) @ w_down

def setup_inputs(seed: int = 0) -> dict:
    key = jax.random.key(seed)
    ks = jax.random.split(key, 24)
    nrm = jax.random.normal
    f32 = jnp.float32
    x = nrm(ks[0], (BATCH, SEQ, D_MODEL), f32)
    mix0_norm = 1.0 + 0.02 * nrm(ks[1], (N_EVEN, D_MODEL), f32)
    w_in0 = nrm(ks[2], (N_EVEN, D_MODEL, IN0_COLS), f32) * D_MODEL ** -0.5
    a_dw_w = nrm(ks[3], (N_EVEN, CONV_WIDTH, CONV_CH), f32) * CONV_WIDTH ** -0.5
    a_dw_b = 0.02 * nrm(ks[4], (N_EVEN, CONV_CH), f32)
    a_ln_w = 1.0 + 0.02 * nrm(ks[5], (N_EVEN, CONV_CH), f32)
    a_ln_b = 0.02 * nrm(ks[6], (N_EVEN, CONV_CH), f32)
    gdn_conv_w = nrm(ks[7], (N_EVEN, SHORT_CONV, 2 * GDN_KEY + GDN_VAL), f32) * SHORT_CONV ** -0.5
    gdn_a_log = jnp.log(jax.random.uniform(ks[8], (N_EVEN, GDN_HEADS), f32, 1.0, 16.0))
    dt = jnp.exp(jax.random.uniform(ks[9], (N_EVEN, GDN_HEADS), f32)
                 * (math.log(0.1) - math.log(0.001)) + math.log(0.001))
    gdn_dt_bias = dt + jnp.log(-jnp.expm1(-dt))
    gdn_onorm_w = 1.0 + 0.02 * nrm(ks[10], (N_EVEN, GDN_DV), f32)
    w_out0 = nrm(ks[11], (N_EVEN, CONV_CH + GDN_VAL, D_MODEL), f32) * (CONV_CH + GDN_VAL) ** -0.5
    mix1_norm = 1.0 + 0.02 * nrm(ks[12], (N_ODD, D_MODEL), f32)
    w_qkv1 = nrm(ks[13], (N_ODD, D_MODEL, 3 * SB_HEADS * SB_HD), f32) * D_MODEL ** -0.5
    w_out1 = nrm(ks[14], (N_ODD, SB_HEADS * SB_HD, D_MODEL), f32) * (SB_HEADS * SB_HD) ** -0.5
    ffn_norm = 1.0 + 0.02 * nrm(ks[15], (DEPTH, D_MODEL), f32)
    w_up = nrm(ks[16], (DEPTH, D_MODEL, 2 * D_FF), f32) * D_MODEL ** -0.5
    ffn_conv_w = nrm(ks[17], (DEPTH, FFN_CONV, 2 * D_FF), f32) * FFN_CONV ** -0.5
    w_down = nrm(ks[18], (DEPTH, D_FF, D_MODEL), f32) * D_FF ** -0.5
    final_norm = 1.0 + 0.02 * nrm(ks[19], (D_MODEL,), f32)
    return {'x': x, 'mix0_norm': mix0_norm, 'w_in0': w_in0, 'a_dw_w': a_dw_w, 'a_dw_b': a_dw_b,
            'a_ln_w': a_ln_w, 'a_ln_b': a_ln_b, 'gdn_conv_w': gdn_conv_w, 'gdn_a_log': gdn_a_log,
            'gdn_dt_bias': gdn_dt_bias, 'gdn_onorm_w': gdn_onorm_w, 'w_out0': w_out0,
            'mix1_norm': mix1_norm, 'w_qkv1': w_qkv1, 'w_out1': w_out1,
            'ffn_norm': ffn_norm, 'w_up': w_up, 'ffn_conv_w': ffn_conv_w, 'w_down': w_down,
            'final_norm': final_norm}

def reference(x, mix0_norm, w_in0, a_dw_w, a_dw_b, a_ln_w, a_ln_b, gdn_conv_w, gdn_a_log,
              gdn_dt_bias, gdn_onorm_w, w_out0, mix1_norm, w_qkv1, w_out1,
              ffn_norm, w_up, ffn_conv_w, w_down, final_norm):
    for layer in range(DEPTH):
        j = layer // 2
        if layer % 2 == 0:
            x = x + conv_deltanet_mixer(rmsnorm(x, mix0_norm[j]), w_in0[j], a_dw_w[j], a_dw_b[j],
                                        a_ln_w[j], a_ln_b[j], gdn_conv_w[j], gdn_a_log[j],
                                        gdn_dt_bias[j], gdn_onorm_w[j], w_out0[j])
        else:
            x = x + stick_breaking_mixer(rmsnorm(x, mix1_norm[j]), w_qkv1[j], w_out1[j])
        x = x + conv_ffn(rmsnorm(x, ffn_norm[layer]), w_up[layer], ffn_conv_w[layer], w_down[layer])
    return rmsnorm(x, final_norm)


_drawn_inputs = setup_inputs


def setup_inputs(seed=0):
    import zlib

    import numpy as np

    out = dict(_drawn_inputs(seed))
    spreads = {}
    factors = {'mix0_norm': 2.918,
     'a_dw_b': 3.003,
     'a_ln_w': 17.264,
     'a_ln_b': 17.615,
     'gdn_onorm_w': 5.409,
     'mix1_norm': 5.045,
     'ffn_norm': 2.95,
     'final_norm': 8.05}
    for name, (base, spread) in spreads.items():
        noise = np.random.default_rng([zlib.crc32(name.encode()), seed]).standard_normal(out[name].shape)
        drawn = base * np.exp(spread * noise) if base else spread * noise
        out[name] = __import__('jax').numpy.asarray(drawn.astype(out[name].dtype))
    for name, factor in factors.items():
        out[name] = (out[name] * factor).astype(out[name].dtype)
    return out
```

```python
import concourse.bass as bass
from concourse import mybir
from contextlib import ExitStack
from collections import namedtuple

P = 128
T = 512
D = 1024
KT = D // P
FF = 2816
FT = FF // P
DOWN = (8, 8, 6)
C31 = 31
CA = 4
NH = 4
NC = T // P
LEVELS = 7
PAIRS = 8
NB0, NBO, NBU, NBD, NBQ = 25, 8, 2 * FT, 24, 24
RING = 3

PAR = {}
_n = 0
for _name, _w in (("norm", 5 * KT), ("dwb", CA), ("lnw", CA), ("lnb", CA), ("onorm", 1), ("c4", 12 * 4),
                  ("c31", CA * C31), ("fc0", 2 * FT * 3), ("fc1", 2 * FT * 3), ("dtb", NH), ("alog", NH)):
    PAR[_name] = _n
    _n += _w
NPAR = _n
IDENT, UPPER, AFTER, ONES, LEV0, NTRI, NEG = 0, 1, 2, 3, 4, 11, 12
NCONST = 13


def trunk(nc, xT, w_ab, w_in0, w_out0, w_up0, w_dn0, w_qkv, w_out1, w_up1, w_dn1, par_d, const_d, outT):
    f32, f32r = mybir.dt.float32, mybir.dt.float32r
    ACT, ALU = mybir.ActivationFunctionType, mybir.AluOpType
    ctx = ExitStack()
    with ctx:
        def sb(name, shape, dt=f32, c=ctx):
            return c.enter_context(nc.sbuf_tensor(name, shape, dt))

        def sem(name):
            return ctx.enter_context(nc.semaphore(name))

        x = sb("x", [P, KT, T])
        h_hi, h_lo = sb("h_hi", [P, KT, T], f32r), sb("h_lo", [P, KT, T], f32r)
        stage = sb("stage", [P, RING, D])
        w_hi, w_lo = sb("w_hi", [P, RING, D], f32r), sb("w_lo", [P, RING, D], f32r)
        rms = sb("rms", [P, T])
        ssq = sb("ssq", [P, T])
        sq2 = sb("sq2", [P, 2, T])
        par = sb("par", [P, NPAR])
        const = sb("const", [P, NCONST, P])
        eps = sb("eps", [P, 4])
        za = ExitStack()
        yb_hi, yb_lo = sb("yb_hi", [P, NH, T], f32r, za), sb("yb_lo", [P, NH, T], f32r, za)
        ya_hi, ya_lo = sb("ya_hi", [P, CA, T], f32r, za), sb("ya_lo", [P, CA, T], f32r, za)
        hb = sb("hb", [P, CA, T + C31 - 1], f32, za)
        tc = sb("tc", [P, CA, T], f32, za)
        sig = sb("sig", [P, T], f32, za)
        cb = sb("cb", [P, T + 3], f32, za)
        sk, sq, sv = (sb(n, [P, T], f32, za) for n in ("sk", "sq", "sv"))
        sqb = sb("sqb", [P, 2, T], f32, za)
        rkq = sb("rkq", [P, 2, T], f32, za)
        kn, qn = sb("kn", [P, NC, P], f32, za), sb("qn", [P, NC, P], f32, za)
        gU, eDn, qkd, qd = (sb(n, [P, NC, P], f32, za) for n in ("gU", "eDn", "qkd", "qd"))
        X, Y, T2, ktail, kbg, vb, nWT = (sb(n, [P, NC, P], f32, za)
                                         for n in ("X", "Y", "T2", "ktail", "kbg", "vb", "nWT"))
        vnew, S = sb("vnew", [P, P], f32, za), sb("S", [P, P], f32, za)
        oc, ro = sb("oc", [P, NH, T], f32, za), sb("ro", [P, T], f32, za)
        ab = sb("ab", [8, T], f32, za)
        sm = sb("sm", [P, 12, NC * NH], f32, za)
        za.close()
        zf = ExitStack()
        p_hi, p_lo = sb("p_hi", [P, FT, T], f32r, zf), sb("p_lo", [P, FT, T], f32r, zf)
        ug, uv = sb("ug", [P, T + 2], f32, zf), sb("uv", [P, T + 2], f32, zf)
        tg, tv = sb("tg", [P, 3, T], f32, zf), sb("tv", [P, 3, T], f32, zf)
        zf.close()
        zt = ExitStack()
        y1_hi, y1_lo = sb("y1_hi", [P, PAIRS, T], f32r, zt), sb("y1_lo", [P, PAIRS, T], f32r, zt)
        q_hi, q_lo = sb("q_hi", [P, 2, T], f32r, zt), sb("q_lo", [P, 2, T], f32r, zt)
        k_hi, k_lo = sb("k_hi", [P, 2, T], f32r, zt), sb("k_lo", [P, 2, T], f32r, zt)
        v_hi, v_lo = sb("v_hi", [P, 2, NC, 2, P], f32r, zt), sb("v_lo", [P, 2, NC, 2, P], f32r, zt)
        pf = sb("pf", [P, T], f32, zt)
        vT = sb("vT", [P, T], f32, zt)
        AW = 1280
        t_ = sb("t_", [P, 2, AW], f32, zt)
        s_hi, s_lo = sb("s_hi", [P, 2, AW], f32r, zt), sb("s_lo", [P, 2, AW], f32r, zt)
        ntri, nones, negm, identr = (sb(n, [P, P], f32r, zt) for n in ("ntri", "nones", "negm", "identr"))
        zt.close()

        B = [ctx.enter_context(nc.psum_tensor(f"bank{i}", [P, T], f32)) for i in range(8)]

        names = (
            "x_in0 x_in1 par_in const_in out_w w_split_hi w_split_lo block_done x_new "
            "h_hi_done h_lo_done sq_done ssq_done stat_mm rms_ln rms_done ones_set halo_set "
            "a_free ab_t sg_beta sg_xa sg_abs sg_e sg_l sg_sp "
            "sg_ea sg_g sg_bg cols_mm cols_exp sig_done hb_done "
            "cf0 cf_tap c0_done ctap silu_done sqh_done kqss_mm kq_ln "
            "kq_r kn_done qn_done kt_mm vt_mm ktail_done kbg_done vb_done kk_mm "
            "qk_mm gu_done dn_mm dt_mm gb_mm edn_done edt_done egb_done a1_done "
            "a2_done qkd_done qkd_masked qd_done t_mm t2_done xm_mm x_done ym_mm "
            "y_done wt_mm wt_done v_mm v_done o_mm s_mm s_done oc_done "
            "osq_done oss_mm o_ln o_r on_done sz_done yb_f yb_hid "
            "yb_lod mu_mm xc_done csq_done var_mm c_ln c_r cn_done ya_f "
            "ya_hid ya_lod up_free tap0 tap1 silu_f prod prod_hi prod_lo "
            "halo_f consts_r q_f q_hid q_lod k_f k_hid k_lod v_f "
            "vt2_mm v_hid v_lod z_mm za_done ze_done zl_done sp_done "
            "sp_hid sp_lod cum_mm att_done att_hid att_lod av_mm y1_hid y1_lod "
            "vp_zero out_f "
        )
        s = namedtuple("Sems", names)(*(sem(n) for n in names.split()))
        w_in = [sem(f"w_in{i}") for i in range(RING)]

        def col(name, i=0):
            return par[:, PAR[name] + i:PAR[name] + i + 1]

        def cm(i):
            return const[:, i, :]

        def bc(ap):
            return ap.unsqueeze(1).to_broadcast([P, NC, P])

        def tok(i, h):
            return sm[:, i, :].rearrange("p (c h) -> p c h", h=NH)[:, :, h:h + 1].to_broadcast([P, NC, P])

        def w_load(sp, dram, b, n, r=None, m=0):
            if r is None and b >= RING:
                sp.wait_ge(s.w_split_lo, b - RING + 1)
            if r is not None:
                sp.wait_ge(s.w_split_lo, r * m + (b - RING + 1))
            sp.dma_start(stage[:, b % RING, 0:n], dram).then_inc(w_in[b % RING], 16)

        def w_hi_of(act, b, n, r=None, m=0):
            if r is None:
                act.wait_ge(w_in[b % RING], 16 * (b // RING + 1))
                if b >= RING:
                    act.wait_ge(s.block_done, b - RING + 1)
            else:
                act.wait_ge(w_in[b % RING], r * (16 * m // RING) + 16 * (b // RING + 1))
                act.wait_ge(s.block_done, r * m + (b - RING + 1))
            nc.scalar.activation(w_hi[:, b % RING, 0:n], stage[:, b % RING, 0:n], ACT.Copy).then_inc(s.w_split_hi, 1)

        def w_lo_of(dve, b, n, r=None, m=0):
            dve.wait_ge(s.w_split_hi, (b + 1) if r is None else r * m + (b + 1))
            nc.vector.tensor_tensor(w_lo[:, b % RING, 0:n], stage[:, b % RING, 0:n],
                                    w_hi[:, b % RING, 0:n].bitcast(f32), ALU.subtract).then_inc(s.w_split_lo, 1)

        def mm3(out, whi, wlo, ahi, alo, start, stop):
            nc.tensor.matmul(out, wlo, ahi, start=start, stop=False, skip_group_check=True)
            nc.tensor.matmul(out, whi, alo, start=False, stop=False, skip_group_check=True)
            return nc.tensor.matmul(out, whi, ahi, start=False, stop=stop, skip_group_check=True)

        def w_wait(pe, b, r=None, m=0):
            pe.wait_ge(s.w_split_lo, (b + 1) if r is None else r * m + (b + 1))

        def gemm(bank, b, k0, k1, ahi, alo, first, last, mcols=P, a0=0):
            for k in range(k0, k1):
                mm = mm3(bank[0:mcols, :], w_hi[:, b % RING, k * mcols:(k + 1) * mcols],
                         w_lo[:, b % RING, k * mcols:(k + 1) * mcols], ahi[:, a0 + k, :], alo[:, a0 + k, :],
                         first and k == k0, last and k == k1 - 1)
            return mm

        def norm_act(act, n, k, split, r=None, m=0):
            kk, c = (k, KT * n + k) if r is None else (r * m + k, r * m + (KT * n + k))
            act.wait_ge(s.x_new, c + 1)
            if split:
                w = par[:, bass.ds(PAR["norm"] + KT * n + kk, 1)] if r is not None else col("norm", KT * n + k)
                nc.scalar.activation(h_hi[:, kk, :] if r is None else h_hi[:, bass.ds(kk, 1), :].rearrange("p o t -> p (o t)"),
                                     x[:, kk, :] if r is None else x[:, bass.ds(kk, 1), :].rearrange("p o t -> p (o t)"),
                                     ACT.Copy, scale=w).then_inc(s.h_hi_done, 1)
            if not (r is None and c < 2):
                act.wait_ge(s.ssq_done, c - 1)
            nc.scalar.activation(sq2[:, k % 2, :], x[:, kk, :] if r is None else x[:, bass.ds(kk, 1), :].rearrange("p o t -> p (o t)"),
                                 ACT.Square).then_inc(s.sq_done, 1)

        def norm_lo(dve, n, k, r=None, m=0):
            kk, c = (k, KT * n + k) if r is None else (r * m + k, r * m + (KT * n + k))
            dve.wait_ge(s.h_hi_done, c + 1)
            if r is None:
                nc.vector.scalar_tensor_tensor(h_lo[:, k, :], x[:, k, :], col("norm", KT * n + k),
                                               h_hi[:, k, :].bitcast(f32), ALU.mult, ALU.subtract).then_inc(s.h_lo_done, 1)
            else:
                g = lambda a: a[:, bass.ds(kk, 1), :].rearrange("p o t -> p (o t)")
                nc.vector.scalar_tensor_tensor(g(h_lo), g(x), par[:, bass.ds(PAR["norm"] + KT * n + kk, 1)],
                                               g(h_hi).bitcast(f32), ALU.mult, ALU.subtract).then_inc(s.h_lo_done, 1)

        def norm_pool(pool, n):
            for k in range(KT):
                c = KT * n + k
                pool.wait_ge(s.sq_done, c + 1)
                if k == 0:
                    if n:
                        pool.wait_ge(s.stat_mm, n)
                    nc.gpsimd.tensor_scalar(ssq[:], sq2[:, 0, :], 1.0, None, ALU.mult).then_inc(s.ssq_done, 1)
                else:
                    pool.wait_ge(s.ssq_done, c)
                    nc.gpsimd.tensor_tensor(ssq[:], ssq[:], sq2[:, k % 2, :], ALU.add).then_inc(s.ssq_done, 1)

        def stat_pe(pe, n, bank):
            pe.wait_ge(s.ssq_done, KT * (n + 1))
            nc.tensor.matmul(bank[:], cm(ONES), ssq[:], start=True, stop=True).then_inc(s.stat_mm, 1)

        def stat_act(act, n, bank):
            act.preload_act_table_set("natural_log_exp_and_others")
            act.wait_ge(s.stat_mm, n + 1)
            nc.scalar.activation(rms[:], bank[:], ACT.Ln, bias=eps[:, 0:1], scale=1.0 / D).then_inc(s.rms_ln, 1)
            act.wait_ge(s.rms_ln, n + 1)
            nc.scalar.activation(rms[:], rms[:], ACT.Exp, scale=-0.5).then_inc(s.rms_done, 1)

        ORDER = [("ab", 0)] + [(c, i) for i in range(CA) for c in ("g", "v")] + \
                [(c, h) for h in range(NH) for c in ("k", "q", "u")] + [("z", h) for h in range(NH)]
        GB = {kind: g for g, kind in enumerate(ORDER)}
        n_of = lambda g: 64 if g == 0 else D

        def nblk(b):
            if b == 0:
                return 64
            for size, kind in ((NB0 + NBO, 0), (NBU, 0), (NBD, 1), (NBQ + NBO, 0), (NBU, 0), (NBD, 1)):
                if b < size:
                    return DOWN[b % 3] * P if kind else D
                b -= size
            return 0
        BO0 = NB0
        BU0 = BO0 + NBO
        BD0 = BU0 + NBU
        BQ = BD0 + NBD
        BO1 = BQ + NBQ
        BU1 = BO1 + NBO
        BD1 = BU1 + NBU
        BEND = BD1 + NBD

        TAPS = CA * (C31 - 1)
        tap_plan = [0] * (NB0 + 1)
        for g in range(4, 9):
            tap_plan[g] = 4
        for g in range(9, NB0):
            tap_plan[g] = 3
        tap_plan[NB0] = TAPS - sum(tap_plan)
        tap_at = [sum(tap_plan[:g]) for g in range(NB0 + 1)] + [TAPS]

        def a_dve_taps(dve, n0, n1):
            for n in range(n0, n1):
                i, j = n // (C31 - 1), n % (C31 - 1) + 1
                if j == 1:
                    dve.wait_ge(s.cf0, i + 1)
                else:
                    dve.wait_ge(s.cf_tap, n)
                nc.vector.scalar_tensor_tensor(tc[:, i, :], hb[:, i, j:j + T], col("c31", i * C31 + j), tc[:, i, :],
                                               ALU.mult, ALU.add).then_inc(s.cf_tap, 1)

        def a_post_dve(dve, g):
            kind, i = ORDER[g]
            bank = B[g % 3]
            dve.wait_ge(s.block_done, g + 1)
            if g == 0:
                dve.wait_ge(s.rms_done, 1)
                nc.vector.tensor_tensor(ab[:], bank[0:8, :], rms[0:8, :], ALU.mult).then_inc(s.a_free, 1)
            elif kind == "g":
                if i:
                    dve.wait_ge(s.hb_done, i)
                nc.vector.tensor_tensor(sig[:], bank[:], rms[:], ALU.mult).then_inc(s.a_free, 1)
            elif kind == "v":
                nc.vector.tensor_tensor(hb[:, i, C31 - 1:], bank[:], rms[:], ALU.mult).then_inc(s.a_free, 1)
                dve.wait_ge(s.a_free, g + 1)
                dve.wait_ge(s.sig_done, i + 1)
                nc.vector.tensor_tensor(hb[:, i, C31 - 1:], hb[:, i, C31 - 1:], sig[:], ALU.mult).then_inc(s.hb_done, 1)
            elif kind in "kqu":
                m = 3 * i + "kqu".index(kind)
                dst = (sk, sq, sv)["kqu".index(kind)]
                if m:
                    dve.wait_ge(s.ctap, 3 * m)
                nc.vector.tensor_tensor(cb[:, 3:], bank[:], rms[:], ALU.mult).then_inc(s.a_free, 1)
                tile = {"k": NH, "q": 0, "u": 2 * NH}[kind] + i
                dve.wait_ge(s.c0_done, m + 1)
                for j in range(1, 4):
                    if j > 1:
                        dve.wait_ge(s.ctap, 3 * m + j - 1)
                    nc.vector.scalar_tensor_tensor(dst[:], cb[:, j:j + T], col("c4", tile * 4 + j), dst[:],
                                                   ALU.mult, ALU.add).then_inc(s.ctap, 1)
            else:
                if i:
                    dve.wait_ge(s.yb_f, i)
                nc.vector.tensor_tensor(sig[:], bank[:], rms[:], ALU.mult).then_inc(s.a_free, 1)

        def a_post_act(act, g):
            kind, i = ORDER[g]
            if kind == "g":
                act.wait_ge(s.a_free, g + 1)
                nc.scalar.activation(sig[:], sig[:], ACT.Sigmoid).then_inc(s.sig_done, 1)
            elif kind == "v":
                act.wait_ge(s.hb_done, i + 1)
                nc.scalar.activation(tc[:, i, :], hb[:, i, 0:T], ACT.Identity, scale=col("c31", i * C31),
                                     bias=col("dwb", i)).then_inc(s.cf0, 1)
            elif kind in "kqu":
                m = 3 * i + "kqu".index(kind)
                dst = (sk, sq, sv)["kqu".index(kind)]
                tile = {"k": NH, "q": 0, "u": 2 * NH}[kind] + i
                act.wait_ge(s.a_free, g + 1)
                if i:
                    act.wait_ge((s.kn_done, s.qn_done, s.vt_mm)["kqu".index(kind)], i)
                nc.scalar.activation(dst[:], cb[:, 0:T], ACT.Copy, scale=col("c4", tile * 4)).then_inc(s.c0_done, 1)
                act.wait_ge(s.ctap, 3 * m + 3)
                nc.scalar.activation(dst[:], dst[:], ACT.Silu).then_inc(s.silu_done, 1)
                if kind != "u":
                    n = 2 * i + (kind == "q")
                    act.wait_ge(s.silu_done, m + 1)
                    if n >= 2:
                        act.wait_ge(s.kqss_mm, n - 1)
                    nc.scalar.activation(sqb[:, n % 2, :], dst[:], ACT.Square).then_inc(s.sqh_done, 1)
            elif kind == "z":
                act.wait_ge(s.a_free, g + 1)
                nc.scalar.activation(sig[:], sig[:], ACT.Silu).then_inc(s.sz_done, 1)

        def ab_pe(pe):
            pe.wait_ge(s.const_in, 16)
            pe.wait_ge(s.a_free, 1)
            for c in range(NC):
                mm = nc.tensor.transpose(B[3][:, c * 8:(c + 1) * 8], ab[:, c * P:(c + 1) * P], const[0:8, IDENT, 0:8])
            mm.then_inc(s.ab_t, 1)
            pe.wait_ge(s.sg_g, 1)
            for i, m in enumerate((UPPER, AFTER, ONES)):
                mm = nc.tensor.matmul(B[3][:, 16 * i:16 * i + 16], cm(m), sm[:, 4, :], start=(i == 0), stop=(i == 2),
                                      skip_group_check=True)
            mm.then_inc(s.cols_mm, 1)

        def ab_act(act):
            pa = B[3][:, 0:32].rearrange("p (c k) -> p c k", k=8)
            v = lambda i: sm[:, i, :].rearrange("p (c h) -> p c h", h=NH)
            act.wait_ge(s.sg_xa, 1)
            nc.scalar.activation(v(0), pa[:, :, NH:2 * NH], ACT.Sigmoid).then_inc(s.sg_beta, 1)
            act.preload_act_table_set("natural_log_exp_and_others")
            act.wait_ge(s.sg_abs, 1)
            nc.scalar.activation(sm[:, 2, :], sm[:, 2, :], ACT.Exp).then_inc(s.sg_e, 1)
            act.wait_ge(s.sg_e, 1)
            nc.scalar.activation(sm[:, 3, :], sm[:, 2, :], ACT.Ln, bias=1.0).then_inc(s.sg_l, 1)
            nc.scalar.activation(sm[:, 9, 0:NH], par[:, PAR["alog"]:PAR["alog"] + NH], ACT.Exp).then_inc(s.sg_ea, 1)
            act.wait_ge(s.cols_mm, 1)
            nc.scalar.activation(sm[:, 5:8, :].rearrange("p a b -> p (a b)"), B[3][:, 0:48], ACT.Exp).then_inc(s.cols_exp, 1)

        def ab_dve(dve):
            pa = B[3][:, 0:32].rearrange("p (c k) -> p c k", k=8)
            v = lambda i: sm[:, i, :].rearrange("p (c h) -> p c h", h=NH)
            hbc = lambda ap: ap.unsqueeze(1).to_broadcast([P, NC, NH])
            dve.wait_ge(s.ab_t, 1)
            nc.vector.tensor_tensor(v(1), pa[:, :, 0:NH], hbc(par[:, PAR["dtb"]:PAR["dtb"] + NH]), ALU.add).then_inc(s.sg_xa, 1)
            dve.wait_ge(s.sg_xa, 1)
            nc.vector.scalar_tensor_tensor(sm[:, 2, :], sm[:, 1, :], -1.0, sm[:, 1, :], ALU.mult, ALU.min).then_inc(s.sg_abs, 1)
            dve.wait_ge(s.sg_l, 1)
            nc.vector.scalar_tensor_tensor(sm[:, 10, :], sm[:, 1, :], 0.0, sm[:, 3, :], ALU.max, ALU.add).then_inc(s.sg_sp, 1)
            dve.wait_ge(s.sg_ea, 1)
            dve.wait_ge(s.sg_sp, 1)
            nc.vector.scalar_tensor_tensor(v(4), v(10), -1.0, hbc(sm[:, 9, 0:NH]), ALU.mult, ALU.mult).then_inc(s.sg_g, 1)
            dve.wait_ge(s.cols_exp, 1)
            nc.vector.tensor_tensor(sm[:, 8, :], sm[:, 0, :], sm[:, 5, :], ALU.mult).then_inc(s.sg_bg, 1)

        def s1_pe(pe, h):
            for j in range(2):
                pe.wait_ge(s.sqh_done, 2 * h + j + 1)
                nc.tensor.matmul(B[3 + j][:], cm(ONES), sqb[:, j, :], start=True, stop=True).then_inc(s.kqss_mm, 1)

        def s1_act(act, h):
            act.preload_act_table_set("natural_log_exp_and_others")
            for j in range(2):
                act.wait_ge(s.kqss_mm, 2 * h + j + 1)
                nc.scalar.activation(rkq[:, j, :], B[3 + j][:], ACT.Ln, bias=eps[:, 0:1]).then_inc(s.kq_ln, 1)
            for j in range(2):
                act.wait_ge(s.kq_ln, 2 * h + j + 1)
                nc.scalar.activation(rkq[:, j, :], rkq[:, j, :], ACT.Exp, scale=-0.5).then_inc(s.kq_r, 1)

        def s1_dve(dve, h):
            fl = lambda a: a.rearrange("p c t -> p (c t)")
            dve.wait_ge(s.kq_r, 2 * h + 1)
            nc.vector.tensor_tensor(fl(kn[:]), sk[:], rkq[:, 0, :], ALU.mult).then_inc(s.kn_done, 1)
            dve.wait_ge(s.kq_r, 2 * h + 2)
            nc.vector.scalar_tensor_tensor(fl(qn[:]), sq[:], P ** -0.5, rkq[:, 1, :], ALU.mult, ALU.mult).then_inc(s.qn_done, 1)
            nc.vector.tensor_tensor(gU[:], bc(cm(UPPER)), tok(4, h), ALU.mult).then_inc(s.gu_done, 1)

        def s2_pe(pe, h):
            fl = lambda a: a.rearrange("p c t -> p (c t)")
            pe.wait_ge(s.silu_done, 3 * h + 3)
            for c in range(NC):
                mm = nc.tensor.transpose(B[6][:, c * P:(c + 1) * P], sv[:, c * P:(c + 1) * P], cm(IDENT))
            mm.then_inc(s.vt_mm, 1)
            pe.wait_ge(s.gu_done, h + 1)
            if h:
                pe.wait_ge(s.o_ln, h)
            nc.tensor.matmul(B[7][:], cm(ONES), fl(gU[:]), start=True, stop=True).then_inc(s.gb_mm, 1)
            pe.wait_ge(s.kn_done, h + 1)
            for c in range(NC):
                mm = nc.tensor.transpose(B[5][:, c * P:(c + 1) * P], kn[:, c, :], cm(IDENT))
            mm.then_inc(s.kt_mm, 1)
            pe.wait_ge(s.kq_ln, 2 * h + 2)
            for c in range(NC):
                mm = nc.tensor.matmul(B[3][:, c * P:(c + 1) * P], kn[:, c, :], kn[:, c, :], start=True, stop=True)
            mm.then_inc(s.kk_mm, 1)
            pe.wait_ge(s.qn_done, h + 1)
            for c in range(NC):
                mm = nc.tensor.matmul(B[4][:, c * P:(c + 1) * P], kn[:, c, :], qn[:, c, :], start=True, stop=True)
            mm.then_inc(s.qk_mm, 1)
            pe.wait_ge(s.kbg_done, h + 1)
            for c in range(NC):
                mm = nc.tensor.matmul(B[5][:, c * P:(c + 1) * P], gU[:, c, :], cm(AFTER), start=True, stop=True)
            mm.then_inc(s.dn_mm, 1)
            pe.wait_ge(s.vb_done, h + 1)
            nc.tensor.matmul(B[6][:], cm(AFTER), fl(gU[:]), start=True, stop=True).then_inc(s.dt_mm, 1)

        def s2_act(act, h):
            fl = lambda a: a.rearrange("p c t -> p (c t)")
            act.wait_ge(s.gb_mm, h + 1)
            nc.scalar.activation(fl(qd[:]), B[7][:], ACT.Exp).then_inc(s.egb_done, 1)
            act.wait_ge(s.dn_mm, h + 1)
            nc.scalar.activation(fl(eDn[:]), B[5][:], ACT.Exp).then_inc(s.edn_done, 1)
            act.wait_ge(s.dt_mm, h + 1)
            nc.scalar.activation(fl(qkd[:]), B[6][:], ACT.Exp).then_inc(s.edt_done, 1)

        def s2_pool(pool, h):
            pool.wait_ge(s.qkd_done, h + 1)
            nc.gpsimd.affine_select(out=qkd[:], in_=qkd[:], compare_op=ALU.is_ge, fill=0.0, base=0,
                                    pattern=[[0, NC], [1, P]], channel_multiplier=-1).then_inc(s.qkd_masked, 1)

        def s2_dve(dve, h):
            r3 = lambda b: b[:].rearrange("p (c t) -> p c t", c=NC)
            dve.wait_ge(s.vt_mm, h + 1)
            nc.vector.tensor_tensor(vb[:], r3(B[6]), tok(0, h), ALU.mult).then_inc(s.vb_done, 1)
            dve.wait_ge(s.kt_mm, h + 1)
            nc.vector.tensor_tensor(ktail[:], r3(B[5]), tok(6, h), ALU.mult).then_inc(s.ktail_done, 1)
            nc.vector.tensor_tensor(kbg[:], r3(B[5]), tok(8, h), ALU.mult).then_inc(s.kbg_done, 1)
            dve.wait_ge(s.egb_done, h + 1)
            nc.vector.tensor_tensor(qd[:], qd[:], qn[:], ALU.mult).then_inc(s.qd_done, 1)
            dve.wait_ge(s.kk_mm, h + 1)
            dve.wait_ge(s.edn_done, h + 1)
            nc.vector.tensor_tensor(eDn[:], r3(B[3]), eDn[:], ALU.mult).then_inc(s.a1_done, 1)
            dve.wait_ge(s.qk_mm, h + 1)
            dve.wait_ge(s.edt_done, h + 1)
            nc.vector.tensor_tensor(qkd[:], r3(B[4]), qkd[:], ALU.mult).then_inc(s.qkd_done, 1)
            dve.wait_ge(s.a1_done, h + 1)
            nc.vector.tensor_tensor(eDn[:], eDn[:], tok(0, h), ALU.mult).then_inc(s.a2_done, 1)

        def inv_t_pe(pe, h, l):
            n = LEVELS * h + l
            if l == 0:
                pe.wait_ge(s.a2_done, h + 1)
            else:
                pe.wait_ge(s.y_done, n)
            for c in range(NC):
                mm = nc.tensor.matmul(B[3][:, c * P:(c + 1) * P], eDn[:, c, :], Y[:, c, :] if l else cm(IDENT),
                                      start=True, stop=True)
            mm.then_inc(s.t_mm, 1)

        def inv_xy_pe(pe, h, l):
            n = LEVELS * h + l
            pe.wait_ge(s.t2_done, n + 1)
            if l < LEVELS - 1:
                for c in range(NC):
                    mm = nc.tensor.matmul(B[4][:, c * P:(c + 1) * P], T2[:, c, :], X[:, c, :] if l else cm(IDENT),
                                          start=True, stop=True)
                mm.then_inc(s.xm_mm, 1)
            if l:
                for c in range(NC):
                    mm = nc.tensor.matmul(B[5][:, c * P:(c + 1) * P], X[:, c, :], T2[:, c, :], start=True, stop=True)
                mm.then_inc(s.ym_mm, 1)

        def inv_t_dve(dve, h, l):
            n = LEVELS * h + l
            dve.wait_ge(s.t_mm, n + 1)
            if l == 0 and h:
                dve.wait_ge(s.ym_mm, (LEVELS - 1) * h)
            nc.vector.tensor_tensor(T2[:], B[3][:].rearrange("p (c t) -> p c t", c=NC), bc(cm(LEV0 + l)),
                                    ALU.mult).then_inc(s.t2_done, 1)

        def inv_xy_dve(dve, h, l):
            n = LEVELS * h + l
            r3 = lambda b: b[:].rearrange("p (c t) -> p c t", c=NC)
            if l == 0:
                dve.wait_ge(s.t2_done, n + 1)
                if h:
                    dve.wait_ge(s.o_mm, h)
                nc.vector.tensor_tensor(Y[:], bc(cm(IDENT)), T2[:], ALU.subtract).then_inc(s.y_done, 1)
                dve.wait_ge(s.xm_mm, (LEVELS - 1) * h + 1)
                nc.vector.tensor_tensor(X[:], bc(cm(IDENT)), r3(B[4]), ALU.subtract).then_inc(s.x_done, 1)
                return
            dve.wait_ge(s.ym_mm, (LEVELS - 1) * h + l)
            if l < LEVELS - 1:
                dve.wait_ge(s.x_done, (LEVELS - 1) * h + l)
                nc.vector.tensor_tensor(X[:], X[:], r3(B[4]), ALU.subtract).then_inc(s.x_done, 1)
            dve.wait_ge(s.y_done, n)
            nc.vector.tensor_tensor(Y[:], Y[:], r3(B[5]), ALU.subtract).then_inc(s.y_done, 1)

        def wt_pe(pe, h):
            pe.wait_ge(s.y_done, LEVELS * (h + 1))
            for c in range(NC):
                mm = nc.tensor.matmul(B[6][:, c * P:(c + 1) * P], kbg[:, c, :], Y[:, c, :], start=True, stop=True)
            mm.then_inc(s.wt_mm, 1)

        def wt_act(act, h):
            act.wait_ge(s.wt_mm, h + 1)
            nc.scalar.activation(nWT[:].rearrange("p c t -> p (c t)"), B[6][:], ACT.Copy, scale=-1.0).then_inc(s.wt_done, 1)

        def seq_v_pe(pe, h, c):
            if c == 0:
                pe.wait_ge(s.wt_done, h + 1)
            else:
                pe.wait_ge(s.s_done, (NC - 1) * h + c)
            mm = nc.tensor.matmul(B[6][:, 0:P], Y[:, c, :], vb[:, c, :], start=True, stop=(c == 0))
            if c:
                mm = nc.tensor.matmul(B[6][:, 0:P], nWT[:, c, :], S[:], start=False, stop=True)
            mm.then_inc(s.v_mm, 1)

        def seq_o_pe(pe, h, c):
            if c == 0:
                pe.wait_ge(s.qkd_masked, h + 1)
                pe.wait_ge(s.qd_done, h + 1)
            else:
                nc.tensor.matmul(B[7][:, c * P:(c + 1) * P], S[:], qd[:, c, :], start=False, stop=False,
                                 skip_group_check=True)
            pe.wait_ge(s.v_done, NC * h + c + 1)
            mm = nc.tensor.matmul(B[7][:, c * P:(c + 1) * P], vnew[:], qkd[:, c, :], start=(c == 0), stop=True,
                                  skip_group_check=True)
            if c == NC - 1:
                mm.then_inc(s.o_mm, 1)
            else:
                nc.tensor.matmul(B[6][:, P:2 * P], ktail[:, c, :], vnew[:], start=True, stop=True).then_inc(s.s_mm, 1)

        def seq_act(act, h, c):
            act.wait_ge(s.v_mm, NC * h + c + 1)
            nc.scalar.activation(vnew[:], B[6][:, 0:P], ACT.Copy).then_inc(s.v_done, 1)

        def seq_dve(dve, h, c):
            n = (NC - 1) * h + c
            dve.wait_ge(s.s_mm, n + 1)
            if c == 0:
                nc.vector.tensor_copy(S[:], B[6][:, P:2 * P]).then_inc(s.s_done, 1)
            else:
                dve.wait_ge(s.s_done, n)
                nc.vector.scalar_tensor_tensor(S[:], S[:], sm[:, 7, NH * c + h:NH * c + h + 1], B[6][:, P:2 * P],
                                               ALU.mult, ALU.add).then_inc(s.s_done, 1)

        def on_pe(pe, h):
            pe.wait_ge(s.osq_done, h + 1)
            nc.tensor.matmul(B[7][:], cm(ONES), ro[:], start=True, stop=True).then_inc(s.oss_mm, 1)

        def on_act(act, h):
            act.wait_ge(s.o_mm, h + 1)
            nc.scalar.activation(oc[:, h, :], B[7][:], ACT.Copy).then_inc(s.oc_done, 1)
            if h:
                act.wait_ge(s.on_done, h)
            act.wait_ge(s.oc_done, h + 1)
            nc.scalar.activation(ro[:], oc[:, h, :], ACT.Square).then_inc(s.osq_done, 1)
            act.wait_ge(s.oss_mm, h + 1)
            act.preload_act_table_set("natural_log_exp_and_others")
            nc.scalar.activation(ro[:], B[7][:], ACT.Ln, bias=eps[:, 0:1], scale=1.0 / P).then_inc(s.o_ln, 1)
            act.wait_ge(s.o_ln, h + 1)
            nc.scalar.activation(ro[:], ro[:], ACT.Exp, scale=-0.5).then_inc(s.o_r, 1)

        def on_dve(dve, h):
            dve.wait_ge(s.o_r, h + 1)
            nc.vector.scalar_tensor_tensor(oc[:, h, :], oc[:, h, :], col("onorm"), ro[:], ALU.mult,
                                           ALU.mult).then_inc(s.on_done, 1)

        def yb_dve(dve, h):
            dve.wait_ge(s.sz_done, h + 1)
            dve.wait_ge(s.on_done, h + 1)
            nc.vector.tensor_tensor(oc[:, h, :], oc[:, h, :], sig[:], ALU.mult).then_inc(s.yb_f, 1)

        def yb_act(act, h):
            act.wait_ge(s.yb_f, h + 1)
            nc.scalar.activation(yb_hi[:, h, :], oc[:, h, :], ACT.Copy).then_inc(s.yb_hid, 1)

        def yb_lo_dve(dve, h):
            dve.wait_ge(s.yb_hid, h + 1)
            nc.vector.tensor_tensor(yb_lo[:, h, :], oc[:, h, :], yb_hi[:, h, :].bitcast(f32),
                                    ALU.subtract).then_inc(s.yb_lod, 1)

        def ln_pe(pe):
            pe.wait_ge(s.cf_tap, TAPS)
            pe.wait_ge(s.y_done, LEVELS * NH)
            for i in range(CA):
                mm = nc.tensor.matmul(B[3][:], cm(ONES), tc[:, i, :], start=(i == 0), stop=(i == CA - 1))
            mm.then_inc(s.mu_mm, 1)
            for i in range(CA):
                pe.wait_ge(s.csq_done, i + 1)
                mm = nc.tensor.matmul(B[4][:], cm(ONES), sqb[:, i % 2, :], start=(i == 0), stop=(i == CA - 1))
                mm.then_inc(s.var_mm, 1)

        def ln_act1(act):
            for i in range(CA):
                act.wait_ge(s.xc_done, i + 1)
                if i >= 2:
                    act.wait_ge(s.var_mm, i - 1)
                nc.scalar.activation(sqb[:, i % 2, :], tc[:, i, :], ACT.Square).then_inc(s.csq_done, 1)
            act.preload_act_table_set("natural_log_exp_and_others")
            act.wait_ge(s.var_mm, CA)
            nc.scalar.activation(rkq[:, 0, :], B[4][:], ACT.Ln, bias=eps[:, 1:2], scale=1.0 / (CA * P)).then_inc(s.c_ln, 1)
            act.wait_ge(s.c_ln, 1)
            nc.scalar.activation(rkq[:, 0, :], rkq[:, 0, :], ACT.Exp, scale=-0.5).then_inc(s.c_r, 1)

        def ln_dve1(dve):
            dve.wait_ge(s.mu_mm, 1)
            for i in range(CA):
                nc.vector.scalar_tensor_tensor(tc[:, i, :], B[3][:], -1.0 / (CA * P), tc[:, i, :], ALU.mult,
                                               ALU.add).then_inc(s.xc_done, 1)

        def ln_dve2(dve):
            dve.wait_ge(s.c_r, 1)
            for i in range(CA):
                nc.vector.scalar_tensor_tensor(tc[:, i, :], tc[:, i, :], col("lnw", i), rkq[:, 0, :], ALU.mult,
                                               ALU.mult).then_inc(s.cn_done, 1)
            for i in range(CA):
                dve.wait_ge(s.ya_hid, i + 1)
                nc.vector.tensor_tensor(ya_lo[:, i, :], tc[:, i, :], ya_hi[:, i, :].bitcast(f32),
                                        ALU.subtract).then_inc(s.ya_lod, 1)

        def ln_act2(act):
            for i in range(CA):
                act.wait_ge(s.cn_done, i + 1)
                nc.scalar.activation(tc[:, i, :], tc[:, i, :], ACT.Silu, bias=col("lnb", i)).then_inc(s.ya_f, 1)
            for i in range(CA):
                act.wait_ge(s.ya_f, i + 1)
                nc.scalar.activation(ya_hi[:, i, :], tc[:, i, :], ACT.Copy).then_inc(s.ya_hid, 1)

        def head_of(g, off):
            h, rest = divmod(g - (9 + off), 3)
            return h if rest == 0 and 0 <= h < NH else None

        def a_pe(pe):
            for g in range(NB0):
                w_wait(pe, g)
                if g >= 3:
                    pe.wait_ge(s.a_free, g - 2)
                bank = B[g % 3]
                mc = 8 if g == 0 else P
                def part(k0, k1):
                    mm = gemm(bank, g, k0, k1, h_hi, h_lo, k0 == 0, k1 == KT, mc)
                    if k1 == KT:
                        mm.then_inc(s.block_done, 1)
                hs = head_of(g, 6)
                inv = next((h for h in range(NH) if g in (9 + 3 * h + 4, 9 + 3 * h + 5)), None)
                if g == 0:
                    for k in range(KT):
                        pe.wait_ge(s.h_lo_done, k + 1)
                        part(k, k + 1)
                elif hs is not None:
                    wt_pe(pe, hs)
                    for c in range(NC):
                        part(2 * c, 2 * c + 1)
                        seq_v_pe(pe, hs, c)
                        part(2 * c + 1, 2 * c + 2)
                        seq_o_pe(pe, hs, c)
                elif inv is not None:
                    l0 = 0 if g == 9 + 3 * inv + 4 else 4
                    k = 0
                    for l in range(l0, 4 if l0 == 0 else LEVELS):
                        inv_t_pe(pe, inv, l)
                        part(k, k + 1)
                        inv_xy_pe(pe, inv, l)
                        part(k + 1, k + 2)
                        k += 2
                    if k < KT:
                        part(k, KT)
                else:
                    part(0, KT)
                if g == 0:
                    pe.wait_ge(s.const_in, 16)
                    stat_pe(pe, 0, B[7])
                if g == 2:
                    ab_pe(pe)
                if hs is not None:
                    on_pe(pe, hs)
                h1 = head_of(g, 3)
                if h1 is not None:
                    s1_pe(pe, h1)
                    s2_pe(pe, h1)
            ln_pe(pe)

        def split_act(act, b):
            if b < BEND:
                w_hi_of(act, b, nblk(b))

        def split_dve(dve, b):
            if b < BEND:
                w_lo_of(dve, b, nblk(b))

        def a_act(act):
            act.wait_ge(s.par_in, 16)
            act.wait_ge(s.ones_set, 1)
            for k in range(KT):
                norm_act_in(act, k)
                if k < RING:
                    split_act(act, k)
            stat_act(act, 0, B[7])
            for g in range(NB0):
                if g >= 1:
                    split_act(act, g + 2)
                hs, inv = head_of(g, 6), None
                if hs is not None:
                    wt_act(act, hs)
                    for c in range(NC):
                        seq_act(act, hs, c)
                    on_act(act, hs)
                if g >= 1:
                    a_post_act(act, g - 1)
                if g == 3:
                    ab_act(act)
                h1 = head_of(g, 3)
                if h1 is not None:
                    s1_act(act, h1)
                    s2_act(act, h1)
                if g >= 1 and ORDER[g - 1][0] == "z" and ORDER[g - 1][1] < NH - 1:
                    yb_act(act, ORDER[g - 1][1])
            split_act(act, NB0 + 2)
            a_post_act(act, NB0 - 1)
            yb_act(act, NH - 1)
            ln_act1(act)
            ln_act2(act)

        def norm_act_in(act, k):
            act.wait_ge(s.x_in0 if k < 4 else s.x_in1, 16)
            nc.scalar.activation(h_hi[:, k, :], x[:, k, :], ACT.Copy, scale=col("norm", k)).then_inc(s.h_hi_done, 1)
            if k >= 2:
                act.wait_ge(s.ssq_done, k - 1)
            nc.scalar.activation(sq2[:, k % 2, :], x[:, k, :], ACT.Square).then_inc(s.sq_done, 1)

        def a_dve(dve):
            for a in (hb[:, :, 0:C31 - 1], cb[:, 0:3]):
                nc.vector.memset(a, 0.0).then_inc(s.halo_set, 1)
            dve.wait_ge(s.x_in0, 16)
            dve.wait_ge(s.x_in1, 16)
            dve.wait_ge(s.par_in, 16)
            dve.wait_ge(s.halo_set, 2)
            for k in range(KT):
                norm_lo(dve, 0, k)
                if k < RING:
                    split_dve(dve, k)
            dve.wait_ge(s.const_in, 16)
            for g in range(NB0):
                if g >= 1:
                    split_dve(dve, g + 2)
                hs = head_of(g, 6)
                inv = next((h for h in range(NH) if g in (9 + 3 * h + 4, 9 + 3 * h + 5)), None)
                if hs is not None:
                    for c in range(NC - 1):
                        seq_dve(dve, hs, c)
                    on_dve(dve, hs)
                if inv is not None:
                    l0 = 0 if g == 9 + 3 * inv + 4 else 4
                    for l in range(l0, 4 if l0 == 0 else LEVELS):
                        inv_t_dve(dve, inv, l)
                        if l == l0:
                            a_post_dve(dve, g - 1)
                        inv_xy_dve(dve, inv, l)
                elif g >= 1:
                    a_post_dve(dve, g - 1)
                if g == 3:
                    ab_dve(dve)
                h1 = head_of(g, 3)
                if h1 is not None:
                    s1_dve(dve, h1)
                    s2_dve(dve, h1)
                if g >= 1 and ORDER[g - 1][0] == "z" and ORDER[g - 1][1] < NH - 1:
                    yb_dve(dve, ORDER[g - 1][1])
                    yb_lo_dve(dve, ORDER[g - 1][1])
                a_dve_taps(dve, tap_at[g], tap_at[g + 1])
            split_dve(dve, NB0 + 2)
            a_post_dve(dve, NB0 - 1)
            yb_dve(dve, NH - 1)
            yb_lo_dve(dve, NH - 1)
            a_dve_taps(dve, tap_at[NB0], TAPS)
            ln_dve1(dve)
            ln_dve2(dve)

        def a_pool(pool):
            norm_pool(pool, 0)
            for h in range(NH):
                s2_pool(pool, h)
        def resid_dve(dve, r, n, b_last, it=None):
            if it is None:
                dve.wait_ge(s.block_done, b_last + 1)
                xt = x[:, n, :]
            else:
                i, mt, mb = it
                dve.wait_ge(s.block_done, i * mb + (b_last + 1))
                xt = x[:, bass.ds(i * mt + n, 1), :].rearrange("p o t -> p (o t)")
            nc.vector.tensor_tensor(xt, xt, B[6 + n % 2][:], ALU.add).then_inc(s.x_new, 1)

        def rnorm_act(act, r, n, last, it=None):
            i, mt = (None, 0) if it is None else it[:2]
            xn = KT * (r - 1) + n
            c = KT * r + n
            g = lambda a: a[:, n, :] if it is None else a[:, bass.ds(i * mt + n, 1), :].rearrange("p o t -> p (o t)")
            at = lambda v: v if it is None else i * mt + v
            act.wait_ge(s.ssq_done, at(c - 1))
            act.wait_ge(s.x_new, at(xn + 1))
            if not last:
                w = col("norm", KT * r + n) if it is None else par[:, bass.ds(i * mt + (PAR["norm"] + KT * r + n), 1)]
                nc.scalar.activation(g(h_hi), g(x), ACT.Copy, scale=w).then_inc(s.h_hi_done, 1)
            nc.scalar.activation(sq2[:, n % 2, :], g(x), ACT.Square).then_inc(s.sq_done, 1)

        def rnorm_lo(dve, r, n, it=None):
            i, mt = (None, 0) if it is None else it[:2]
            c = KT * r + n
            g = lambda a: a[:, n, :] if it is None else a[:, bass.ds(i * mt + n, 1), :].rearrange("p o t -> p (o t)")
            w = col("norm", KT * r + n) if it is None else par[:, bass.ds(i * mt + (PAR["norm"] + KT * r + n), 1)]
            dve.wait_ge(s.h_hi_done, c + 1 if it is None else i * mt + (c + 1))
            nc.vector.scalar_tensor_tensor(g(h_lo), g(x), w, g(h_hi).bitcast(f32), ALU.mult,
                                           ALU.subtract).then_inc(s.h_lo_done, 1)

        def out_pe(pe, r, b0, act_tile, ready):
            for n in range(KT):
                w_wait(pe, b0 + n)
                if 8 * (r - 1) + n >= 2:
                    pe.wait_ge(s.x_new, 8 * (r - 1) + n - 1)
                for j, k in enumerate(ready["order"]):
                    if n == 0:
                        ready["wait"](pe, k)
                    ahi, alo = act_tile(k)
                    mm = mm3(B[6 + n % 2][:], w_hi[:, (b0 + n) % RING, k * P:(k + 1) * P],
                             w_lo[:, (b0 + n) % RING, k * P:(k + 1) * P], ahi, alo, j == 0, j == KT - 1)
                mm.then_inc(s.block_done, 1)

        def out_act(act, r, b0):
            for n in range(KT):
                split_act(act, b0 + n + 3)
                rnorm_act(act, r, n, False)

        def out_dve(dve, r, b0):
            for n in range(KT):
                resid_dve(dve, r, n, b0 + n)
                split_dve(dve, b0 + n + 3)
                rnorm_lo(dve, r, n)


        PB = 3

        def at(v, it, m):
            return v if it is None else it * m + v

        def up_pe(pe, L, b0, j, it):
            for q in range(2):
                g = 2 * j + q
                w_wait(pe, b0 + g, it, 2 * PB)
                G_ = 2 * FT * L + g
                if it is not None or g >= 6:
                    pe.wait_ge(s.up_free, at(G_ - 5, it, 2 * PB))
                if j == 0 and it is None:
                    for k in range(KT):
                        if q == 0:
                            pe.wait_ge(s.h_lo_done, KT * (2 * L + 1) + k + 1)
                            mm = gemm(B[g % 6], b0 + g, k, k + 1, h_hi, h_lo, k == 0, k == KT - 1)
                    if q == 1:
                        mm = gemm(B[g % 6], b0 + g, 0, KT, h_hi, h_lo, True, True)
                else:
                    mm = gemm(B[g % 6], b0 + g, 0, KT, h_hi, h_lo, True, True)
                mm.then_inc(s.block_done, 1)
                if j == 0 and it is None and q == 0:
                    stat_pe(pe, 2 * L + 1, B[7])

        def fcol(L, j, it, q, tap):
            o = PAR["fc%d" % L] + (2 * j + q) * 3 + tap
            return par[:, o:o + 1] if it is None else par[:, bass.ds(it * (6 * PB) + o, 1)]

        def up_act(act, L, b0, j, it, tail):
            for q in range(2):
                g = 2 * j + q
                if not tail:
                    w_hi_of(act, b0 + g + 3, D, it, 2 * PB)
                else:
                    split_act(act, b0 + g + 3)
                G_ = 2 * FT * L + g
                u, t = (ug, tg) if q == 0 else (uv, tv)
                act.wait_ge(s.up_free, at(G_ + 1, it, 2 * PB))
                nc.scalar.activation(t[:, j % 3, :], u[:, 0:T], ACT.Copy, scale=fcol(L, j, it, q, 0)).then_inc(s.tap0, 1)
            J = FT * L + j
            act.wait_ge(s.tap1, at(4 * J + 2, it, 4 * PB))
            nc.scalar.activation(tg[:, j % 3, :], tg[:, j % 3, :], ACT.Silu).then_inc(s.silu_f, 1)
            act.wait_ge(s.prod, at(J + 1, it, PB))
            dst = p_hi[:, j, :] if it is None else p_hi[:, bass.ds(it * PB + j, 1), :].rearrange("p o t -> p (o t)")
            nc.scalar.activation(dst, tv[:, j % 3, :], ACT.Copy).then_inc(s.prod_hi, 1)

        def up_taps(dve, L, j, it, q):
            J = FT * L + j
            u, t = (ug, tg) if q == 0 else (uv, tv)
            n = 4 * J + 2 * q
            dve.wait_ge(s.tap0, at(2 * J + q + 1, it, 2 * PB))
            nc.vector.scalar_tensor_tensor(t[:, j % 3, :], u[:, 1:T + 1], fcol(L, j, it, q, 1), t[:, j % 3, :],
                                           ALU.mult, ALU.add).then_inc(s.tap1, 1)
            dve.wait_ge(s.tap1, at(n + 1, it, 4 * PB))
            nc.vector.scalar_tensor_tensor(t[:, j % 3, :], u[:, 2:T + 2], fcol(L, j, it, q, 2), t[:, j % 3, :],
                                           ALU.mult, ALU.add).then_inc(s.tap1, 1)

        def up_evac(dve, L, b0, j, it, q):
            g = 2 * j + q
            u = ug if q == 0 else uv
            dve.wait_ge(s.block_done, at(b0 + g + 1, it, 2 * PB))
            nc.vector.tensor_tensor(u[:, 2:], B[g % 6][:], rms[:], ALU.mult).then_inc(s.up_free, 1)

        def up_plo(dve, L, j, it):
            J = FT * L + j
            dve.wait_ge(s.prod_hi, at(J + 1, it, PB))
            g = lambda a: a[:, j, :] if it is None else a[:, bass.ds(it * PB + j, 1), :].rearrange("p o t -> p (o t)")
            nc.vector.tensor_tensor(g(p_lo), tv[:, j % 3, :], g(p_hi).bitcast(f32), ALU.subtract).then_inc(s.prod_lo, 1)

        def up_dve(dve, L, b0, j, it, tail):
            J = FT * L + j
            up_evac(dve, L, b0, j, it, 0)
            if not (j == 0 and it is None):
                up_plo(dve, L, j - 1, it)
            if tail:
                split_dve(dve, b0 + 2 * j + 3)
            else:
                w_lo_of(dve, b0 + 2 * j + 3, D, it, 2 * PB)
            up_taps(dve, L, j, it, 0)
            up_evac(dve, L, b0, j, it, 1)
            if tail:
                split_dve(dve, b0 + 2 * j + 4)
            else:
                w_lo_of(dve, b0 + 2 * j + 4, D, it, 2 * PB)
            up_taps(dve, L, j, it, 1)
            dve.wait_ge(s.silu_f, at(J + 1, it, PB))
            dve.wait_ge(s.tap1, at(4 * J + 4, it, 4 * PB))
            nc.vector.tensor_tensor(tv[:, j % 3, :], tg[:, j % 3, :], tv[:, j % 3, :], ALU.mult).then_inc(s.prod, 1)

        UP_FIRST = 1 + PB
        UP_ITERS = (FT - UP_FIRST) // PB - 1

        def up(eng, fn, L, b0):
            for j in range(UP_FIRST):
                fn(eng, L, b0, j, None)
            with eng.Fori(0, UP_ITERS) as it:
                for j in range(UP_FIRST, UP_FIRST + PB):
                    fn(eng, L, b0, j, it)
            for j in range(FT - PB, FT):
                fn(eng, L, b0, j, None)

        def down_pe(pe, L, r, b0, n, it):
            b = b0 + 3 * n
            for q, kts in enumerate(DOWN):
                w_wait(pe, b + q, it, 6)
                k0 = sum(DOWN[:q])
                pe.wait_ge(s.prod_lo, FT * L + k0 + kts)
                if q == 0:
                    pe.wait_ge(s.x_new, at(8 * (r - 1) + n - 1, it, 2))
                mm = gemm(B[6 + n % 2], b + q, 0, kts, p_hi, p_lo, q == 0, q == 2, a0=k0)
                mm.then_inc(s.block_done, 1)

        def down_act(act, L, r, b0, n, it):
            b = b0 + 3 * n
            for q in range(3):
                if it is None:
                    split_act(act, b + q + 3)
                else:
                    w_hi_of(act, b + q + 3, DOWN[q] * P, it, 6)
            rnorm_act(act, r, n, r == 4, None if it is None else (it, 2))

        def down_dve(dve, L, r, b0, n, it):
            b = b0 + 3 * n
            for q in range(3):
                if q == 2:
                    resid_dve(dve, r, n, b + 2, None if it is None else (it, 2, 6))
                if it is None:
                    split_dve(dve, b + q + 3)
                else:
                    w_lo_of(dve, b + q + 3, DOWN[q] * P, it, 6)
            if r != 4:
                rnorm_lo(dve, r, n, None if it is None else (it, 2))

        def down(eng, fn, L, r, b0):
            with eng.Fori(0, KT // 2 - 1) as it:
                for n in range(2):
                    fn(eng, L, r, b0, n, it)
            for n in range(KT - 2, KT):
                fn(eng, L, r, b0, n, None)

        PLACE = {0: (0, 0), 1: (1, 0), 3: (1, 384), 2: (2, 0)}
        BASE = (0, 512, 1024)
        WID = (512, 512, 256)

        def kcols(kb):
            bank, c0 = PLACE[kb]
            return BASE[bank] + c0, T - P * kb

        def proj_pe(pe, p, kind):
            b = BQ + 3 * p + kind
            bank = B[6 if kind == 0 else 7 if kind == 1 else 7]
            w_wait(pe, b)
            if kind == 0:
                if p == 0:
                    pe.wait_ge(s.x_new, 2 * KT - 1)
                if p:
                    pe.wait_ge(s.v_lod, p)
            elif kind == 1:
                if p >= 2:
                    pe.wait_ge(s.y1_lod, p - 1)
            else:
                pe.wait_ge(s.k_f, p + 1)
            if kind == 0 and p == 0:
                for k in range(KT):
                    pe.wait_ge(s.h_lo_done, KT * 2 + k + 1)
                    mm = gemm(bank, b, k, k + 1, h_hi, h_lo, k == 0, k == KT - 1)
            else:
                mm = gemm(bank, b, 0, KT, h_hi, h_lo, True, True)
            mm.then_inc(s.block_done, 1)

        def vt_pe(pe, p):
            pe.wait_ge(s.v_f, p + 1)
            pe.wait_ge(s.q_f, p + 1)
            for c in range(NC):
                mm = nc.tensor.transpose(B[6][:, c * P:(c + 1) * P], vT[:, c * P:(c + 1) * P], cm(IDENT))
            mm.then_inc(s.vt2_mm, 1)

        def proj_dve(dve, p, kind):
            b = BQ + 3 * p + kind
            dve.wait_ge(s.block_done, b + 1)
            if kind == 0:
                if p:
                    dve.wait_ge(s.k_lod, p)
                nc.vector.scalar_tensor_tensor(pf[:], B[6][:], 0.125, rms[:], ALU.mult, ALU.mult).then_inc(s.q_f, 1)
                dve.wait_ge(s.q_hid, p + 1)
                nc.vector.tensor_tensor(q_lo[:, p % 2, :], pf[:], q_hi[:, p % 2, :].bitcast(f32), ALU.subtract).then_inc(s.q_lod, 1)
            elif kind == 1:
                dve.wait_ge(s.q_lod, p + 1)
                nc.vector.tensor_tensor(pf[:], B[7][:], rms[:], ALU.mult).then_inc(s.k_f, 1)
                dve.wait_ge(s.k_hid, p + 1)
                nc.vector.tensor_tensor(k_lo[:, p % 2, :], pf[:], k_hi[:, p % 2, :].bitcast(f32), ALU.subtract).then_inc(s.k_lod, 1)
            else:
                if p:
                    dve.wait_ge(s.vt2_mm, p)
                nc.vector.tensor_tensor(vT[:], B[7][:], rms[:], ALU.mult).then_inc(s.v_f, 1)

        def proj_act(act, p, kind):
            if kind == 0:
                act.wait_ge(s.q_f, p + 1)
                nc.scalar.activation(q_hi[:, p % 2, :], pf[:], ACT.Copy).then_inc(s.q_hid, 1)
            elif kind == 1:
                act.wait_ge(s.k_f, p + 1)
                nc.scalar.activation(k_hi[:, p % 2, :], pf[:], ACT.Copy).then_inc(s.k_hid, 1)

        def vpads(t, p, e):
            return t[:, p % 2, :, e, 64 * e:64 * e + 64]

        def vt_act(act, p):
            act.wait_ge(s.vt2_mm, p + 1)
            for e in range(2):
                nc.scalar.activation(vpads(v_hi, p, e), B[6][:].rearrange("p (c d) -> p c d", c=NC)[:, :, 64 * e:64 * e + 64],
                                     ACT.Copy).then_inc(s.v_hid, 1)

        def vt_dve(dve, p):
            for e in range(2):
                dve.wait_ge(s.v_hid, 2 * p + 2)
                mm = nc.vector.tensor_tensor(vpads(v_lo, p, e),
                                             B[6][:].rearrange("p (c d) -> p c d", c=NC)[:, :, 64 * e:64 * e + 64],
                                             vpads(v_hi, p, e).bitcast(f32), ALU.subtract)
            mm.then_inc(s.v_lod, 1)

        def z_pe(pe, p, e):
            u = 2 * p + e
            rows = slice(64 * e, 64 * e + 64)
            pe.wait_ge(s.k_lod, p + 1)
            if u >= 2:
                pe.wait_ge(s.att_done, 3 * (u - 1))
            if u == 0:
                pe.wait_ge(s.consts_r, 4)
            for bank, kbs in enumerate(((0,), (1, 3), (2,))):
                first = True
                for kb in kbs:
                    c0, w = PLACE[kb][1], T - P * kb
                    out = B[3 * e + bank]
                    kk, qq = slice(P * kb, P * kb + P), slice(P * kb, T)
                    for a, (kt, qt) in enumerate(((k_lo, q_hi), (k_hi, q_lo), (k_hi, q_hi))):
                        nc.tensor.matmul(out[:, c0:c0 + w], kt[rows, p % 2, kk], qt[rows, p % 2, qq],
                                         start=first, stop=False, skip_group_check=True)
                        first = False
                    mm = nc.tensor.matmul(out[:, c0:c0 + P], identr[:], negm[:], start=False, stop=(kb == kbs[-1]),
                                          skip_group_check=True)
                mm.then_inc(s.z_mm, 1)

        def cum_pe(pe, p, e):
            u = 2 * p + e
            pe.wait_ge(s.sp_lod, 3 * u + 3)
            for bank, kbs in enumerate(((0,), (1, 3), (2,))):
                for kb in kbs:
                    out, c0 = B[3 * e + bank], PLACE[kb][1]
                    for kb2 in range(kb, NC):
                        o, w = kcols(kb2)
                        d = c0 + P * (kb2 - kb)
                        for src in (s_lo, s_hi):
                            mm = nc.tensor.matmul(out[:, d:d + w], (ntri if kb2 == kb else nones)[:], src[:, e, o:o + w],
                                                  start=False, stop=False, skip_group_check=True)
                mm.then_inc(s.cum_mm, 1)

        def sp_act(act, p, e):
            u = 2 * p + e
            for bank in range(3):
                n = 3 * u + bank
                o, w = BASE[bank], WID[bank]
                act.wait_ge(s.z_mm, n + 1)
                if u >= 2:
                    act.wait_ge(s.att_lod, 3 * (u - 1))
                nc.scalar.activation(t_[:, e, o:o + w], B[3 * e + bank][:, 0:w], ACT.Abs).then_inc(s.za_done, 1)
            for bank in range(3):
                n = 3 * u + bank
                o, w = BASE[bank], WID[bank]
                act.wait_ge(s.za_done, n + 1)
                nc.scalar.activation(t_[:, e, o:o + w], t_[:, e, o:o + w], ACT.Exp, scale=-1.0).then_inc(s.ze_done, 1)
            for bank in range(3):
                n = 3 * u + bank
                o, w = BASE[bank], WID[bank]
                act.wait_ge(s.ze_done, n + 1)
                nc.scalar.activation(t_[:, e, o:o + w], t_[:, e, o:o + w], ACT.Ln, bias=1.0).then_inc(s.zl_done, 1)

        def sp2_dve(dve, p, e):
            u = 2 * p + e
            for bank in range(3):
                n = 3 * u + bank
                o, w = BASE[bank], WID[bank]
                dve.wait_ge(s.zl_done, n + 1)
                nc.vector.scalar_tensor_tensor(t_[:, e, o:o + w], B[3 * e + bank][:, 0:w], 0.0, t_[:, e, o:o + w],
                                               ALU.max, ALU.add).then_inc(s.sp_done, 1)

        def split_s_act(act, p, e, src_sem, dst_sem):
            u = 2 * p + e
            for bank in range(3):
                n = 3 * u + bank
                o, w = BASE[bank], WID[bank]
                act.wait_ge(src_sem, n + 1)
                nc.scalar.activation(s_hi[:, e, o:o + w], t_[:, e, o:o + w], ACT.Copy).then_inc(dst_sem, 1)

        def split_s_dve(dve, p, e, hi_sem, lo_sem):
            u = 2 * p + e
            for bank in range(3):
                n = 3 * u + bank
                o, w = BASE[bank], WID[bank]
                dve.wait_ge(hi_sem, n + 1)
                nc.vector.tensor_tensor(s_lo[:, e, o:o + w], t_[:, e, o:o + w], s_hi[:, e, o:o + w].bitcast(f32),
                                        ALU.subtract).then_inc(lo_sem, 1)

        def att_act(act, p, e):
            u = 2 * p + e
            for bank in range(3):
                o, w = BASE[bank], WID[bank]
                act.wait_ge(s.cum_mm, 3 * u + 3)
                nc.scalar.activation(t_[:, e, o:o + w], B[3 * e + bank][:, 0:w], ACT.Exp).then_inc(s.att_done, 1)

        def av_pe(pe, p):
            pe.wait_ge(s.v_lod, p + 1)
            pe.wait_ge(s.v_f, min(p + 1, PAIRS - 1) + 0)
            first = True
            for e in range(2):
                pe.wait_ge(s.att_lod, 3 * (2 * p + e) + 3)
                for kb in range(NC):
                    o, w = kcols(kb)
                    for vt, at_ in ((v_lo, s_hi), (v_hi, s_lo), (v_hi, s_hi)):
                        mm = nc.tensor.matmul(B[7][:, P * kb:T], vt[:, p % 2, kb, e, :], at_[:, e, o:o + w], start=first,
                                              stop=(e == 1 and kb == NC - 1 and at_ is s_hi and vt is v_hi),
                                              skip_group_check=True)
                        first = False
            mm.then_inc(s.av_mm, 1)

        def y1_act(act, p):
            act.wait_ge(s.av_mm, p + 1)
            nc.scalar.activation(y1_hi[:, p, :], B[7][:], ACT.Copy).then_inc(s.y1_hid, 1)

        def y1_dve(dve, p):
            dve.wait_ge(s.y1_hid, p + 1)
            nc.vector.tensor_tensor(y1_lo[:, p, :], B[7][:], y1_hi[:, p, :].bitcast(f32), ALU.subtract).then_inc(s.y1_lod, 1)

        def t_pe(pe):
            for kind in range(3):
                proj_pe(pe, 0, kind)
                if kind == 0:
                    stat_pe(pe, 2, B[5])
            vt_pe(pe, 0)
            for p in range(PAIRS):
                nxt = p + 1 < PAIRS
                z_pe(pe, p, 0)
                if nxt:
                    proj_pe(pe, p + 1, 0)
                z_pe(pe, p, 1)
                if p:
                    av_pe_wait(pe, p - 1)
                if nxt:
                    proj_pe(pe, p + 1, 1)
                cum_pe(pe, p, 0)
                if nxt:
                    proj_pe(pe, p + 1, 2)
                cum_pe(pe, p, 1)
                if nxt:
                    vt_pe(pe, p + 1)
            av_pe_wait(pe, PAIRS - 1)

        def av_pe_wait(pe, p):
            av_pe(pe, p)

        def t_act(act):
            for dst, i, sc in ((ntri, NTRI, 1.0), (nones, ONES, -1.0), (negm, NEG, 1.0), (identr, IDENT, 1.0)):
                nc.scalar.activation(dst[:], cm(i), ACT.Copy, scale=sc).then_inc(s.consts_r, 1)
            stat_act(act, 2, B[5])
            for kind in range(3):
                split_act(act, BQ + kind + 3)
                proj_act(act, 0, kind)
            vt_act(act, 0)
            for p in range(PAIRS):
                nxt = p + 1 < PAIRS
                if p:
                    split_s_act(act, p - 1, 1, s.att_done, s.att_hid)
                sp_act(act, p, 0)
                if nxt:
                    split_act(act, BQ + 3 * (p + 1) + 3)
                    proj_act(act, p + 1, 0)
                if p:
                    y1_act(act, p - 1)
                split_s_act(act, p, 0, s.sp_done, s.sp_hid)
                sp_act(act, p, 1)
                if nxt:
                    split_act(act, BQ + 3 * (p + 1) + 4)
                    proj_act(act, p + 1, 1)
                split_s_act(act, p, 1, s.sp_done, s.sp_hid)
                att_act(act, p, 0)
                split_s_act(act, p, 0, s.att_done, s.att_hid)
                if nxt:
                    split_act(act, BQ + 3 * (p + 1) + 5)
                    vt_act(act, p + 1)
                att_act(act, p, 1)
            split_s_act(act, PAIRS - 1, 1, s.att_done, s.att_hid)
            y1_act(act, PAIRS - 1)

        def t_dve(dve):
            dve.wait_ge(s.rms_done, 3)
            for kind in range(3):
                proj_dve(dve, 0, kind)
                split_dve(dve, BQ + kind + 3)
            vt_dve(dve, 0)
            for p in range(PAIRS):
                nxt = p + 1 < PAIRS
                if p:
                    split_s_dve(dve, p - 1, 1, s.att_hid, s.att_lod)
                sp2_dve(dve, p, 0)
                if nxt:
                    proj_dve(dve, p + 1, 0)
                    split_dve(dve, BQ + 3 * (p + 1) + 3)
                if p:
                    y1_dve(dve, p - 1)
                split_s_dve(dve, p, 0, s.sp_hid, s.sp_lod)
                sp2_dve(dve, p, 1)
                if nxt:
                    proj_dve(dve, p + 1, 1)
                    split_dve(dve, BQ + 3 * (p + 1) + 4)
                split_s_dve(dve, p, 1, s.sp_hid, s.sp_lod)
                split_s_dve(dve, p, 0, s.att_hid, s.att_lod)
                if nxt:
                    proj_dve(dve, p + 1, 2)
                    split_dve(dve, BQ + 3 * (p + 1) + 5)
                    vt_dve(dve, p + 1)
            split_s_dve(dve, PAIRS - 1, 1, s.att_hid, s.att_lod)
            y1_dve(dve, PAIRS - 1)

        block = ctx.enter_context(nc.Block())

        @block.sync
        def _(sp):
            sp.dma_start(x[:, 0:4, :], xT[:, 0:4, :]).then_inc(s.x_in0, 16)
            w_load(sp, w_ab, 0, 64)
            sp.dma_start(par[:], par_d).then_inc(s.par_in, 16)
            sp.dma_start(x[:, 4:8, :], xT[:, 4:8, :]).then_inc(s.x_in1, 16)
            for b in range(1, NB0):
                w_load(sp, w_in0[b - 1], b, D)
                if b == 2:
                    sp.dma_start(const[:], const_d).then_inc(s.const_in, 16)

            def out_loads(dram, b0):
                for n in range(KT):
                    w_load(sp, dram[n], b0 + n, D)

            def up_loads(dram, b0):
                for g in range(2):
                    w_load(sp, dram[g], b0 + g, D)
                with sp.Fori(0, (2 * FT - 2) // RING) as i:
                    for j in range(RING):
                        w_load(sp, dram[bass.ds(i * RING + (2 + j), 1)].rearrange("o p n -> (o p) n"), b0 + 2 + j, D, i, RING)

            def down_loads(dram, b0):
                with sp.Fori(0, KT) as i:
                    for q, kts in enumerate(DOWN):
                        k0 = sum(DOWN[:q]) * P
                        w_load(sp, dram[bass.ds(i, 1), :, k0:k0 + kts * P].rearrange("o p n -> (o p) n"), b0 + q, kts * P, i, 3)

            out_loads(w_out0, BO0)
            up_loads(w_up0, BU0)
            down_loads(w_dn0, BD0)
            for b in range(NBQ):
                w_load(sp, w_qkv[b], BQ + b, D)
            out_loads(w_out1, BO1)
            up_loads(w_up1, BU1)
            down_loads(w_dn1, BD1)
            for k in range(KT):
                sp.wait_ge(s.out_f, k + 1)
                sp.dma_start(outT[:, k, :], x[:, k, :]).then_inc(s.out_w, 16)
            sp.wait_ge(s.out_w, 16 * KT)


        @block.gpsimd
        def _(pool):
            nc.gpsimd.memset(eps[:, 0:1], 1e-6)
            nc.gpsimd.memset(eps[:, 1:2], 1e-5).then_inc(s.ones_set, 1)
            a_pool(pool)
            norm_pool(pool, 1)
            norm_pool(pool, 2)
            norm_pool(pool, 3)
            norm_pool(pool, 4)

        @block.scalar
        def _(act):
            a_act(act)
            out_act(act, 1, BO0)
            stat_act(act, 1, B[7])
            up(act, lambda e, L, b0, j, it: up_act(e, L, b0, j, it, it is None), 0, BU0)
            down(act, down_act, 0, 2, BD0)
            t_act(act)
            out_act(act, 3, BO1)
            stat_act(act, 3, B[7])
            up(act, lambda e, L, b0, j, it: up_act(e, L, b0, j, it, it is None), 1, BU1)
            down(act, down_act, 1, 4, BD1)
            stat_act(act, 4, B[7])

        @block.vector
        def _(dve):
            a_dve(dve)
            out_dve(dve, 1, BO0)

            def ffn_up(L, b0):
                dve.wait_ge(s.rms_done, 2 * L + 2)
                nc.vector.memset(ug[:, 0:2], 0.0).then_inc(s.halo_f, 1)
                nc.vector.memset(uv[:, 0:2], 0.0).then_inc(s.halo_f, 1)
                dve.wait_ge(s.halo_f, 2 * L + 2)
                up(dve, lambda e, L, b0, j, it: up_dve(e, L, b0, j, it, it is None), L, b0)
                up_plo(dve, L, FT - 1, None)
            ffn_up(0, BU0)
            down(dve, down_dve, 0, 2, BD0)
            for t in (v_hi, v_lo):
                nc.vector.memset(t[:].bitcast(f32), 0.0).then_inc(s.vp_zero, 1)
            dve.wait_ge(s.vp_zero, 2)
            t_dve(dve)
            out_dve(dve, 3, BO1)
            ffn_up(1, BU1)
            down(dve, down_dve, 1, 4, BD1)
            dve.wait_ge(s.rms_done, 5)
            for k in range(KT):
                nc.vector.scalar_tensor_tensor(x[:, k, :], x[:, k, :], col("norm", 4 * KT + k), rms[:], ALU.mult,
                                               ALU.mult).then_inc(s.out_f, 1)

        @block.tensor
        def _(pe):
            a_pe(pe)
            def wait0(pe, k):
                if k < CA:
                    pe.wait_ge(s.ya_lod, k + 1)
                else:
                    pe.wait_ge(s.yb_lod, k - CA + 1)
            out_pe(pe, 1, BO0, lambda k: (ya_hi[:, k, :], ya_lo[:, k, :]) if k < CA else
                   (yb_hi[:, k - CA, :], yb_lo[:, k - CA, :]), {"order": (4, 5, 6, 7, 0, 1, 2, 3), "wait": wait0})
            up(pe, up_pe, 0, BU0)
            down(pe, down_pe, 0, 2, BD0)
            t_pe(pe)
            out_pe(pe, 3, BO1, lambda k: (y1_hi[:, k, :], y1_lo[:, k, :]),
                   {"order": tuple(range(KT)), "wait": lambda pe, k: pe.wait_ge(s.y1_lod, k + 1)})
            up(pe, up_pe, 1, BU1)
            down(pe, down_pe, 1, 4, BD1)
            stat_pe(pe, 4, B[7])


def _blocks(np, w, cols):
    k = w.shape[0] // P
    a = w.reshape(k, P, w.shape[1] // P, P) if w.shape[1] % P == 0 else None
    return np.ascontiguousarray(a[:, :, cols, :].transpose(2, 1, 0, 3).reshape(len(cols), P, k * P))


def _consts(np):
    i = np.arange(P)
    row, c = i[:, None], i[None, :]
    m = [row == c, row <= c, row > c, np.ones((P, P))]
    for l in range(LEVELS):
        b = 1 << l
        m.append((row // (2 * b) == c // (2 * b)) & ((row // b) % 2 == 0) & ((c // b) % 2 == 1))
    m.append(-1.0 * (row >= c))
    m.append(-(2.0 ** 100) * (row >= c))
    return np.ascontiguousarray(np.stack([np.asarray(a, np.float32) for a in m]).transpose(1, 0, 2))


def _arrays(np, inputs):
    g = {k: np.asarray(v) for k, v in inputs.items()}
    tile = lambda v: v.reshape(-1, P).T
    w0 = g["w_in0"][0]
    c = CA
    order = [t for i in range(CA) for t in (c + i, i)]
    for h in range(NH):
        order += [2 * c + NH + h, 2 * c + h, 2 * c + 2 * NH + h]
    order += [2 * c + 3 * NH + h for h in range(NH)]
    main = w0[:, :24 * P]
    w_ab = np.ascontiguousarray(w0[:, 24 * P:].reshape(KT, P, 8).transpose(1, 0, 2).reshape(P, 64))
    pairs = [t for j in range(FT) for t in (j, FT + j)]
    qkv = [t for p in range(PAIRS) for t in (p, PAIRS + p, 2 * PAIRS + p)]
    par = [tile(g["mix0_norm"][0]), tile(g["ffn_norm"][0]), tile(g["mix1_norm"][0]), tile(g["ffn_norm"][1]),
           tile(g["final_norm"]), tile(g["a_dw_b"][0]), tile(g["a_ln_w"][0]), tile(g["a_ln_b"][0]),
           tile(g["gdn_onorm_w"][0]),
           g["gdn_conv_w"][0].reshape(4, 12, P).transpose(2, 1, 0).reshape(P, 48),
           g["a_dw_w"][0].reshape(C31, CA, P).transpose(2, 1, 0).reshape(P, CA * C31)]
    for L in range(2):
        par.append(g["ffn_conv_w"][L].reshape(3, 2 * FT, P)[:, pairs, :].transpose(2, 1, 0).reshape(P, 6 * FT))
    par += [np.broadcast_to(g[n][0][None, :], (P, NH)) for n in ("gdn_dt_bias", "gdn_a_log")]
    down = lambda w: np.ascontiguousarray(w.reshape(FT, P, KT, P).transpose(2, 1, 0, 3).reshape(KT, P, FT * P))
    return {
        "xT": np.ascontiguousarray(g["x"][0].T.reshape(KT, P, T).transpose(1, 0, 2)),
        "w_ab": w_ab,
        "w_in0": _blocks(np, main, order),
        "w_out0": _blocks(np, g["w_out0"][0], list(range(KT))),
        "w_up0": _blocks(np, g["w_up"][0], pairs),
        "w_dn0": down(g["w_down"][0]),
        "w_qkv": _blocks(np, g["w_qkv1"][0], qkv),
        "w_out1": _blocks(np, g["w_out1"][0], list(range(KT))),
        "w_up1": _blocks(np, g["w_up"][1], pairs),
        "w_dn1": down(g["w_down"][1]),
        "par": np.ascontiguousarray(np.concatenate(par, axis=1)),
        "const": _consts(np),
    }


def kernel(**inputs):
    import numpy as np
    import concourse.bacc as bacc
    from concourse import mybir as mb
    from concourse.bass_utils import run_bass_kernel_spmd
    arrays = {"in_" + n: a for n, a in _arrays(np, inputs).items()}
    nc = bacc.Bacc("TRN2", target_bir_lowering=False, num_devices=1)
    args = [nc.dram_tensor(n, a.shape, mb.dt.from_np(a.dtype), kind="ExternalInput").ap() for n, a in arrays.items()]
    args.append(nc.dram_tensor("outT", (P, KT, T), mb.dt.float32, kind="ExternalOutput").ap())
    trunk(nc, *args)
    r = run_bass_kernel_spmd(nc, [arrays], core_ids=[0])
    out = r.results[0]["outT"]
    return np.ascontiguousarray(out.transpose(1, 0, 2).reshape(D, T).T)[None]
```

```python
import concourse.bass as bass
from concourse import mybir
from contextlib import ExitStack
from collections import namedtuple

P = 128
T = 512
D = 1024
KT = D // P
FF = 2816
FT = FF // P
DOWN = (8, 8, 6)
C31 = 31
CA = 4
NH = 4
NC = T // P
LEVELS = 7
PAIRS = 8
NB0, NBO0, NBO1, NBU, NBD, NBQ = 25, 16, 8, 2 * FT, 24, 24
RING = 3

PAR = {}
_n = 0
for _name, _w in (("norm", 5 * KT), ("dwb", CA), ("lnw", CA), ("lnb", CA), ("onorm", 1), ("c4", 12 * 4),
                  ("c31", CA * C31), ("fc0", 2 * FT * 3), ("fc1", 2 * FT * 3), ("dtb", NH), ("alog", NH)):
    PAR[_name] = _n
    _n += _w
NPAR = _n
IDENT, UPPER, AFTER, ONES, LEV0, NTRI, NEG = 0, 1, 2, 3, 4, 11, 12
NCONST = 13


def trunk(nc, xT, w_ab, w_in0, w_out0, w_up0, w_dn0, w_qkv, w_out1, w_up1, w_dn1, par_d, const_d, outT):
    f32, f32r = mybir.dt.float32, mybir.dt.float32r
    ACT, ALU = mybir.ActivationFunctionType, mybir.AluOpType
    ctx = ExitStack()
    with ctx:
        def sb(name, shape, dt=f32, c=ctx):
            return c.enter_context(nc.sbuf_tensor(name, shape, dt))

        def sem(name):
            return ctx.enter_context(nc.semaphore(name))

        x = sb("x", [P, KT, T])
        h_hi, h_lo = sb("h_hi", [P, KT, T], f32r), sb("h_lo", [P, KT, T], f32r)
        stage = sb("stage", [P, RING, D])
        w_hi, w_lo = sb("w_hi", [P, RING, D], f32r), sb("w_lo", [P, RING, D], f32r)
        rms = sb("rms", [P, T])
        ssq = sb("ssq", [P, T])
        sq2 = sb("sq2", [P, 2, T])
        par = sb("par", [P, NPAR])
        const = sb("const", [P, NCONST, P])
        eps = sb("eps", [P, 4])
        za = ExitStack()
        yb_hi, yb_lo = sb("yb_hi", [P, NH, T], f32r, za), sb("yb_lo", [P, NH, T], f32r, za)
        ya_hi = sb("ya_hi", [P, CA, T], f32r, za)
        with ExitStack() as over:
            ya_lo = sb("ya_lo", [P, CA, T], f32r, over)
        hb = sb("hb", [P, CA, T + C31 - 1], f32, za)
        tc = sb("tc", [P, CA, T], f32, za)
        sig = sb("sig", [P, T], f32, za)
        cb = sb("cb", [P, T + 3], f32, za)
        sk, sq, sv = (sb(n, [P, T], f32, za) for n in ("sk", "sq", "sv"))
        sqb = sb("sqb", [P, 2, T], f32, za)
        rkq = sb("rkq", [P, 2, T], f32, za)
        kn, qn = sb("kn", [P, NC, P], f32, za), sb("qn", [P, NC, P], f32, za)
        gU, eDn, qkd, qd = (sb(n, [P, NC, P], f32, za) for n in ("gU", "eDn", "qkd", "qd"))
        X, Y, ktail, kbg, vb, nWT = (sb(n, [P, NC, P], f32, za) for n in ("X", "Y", "ktail", "kbg", "vb", "nWT"))
        T2 = sb("T2", [P, 2, NC, P], f32, za)
        vnew, S = sb("vnew", [P, P], f32, za), sb("S", [P, P], f32, za)
        oc, ro = sb("oc", [P, NH, T], f32, za), sb("ro", [P, T], f32, za)
        ab = sb("ab", [8, T], f32, za)
        sm = sb("sm", [P, 12, NC * NH], f32, za)
        za.close()
        zf = ExitStack()
        p_hi, p_lo = sb("p_hi", [P, FT, T], f32r, zf), sb("p_lo", [P, FT, T], f32r, zf)
        ug, uv = sb("ug", [P, T + 2], f32, zf), sb("uv", [P, T + 2], f32, zf)
        tg, tv = sb("tg", [P, 3, T], f32, zf), sb("tv", [P, 3, T], f32, zf)
        zf.close()
        zt = ExitStack()
        y1_hi, y1_lo = sb("y1_hi", [P, PAIRS, T], f32r, zt), sb("y1_lo", [P, PAIRS, T], f32r, zt)
        q_hi, q_lo = sb("q_hi", [P, 2, T], f32r, zt), sb("q_lo", [P, 2, T], f32r, zt)
        k_hi, k_lo = sb("k_hi", [P, 2, T], f32r, zt), sb("k_lo", [P, 2, T], f32r, zt)
        v_hi, v_lo = sb("v_hi", [P, 2, NC, 2, P], f32r, zt), sb("v_lo", [P, 2, NC, 2, P], f32r, zt)
        pf = sb("pf", [P, T], f32, zt)
        vT = sb("vT", [P, T], f32, zt)
        AW = 1280
        t_ = sb("t_", [P, 2, AW], f32, zt)
        s_hi, s_lo = sb("s_hi", [P, 2, AW], f32r, zt), sb("s_lo", [P, 2, AW], f32r, zt)
        ntri, nones, negm, identr = (sb(n, [P, P], f32r, zt) for n in ("ntri", "nones", "negm", "identr"))
        zt.close()

        B = [ctx.enter_context(nc.psum_tensor(f"bank{i}", [P, T], f32)) for i in range(8)]

        names = (
            "x_in0 x_in1 par_in const_in out_w w_split_hi w_split_lo block_done x_new "
            "h_hi_done h_lo_done sq_done ssq_done stat_mm rms_ln rms_done ones_set halo_set "
            "a_free ab_t sg_beta sg_xa sg_abs sg_e sg_l sg_sp "
            "sg_ea sg_g sg_bg cols_mm cols_exp sig_done hb_done "
            "cf0 cf_tap c0_done ctap silu_done sqh_done kqss_mm kq_ln "
            "kq_r kn_done qn_done kt_mm vt_mm ktail_done kbg_done vb_done kk_mm "
            "qk_mm gu_done dn_mm dt_mm gb_mm edn_done edt_done egb_done a1_done "
            "a2_done qkd_done qkd_masked qd_done t_mm t2_done xm_mm x_done ym_mm "
            "y_done wt_mm wt_done v_mm v_done o_mm s_mm s_done oc_done "
            "osq_done oss_mm o_ln o_r on_done sz_done yb_f yb_hid "
            "yb_lod mu_mm xc_done csq_done var_mm c_ln c_r cn_done ya_f "
            "ya_hid ya_lod up_free tap0 tap1 silu_f prod prod_hi prod_lo "
            "halo_f consts_r q_f q_hid q_lod k_f k_hid k_lod v_f "
            "vt2_mm v_hid v_lod z_mm za_done ze_done zl_done sp_done "
            "sp_hid sp_lod cum_mm att_done att_hid att_lod av_mm y1_hid y1_lod "
            "vp_zero out_f t2_zero "
        )
        s = namedtuple("Sems", names)(*(sem(n) for n in names.split()))
        w_in = [sem(f"w_in{i}") for i in range(RING)]

        def col(name, i=0):
            return par[:, PAR[name] + i:PAR[name] + i + 1]

        def cm(i):
            return const[:, i, :]

        def bc(ap):
            return ap.unsqueeze(1).to_broadcast([P, NC, P])

        def flat(a):
            return a[:].rearrange("p c t -> p (c t)")

        def r3(bank):
            return bank[:].rearrange("p (c t) -> p c t", c=NC)

        def tok(i, h):
            return sm[:, i, :].rearrange("p (c h) -> p c h", h=NH)[:, :, h:h + 1].to_broadcast([P, NC, P])

        def w_load(sp, dram, b, n, r=None, m=0):
            if r is None and b >= RING:
                sp.wait_ge(s.w_split_lo, b - RING + 1)
            if r is not None:
                sp.wait_ge(s.w_split_lo, r * m + (b - RING + 1))
            sp.dma_start(stage[:, b % RING, 0:n], dram).then_inc(w_in[b % RING], 16)

        def w_hi_of(act, b, n, r=None, m=0):
            if r is None:
                act.wait_ge(w_in[b % RING], 16 * (b // RING + 1))
                if b >= RING:
                    act.wait_ge(s.block_done, b - RING + 1)
            else:
                act.wait_ge(w_in[b % RING], r * (16 * m // RING) + 16 * (b // RING + 1))
                act.wait_ge(s.block_done, r * m + (b - RING + 1))
            nc.scalar.activation(w_hi[:, b % RING, 0:n], stage[:, b % RING, 0:n], ACT.Copy).then_inc(s.w_split_hi, 1)

        def w_lo_of(dve, b, n, r=None, m=0):
            dve.wait_ge(s.w_split_hi, (b + 1) if r is None else r * m + (b + 1))
            nc.vector.tensor_tensor(w_lo[:, b % RING, 0:n], stage[:, b % RING, 0:n],
                                    w_hi[:, b % RING, 0:n].bitcast(f32), ALU.subtract).then_inc(s.w_split_lo, 1)

        def mm3(out, whi, wlo, ahi, alo, start, stop):
            nc.tensor.matmul(out, wlo, ahi, start=start, stop=False, skip_group_check=True)
            nc.tensor.matmul(out, whi, alo, start=False, stop=False, skip_group_check=True)
            return nc.tensor.matmul(out, whi, ahi, start=False, stop=stop, skip_group_check=True)

        def w_wait(pe, b, r=None, m=0):
            pe.wait_ge(s.w_split_lo, (b + 1) if r is None else r * m + (b + 1))

        def gemm(bank, b, k0, k1, ahi, alo, first, last, mcols=P, a0=0):
            for k in range(k0, k1):
                mm = mm3(bank[0:mcols, :], w_hi[:, b % RING, k * mcols:(k + 1) * mcols],
                         w_lo[:, b % RING, k * mcols:(k + 1) * mcols], ahi[:, a0 + k, :], alo[:, a0 + k, :],
                         first and k == k0, last and k == k1 - 1)
            return mm

        def norm_act(act, n, k, split, r=None, m=0):
            kk, c = (k, KT * n + k) if r is None else (r * m + k, r * m + (KT * n + k))
            act.wait_ge(s.x_new, c + 1)
            if split:
                w = par[:, bass.ds(PAR["norm"] + KT * n + kk, 1)] if r is not None else col("norm", KT * n + k)
                nc.scalar.activation(h_hi[:, kk, :] if r is None else h_hi[:, bass.ds(kk, 1), :].rearrange("p o t -> p (o t)"),
                                     x[:, kk, :] if r is None else x[:, bass.ds(kk, 1), :].rearrange("p o t -> p (o t)"),
                                     ACT.Copy, scale=w).then_inc(s.h_hi_done, 1)
            if not (r is None and c < 2):
                act.wait_ge(s.ssq_done, c - 1)
            nc.scalar.activation(sq2[:, k % 2, :], x[:, kk, :] if r is None else x[:, bass.ds(kk, 1), :].rearrange("p o t -> p (o t)"),
                                 ACT.Square).then_inc(s.sq_done, 1)

        def norm_lo(dve, n, k, r=None, m=0):
            kk, c = (k, KT * n + k) if r is None else (r * m + k, r * m + (KT * n + k))
            dve.wait_ge(s.h_hi_done, c + 1)
            if r is None:
                nc.vector.scalar_tensor_tensor(h_lo[:, k, :], x[:, k, :], col("norm", KT * n + k),
                                               h_hi[:, k, :].bitcast(f32), ALU.mult, ALU.subtract).then_inc(s.h_lo_done, 1)
            else:
                g = lambda a: a[:, bass.ds(kk, 1), :].rearrange("p o t -> p (o t)")
                nc.vector.scalar_tensor_tensor(g(h_lo), g(x), par[:, bass.ds(PAR["norm"] + KT * n + kk, 1)],
                                               g(h_hi).bitcast(f32), ALU.mult, ALU.subtract).then_inc(s.h_lo_done, 1)

        def norm_pool(pool, n):
            for k in range(KT):
                c = KT * n + k
                pool.wait_ge(s.sq_done, c + 1)
                if k == 0:
                    if n:
                        pool.wait_ge(s.stat_mm, n)
                    nc.gpsimd.tensor_scalar(ssq[:], sq2[:, 0, :], 1.0, None, ALU.mult).then_inc(s.ssq_done, 1)
                else:
                    pool.wait_ge(s.ssq_done, c)
                    nc.gpsimd.tensor_tensor(ssq[:], ssq[:], sq2[:, k % 2, :], ALU.add).then_inc(s.ssq_done, 1)

        def stat_pe(pe, n, bank):
            pe.wait_ge(s.ssq_done, KT * (n + 1))
            nc.tensor.matmul(bank[:], cm(ONES), ssq[:], start=True, stop=True).then_inc(s.stat_mm, 1)

        def stat_act(act, n, bank):
            act.preload_act_table_set("natural_log_exp_and_others")
            act.wait_ge(s.stat_mm, n + 1)
            nc.scalar.activation(rms[:], bank[:], ACT.Ln, bias=eps[:, 0:1], scale=1.0 / D).then_inc(s.rms_ln, 1)
            act.wait_ge(s.rms_ln, n + 1)
            nc.scalar.activation(rms[:], rms[:], ACT.Exp, scale=-0.5).then_inc(s.rms_done, 1)

        ORDER = [("ab", 0)] + [(c, i) for i in range(CA) for c in ("g", "v")] + \
                [(c, h) for h in range(NH) for c in ("k", "q", "u")] + [("z", h) for h in range(NH)]
        GB = {kind: g for g, kind in enumerate(ORDER)}
        n_of = lambda g: 64 if g == 0 else D

        def nblk(b):
            if b == 0:
                return 64
            for size, kind in ((NB0, 0), (NBO0, 2), (NBU, 0), (NBD, 1), (NBQ + NBO1, 0), (NBU, 0), (NBD, 1)):
                if b < size:
                    return DOWN[b % 3] * P if kind == 1 else D // 2 if kind == 2 else D
                b -= size
            return 0
        BO0 = NB0
        BU0 = BO0 + NBO0
        BD0 = BU0 + NBU
        BQ = BD0 + NBD
        BO1 = BQ + NBQ
        BU1 = BO1 + NBO1
        BD1 = BU1 + NBU
        BEND = BD1 + NBD

        TAPS = CA * (C31 - 1)
        LEAD = 12
        even = [(i, j) for i in (0, 2) for j in range(1, C31)]
        odd = [(i, j) for i in (1, 3) for j in range(1, C31)]
        TAP = even[:LEAD]
        for a_, b_ in zip(odd, even[LEAD:]):
            TAP += [a_, b_]
        TAP += odd[len(even) - LEAD:]
        EARLY = (0, 0, 0, 0, 3, 4, 4, 5, 4, 6, 6, 6)
        TAPS0, TAPS1, TAPS2 = 4, 2, 2
        tap_next = [0]

        def taps(dve, n):
            for _ in range(min(n, TAPS - tap_next[0])):
                i, j = TAP[tap_next[0]]
                if j == 1:
                    dve.wait_ge(s.cf0, i + 1)
                else:
                    dve.wait_ge(s.cf_tap, TAP.index((i, j - 1)) + 1)
                nc.vector.scalar_tensor_tensor(tc[:, i, :], hb[:, i, j:j + T], col("c31", i * C31 + j), tc[:, i, :],
                                               ALU.mult, ALU.add).then_inc(s.cf_tap, 1)
                tap_next[0] += 1

        def post_evac(dve, g):
            kind, i = ORDER[g]
            bank = B[g % 2]
            dve.wait_ge(s.block_done, g + 1)
            if kind == "ab":
                dve.wait_ge(s.rms_done, 1)
                nc.vector.tensor_tensor(ab[:], bank[0:8, :], rms[0:8, :], ALU.mult).then_inc(s.a_free, 1)
            elif kind == "g":
                if i:
                    dve.wait_ge(s.hb_done, i)
                nc.vector.tensor_tensor(sig[:], bank[:], rms[:], ALU.mult).then_inc(s.a_free, 1)
            elif kind == "v":
                nc.vector.tensor_tensor(hb[:, i, C31 - 1:], bank[:], rms[:], ALU.mult).then_inc(s.a_free, 1)
            elif kind == "z":
                if i:
                    dve.wait_ge(s.yb_f, i)
                nc.vector.tensor_tensor(sig[:], bank[:], rms[:], ALU.mult).then_inc(s.a_free, 1)
            else:
                m = 3 * i + "kqu".index(kind)
                if m:
                    dve.wait_ge(s.ctap, 3 * m)
                nc.vector.tensor_tensor(cb[:, 3:], bank[:], rms[:], ALU.mult).then_inc(s.a_free, 1)

        def glu(dve, g):
            i = ORDER[g][1]
            dve.wait_ge(s.a_free, g + 1)
            dve.wait_ge(s.sig_done, i + 1)
            nc.vector.tensor_tensor(hb[:, i, C31 - 1:], hb[:, i, C31 - 1:], sig[:], ALU.mult).then_inc(s.hb_done, 1)

        def short_tap(dve, g, j):
            kind, i = ORDER[g]
            if kind not in "kqu":
                taps(dve, 1)
                return
            m = 3 * i + "kqu".index(kind)
            dst = (sk, sq, sv)["kqu".index(kind)]
            tile = {"k": NH, "q": 0, "u": 2 * NH}[kind] + i
            if j == 1:
                dve.wait_ge(s.c0_done, m + 1)
            else:
                dve.wait_ge(s.ctap, 3 * m + j - 1)
            nc.vector.scalar_tensor_tensor(dst[:], cb[:, j:j + T], col("c4", tile * 4 + j), dst[:],
                                           ALU.mult, ALU.add).then_inc(s.ctap, 1)

        def post_act0(act, g):
            kind, i = ORDER[g]
            if kind == "g":
                act.wait_ge(s.a_free, g + 1)
                nc.scalar.activation(sig[:], sig[:], ACT.Sigmoid).then_inc(s.sig_done, 1)
            elif kind == "v":
                act.wait_ge(s.hb_done, i + 1)
                nc.scalar.activation(tc[:, i, :], hb[:, i, 0:T], ACT.Identity, scale=col("c31", i * C31),
                                     bias=col("dwb", i)).then_inc(s.cf0, 1)
            elif kind in "kqu":
                m = 3 * i + "kqu".index(kind)
                dst = (sk, sq, sv)["kqu".index(kind)]
                tile = {"k": NH, "q": 0, "u": 2 * NH}[kind] + i
                act.wait_ge(s.a_free, g + 1)
                if i:
                    act.wait_ge((s.kn_done, s.qn_done, s.vt_mm)["kqu".index(kind)], i)
                nc.scalar.activation(dst[:], cb[:, 0:T], ACT.Copy, scale=col("c4", tile * 4)).then_inc(s.c0_done, 1)
            elif kind == "z":
                act.wait_ge(s.a_free, g + 1)
                nc.scalar.activation(sig[:], sig[:], ACT.Silu).then_inc(s.sz_done, 1)

        def post_act1(act, g):
            kind, i = ORDER[g]
            if kind not in "kqu":
                return
            m = 3 * i + "kqu".index(kind)
            dst = (sk, sq, sv)["kqu".index(kind)]
            act.wait_ge(s.ctap, 3 * m + 3)
            nc.scalar.activation(dst[:], dst[:], ACT.Silu).then_inc(s.silu_done, 1)
            if kind != "u":
                n = 2 * i + (kind == "q")
                act.wait_ge(s.silu_done, m + 1)
                if n >= 2:
                    act.wait_ge(s.kqss_mm, n - 1)
                nc.scalar.activation(sqb[:, n % 2, :], dst[:], ACT.Square).then_inc(s.sqh_done, 1)

        def ab_pe(pe):
            pe.wait_ge(s.const_in, 16)
            pe.wait_ge(s.a_free, 1)
            for c in range(NC):
                mm = nc.tensor.transpose(B[3][:, c * 8:(c + 1) * 8], ab[:, c * P:(c + 1) * P], const[0:8, IDENT, 0:8])
            mm.then_inc(s.ab_t, 1)
            pe.wait_ge(s.sg_g, 1)
            for i, m in enumerate((UPPER, AFTER, ONES)):
                mm = nc.tensor.matmul(B[3][:, 16 * i:16 * i + 16], cm(m), sm[:, 4, :], start=(i == 0), stop=(i == 2),
                                      skip_group_check=True)
            mm.then_inc(s.cols_mm, 1)

        def ab_act(act):
            pa = B[3][:, 0:32].rearrange("p (c k) -> p c k", k=8)
            v = lambda i: sm[:, i, :].rearrange("p (c h) -> p c h", h=NH)
            act.wait_ge(s.sg_xa, 1)
            nc.scalar.activation(v(0), pa[:, :, NH:2 * NH], ACT.Sigmoid).then_inc(s.sg_beta, 1)
            act.preload_act_table_set("natural_log_exp_and_others")
            act.wait_ge(s.sg_abs, 1)
            nc.scalar.activation(sm[:, 2, :], sm[:, 2, :], ACT.Exp).then_inc(s.sg_e, 1)
            act.wait_ge(s.sg_e, 1)
            nc.scalar.activation(sm[:, 3, :], sm[:, 2, :], ACT.Ln, bias=1.0).then_inc(s.sg_l, 1)
            nc.scalar.activation(sm[:, 9, 0:NH], par[:, PAR["alog"]:PAR["alog"] + NH], ACT.Exp).then_inc(s.sg_ea, 1)
            act.wait_ge(s.cols_mm, 1)
            nc.scalar.activation(sm[:, 5:8, :].rearrange("p a b -> p (a b)"), B[3][:, 0:48], ACT.Exp).then_inc(s.cols_exp, 1)

        def ab_dve(dve):
            pa = B[3][:, 0:32].rearrange("p (c k) -> p c k", k=8)
            v = lambda i: sm[:, i, :].rearrange("p (c h) -> p c h", h=NH)
            hbc = lambda ap: ap.unsqueeze(1).to_broadcast([P, NC, NH])
            dve.wait_ge(s.ab_t, 1)
            nc.vector.tensor_tensor(v(1), pa[:, :, 0:NH], hbc(par[:, PAR["dtb"]:PAR["dtb"] + NH]), ALU.add).then_inc(s.sg_xa, 1)
            dve.wait_ge(s.sg_xa, 1)
            nc.vector.scalar_tensor_tensor(sm[:, 2, :], sm[:, 1, :], -1.0, sm[:, 1, :], ALU.mult, ALU.min).then_inc(s.sg_abs, 1)
            dve.wait_ge(s.sg_l, 1)
            nc.vector.scalar_tensor_tensor(sm[:, 10, :], sm[:, 1, :], 0.0, sm[:, 3, :], ALU.max, ALU.add).then_inc(s.sg_sp, 1)
            dve.wait_ge(s.sg_ea, 1)
            dve.wait_ge(s.sg_sp, 1)
            nc.vector.scalar_tensor_tensor(v(4), v(10), -1.0, hbc(sm[:, 9, 0:NH]), ALU.mult, ALU.mult).then_inc(s.sg_g, 1)
            dve.wait_ge(s.cols_exp, 1)
            nc.vector.tensor_tensor(sm[:, 8, :], sm[:, 0, :], sm[:, 5, :], ALU.mult).then_inc(s.sg_bg, 1)

        def l2_pe(pe, h):
            if h:
                pe.wait_ge(s.y_done, LEVELS * h)
            for j in range(2):
                pe.wait_ge(s.sqh_done, 2 * h + j + 1)
                nc.tensor.matmul(B[3 + j][:], cm(ONES), sqb[:, j, :], start=True, stop=True).then_inc(s.kqss_mm, 1)

        def l2_act(act, h):
            act.preload_act_table_set("natural_log_exp_and_others")
            for j in range(2):
                act.wait_ge(s.kqss_mm, 2 * h + j + 1)
                nc.scalar.activation(rkq[:, j, :], B[3 + j][:], ACT.Ln, bias=eps[:, 0:1]).then_inc(s.kq_ln, 1)
            for j in range(2):
                act.wait_ge(s.kq_ln, 2 * h + j + 1)
                nc.scalar.activation(rkq[:, j, :], rkq[:, j, :], ACT.Exp, scale=-0.5).then_inc(s.kq_r, 1)

        def kn_dve(dve, h):
            dve.wait_ge(s.kq_r, 2 * h + 1)
            if h:
                dve.wait_ge(s.kt_mm, h)
            nc.vector.tensor_tensor(flat(kn), sk[:], rkq[:, 0, :], ALU.mult).then_inc(s.kn_done, 1)

        def qn_dve(dve, h):
            dve.wait_ge(s.kq_r, 2 * h + 2)
            nc.vector.scalar_tensor_tensor(flat(qn), sq[:], P ** -0.5, rkq[:, 1, :], ALU.mult, ALU.mult).then_inc(s.qn_done, 1)

        def gu_pool(pool, h):
            if h:
                pool.wait_ge(s.gb_mm, h)
            nc.gpsimd.tensor_tensor(gU[:], bc(cm(UPPER)), tok(4, h), ALU.mult).then_inc(s.gu_done, 1)

        def dn_pe(pe, h):
            pe.wait_ge(s.gu_done, h + 1)
            for c in range(NC):
                mm = nc.tensor.matmul(B[5][:, c * P:(c + 1) * P], gU[:, c, :], cm(AFTER), start=True, stop=True)
            mm.then_inc(s.dn_mm, 1)

        def dn_act(act, h):
            act.wait_ge(s.dn_mm, h + 1)
            nc.scalar.activation(flat(eDn), B[5][:], ACT.Exp).then_inc(s.edn_done, 1)

        def kk_pe(pe, h):
            pe.wait_ge(s.kn_done, h + 1)
            pe.wait_ge(s.kq_ln, 2 * h + 1)
            for c in range(NC):
                mm = nc.tensor.matmul(B[3][:, c * P:(c + 1) * P], kn[:, c, :], kn[:, c, :], start=True, stop=True)
            mm.then_inc(s.kk_mm, 1)

        def a1_dve(dve, h):
            dve.wait_ge(s.kk_mm, h + 1)
            dve.wait_ge(s.edn_done, h + 1)
            nc.vector.tensor_tensor(eDn[:], r3(B[3]), eDn[:], ALU.mult).then_inc(s.a1_done, 1)

        def a2_dve(dve, h):
            dve.wait_ge(s.a1_done, h + 1)
            nc.vector.tensor_tensor(eDn[:], eDn[:], tok(0, h), ALU.mult).then_inc(s.a2_done, 1)

        def dt_pe(pe, h):
            if h:
                pe.wait_ge(s.v_done, NC * h)
            nc.tensor.matmul(B[6][:], cm(AFTER), flat(gU), start=True, stop=True).then_inc(s.dt_mm, 1)

        def qk_pe(pe, h):
            pe.wait_ge(s.qn_done, h + 1)
            if h:
                pe.wait_ge(s.kbg_done, h)
            for c in range(NC):
                mm = nc.tensor.matmul(B[2][:, c * P:(c + 1) * P], kn[:, c, :], qn[:, c, :], start=True, stop=True)
            mm.then_inc(s.qk_mm, 1)

        def kt_pe(pe, h):
            pe.wait_ge(s.qkd_done, h + 1)
            for c in range(NC):
                mm = nc.tensor.transpose(B[2][:, c * P:(c + 1) * P], kn[:, c, :], cm(IDENT))
            mm.then_inc(s.kt_mm, 1)

        def gb_pe(pe, h):
            pe.wait_ge(s.edt_done, h + 1)
            nc.tensor.matmul(B[6][:], cm(ONES), flat(gU), start=True, stop=True).then_inc(s.gb_mm, 1)

        def vt0_pe(pe, h):
            pe.wait_ge(s.silu_done, 3 * h + 3)
            pe.wait_ge(s.egb_done, h + 1)
            for c in range(NC):
                mm = nc.tensor.transpose(B[6][:, c * P:(c + 1) * P], sv[:, c * P:(c + 1) * P], cm(IDENT))
            mm.then_inc(s.vt_mm, 1)

        def dt_act(act, h):
            act.wait_ge(s.dt_mm, h + 1)
            nc.scalar.activation(flat(qkd), B[6][:], ACT.Exp).then_inc(s.edt_done, 1)

        def gb_act(act, h):
            act.wait_ge(s.gb_mm, h + 1)
            nc.scalar.activation(flat(qd), B[6][:], ACT.Exp).then_inc(s.egb_done, 1)

        def scaled_act(dst, bank, i, h, done):
            for c in range(NC):
                a = nc.scalar.activation(dst[:, c, :], bank[:, c * P:(c + 1) * P], ACT.Copy,
                                         scale=sm[:, i, NH * c + h:NH * c + h + 1])
            a.then_inc(done, 1)

        def kt_act(act, h):
            act.wait_ge(s.kt_mm, h + 1)
            scaled_act(ktail, B[2], 6, h, s.ktail_done)
            scaled_act(kbg, B[2], 8, h, s.kbg_done)

        def vt0_act(act, h):
            act.wait_ge(s.vt_mm, h + 1)
            scaled_act(vb, B[6], 0, h, s.vb_done)

        def qkd_dve(dve, h):
            dve.wait_ge(s.qk_mm, h + 1)
            dve.wait_ge(s.edt_done, h + 1)
            nc.vector.tensor_tensor(qkd[:], r3(B[2]), qkd[:], ALU.mult).then_inc(s.qkd_done, 1)

        def qkd_pool(pool, h):
            pool.wait_ge(s.qkd_done, h + 1)
            nc.gpsimd.affine_select(out=qkd[:], in_=qkd[:], compare_op=ALU.is_ge, fill=0.0, base=0,
                                    pattern=[[0, NC], [1, P]], channel_multiplier=-1).then_inc(s.qkd_masked, 1)

        def qd_dve(dve, h):
            dve.wait_ge(s.egb_done, h + 1)
            nc.vector.tensor_tensor(qd[:], qd[:], qn[:], ALU.mult).then_inc(s.qd_done, 1)

        HP = P // 2

        def half(a, l, odd):
            return a.rearrange("p (g two b) -> p g two b", two=2, b=1 << l)[:, :, odd, :]

        def halves(a, l, odd):
            return a.rearrange("p c (g two b) -> p c g two b", two=2, b=1 << l)[:, :, :, odd, :]

        def packed(bank, l):
            return bank[:, 0:NC * HP].rearrange("p (c g b) -> p c g b", c=NC, b=1 << l)

        def inv_t_pe(pe, h, l):
            n = LEVELS * h + l
            if l == 0:
                pe.wait_ge(s.a2_done, h + 1)
            else:
                pe.wait_ge(s.y_done, n)
            for c in range(NC):
                mm = nc.tensor.matmul(B[3][:, c * HP:(c + 1) * HP], eDn[:, c, :], half(Y[:, c, :] if l else cm(IDENT), l, 1),
                                      start=True, stop=True)
            mm.then_inc(s.t_mm, 1)

        def inv_xy_pe(pe, h, l):
            n = LEVELS * h + l
            t2 = T2[:, n % 2]
            pe.wait_ge(s.t2_done, n + 1)
            if l == 0:
                for c in range(NC):
                    mm = nc.tensor.matmul(B[4][:, c * P:(c + 1) * P], t2[:, c, :], cm(IDENT), start=True, stop=True)
                mm.then_inc(s.xm_mm, 1)
                return
            if l < LEVELS - 1:
                pe.wait_ge(s.x_done, (LEVELS - 1) * h + l)
                for c in range(NC):
                    mm = nc.tensor.matmul(B[4][:, c * HP:(c + 1) * HP], t2[:, c, :], half(X[:, c, :], l, 0),
                                          start=True, stop=True)
                mm.then_inc(s.xm_mm, 1)
            for c in range(NC):
                mm = nc.tensor.matmul(B[5][:, c * HP:(c + 1) * HP], X[:, c, :], half(t2[:, c, :], l, 1), start=True, stop=True)
            mm.then_inc(s.ym_mm, 1)

        def inv_t_dve(dve, h, l):
            n = LEVELS * h + l
            dve.wait_ge(s.t_mm, n + 1)
            dve.wait_ge(s.t2_zero, n + 1)
            nc.vector.tensor_tensor(halves(T2[:, n % 2], l, 1), packed(B[3], l),
                                    half(cm(LEV0 + l), l, 1).unsqueeze(1).to_broadcast([P, NC, HP >> l, 1 << l]),
                                    ALU.mult).then_inc(s.t2_done, 1)

        def inv_xy_dve(dve, h, l):
            n = LEVELS * h + l
            if l == 0:
                dve.wait_ge(s.t2_done, n + 1)
                if h:
                    dve.wait_ge(s.o_mm, h)
                nc.vector.tensor_tensor(Y[:], bc(cm(IDENT)), T2[:, n % 2], ALU.subtract).then_inc(s.y_done, 1)
                dve.wait_ge(s.xm_mm, (LEVELS - 1) * h + 1)
                nc.vector.tensor_tensor(X[:], bc(cm(IDENT)), r3(B[4]), ALU.subtract).then_inc(s.x_done, 1)
                return
            dve.wait_ge(s.ym_mm, (LEVELS - 1) * h + l)
            dve.wait_ge(s.y_done, n)
            nc.vector.tensor_tensor(halves(Y, l, 1), halves(Y, l, 1), packed(B[5], l), ALU.subtract).then_inc(s.y_done, 1)
            if l < LEVELS - 1:
                dve.wait_ge(s.x_done, (LEVELS - 1) * h + l)
                nc.vector.tensor_tensor(halves(X, l, 0), halves(X, l, 0), packed(B[4], l), ALU.subtract).then_inc(s.x_done, 1)

        def t2_zero_pool(pool, h, l):
            n = LEVELS * h + l
            if n >= 2:
                h2, l2 = divmod(n - 2, LEVELS)
                if l2:
                    pool.wait_ge(s.ym_mm, (LEVELS - 1) * h2 + l2)
                else:
                    pool.wait_ge(s.y_done, n - 1)
                    pool.wait_ge(s.xm_mm, (LEVELS - 1) * h2 + 1)
            nc.gpsimd.memset(T2[:, n % 2], 0.0).then_inc(s.t2_zero, 1)

        def wt_pe(pe, h):
            pe.wait_ge(s.y_done, LEVELS * (h + 1))
            pe.wait_ge(s.kbg_done, h + 1)
            pe.wait_ge(s.vb_done, h + 1)
            for c in range(NC):
                mm = nc.tensor.matmul(B[6][:, c * P:(c + 1) * P], kbg[:, c, :], Y[:, c, :], start=True, stop=True)
            mm.then_inc(s.wt_mm, 1)

        def wt_act(act, h):
            act.wait_ge(s.wt_mm, h + 1)
            nc.scalar.activation(nWT[:].rearrange("p c t -> p (c t)"), B[6][:], ACT.Copy, scale=-1.0).then_inc(s.wt_done, 1)

        def seq_v_pe(pe, h, c):
            if c == 0:
                pe.wait_ge(s.wt_done, h + 1)
            else:
                pe.wait_ge(s.s_done, (NC - 1) * h + c)
            mm = nc.tensor.matmul(B[6][:, 0:P], Y[:, c, :], vb[:, c, :], start=True, stop=(c == 0))
            if c:
                mm = nc.tensor.matmul(B[6][:, 0:P], nWT[:, c, :], S[:], start=False, stop=True)
            mm.then_inc(s.v_mm, 1)

        def seq_o_pe(pe, h, c):
            if c == 0:
                pe.wait_ge(s.qkd_masked, h + 1)
                pe.wait_ge(s.qd_done, h + 1)
                if h:
                    pe.wait_ge(s.o_ln, h)
            else:
                nc.tensor.matmul(B[7][:, c * P:(c + 1) * P], S[:], qd[:, c, :], start=False, stop=False,
                                 skip_group_check=True)
            pe.wait_ge(s.v_done, NC * h + c + 1)
            mm = nc.tensor.matmul(B[7][:, c * P:(c + 1) * P], vnew[:], qkd[:, c, :], start=(c == 0), stop=True,
                                  skip_group_check=True)
            if c == NC - 1:
                mm.then_inc(s.o_mm, 1)
            else:
                nc.tensor.matmul(B[6][:, P:2 * P], ktail[:, c, :], vnew[:], start=True, stop=True).then_inc(s.s_mm, 1)

        def seq_act(act, h, c):
            act.wait_ge(s.v_mm, NC * h + c + 1)
            nc.scalar.activation(vnew[:], B[6][:, 0:P], ACT.Copy).then_inc(s.v_done, 1)

        def seq_dve(dve, h, c):
            n = (NC - 1) * h + c
            dve.wait_ge(s.s_mm, n + 1)
            if c == 0:
                nc.vector.tensor_copy(S[:], B[6][:, P:2 * P]).then_inc(s.s_done, 1)
            else:
                dve.wait_ge(s.s_done, n)
                nc.vector.scalar_tensor_tensor(S[:], S[:], sm[:, 7, NH * c + h:NH * c + h + 1], B[6][:, P:2 * P],
                                               ALU.mult, ALU.add).then_inc(s.s_done, 1)

        def on_pe(pe, h):
            pe.wait_ge(s.osq_done, h + 1)
            nc.tensor.matmul(B[7][:], cm(ONES), ro[:], start=True, stop=True).then_inc(s.oss_mm, 1)

        def on_act(act, h):
            act.wait_ge(s.o_mm, h + 1)
            nc.scalar.activation(oc[:, h, :], B[7][:], ACT.Copy).then_inc(s.oc_done, 1)
            if h:
                act.wait_ge(s.on_done, h)
            act.wait_ge(s.oc_done, h + 1)
            nc.scalar.activation(ro[:], oc[:, h, :], ACT.Square).then_inc(s.osq_done, 1)

        def on_act2(act, h):
            act.wait_ge(s.oss_mm, h + 1)
            act.preload_act_table_set("natural_log_exp_and_others")
            nc.scalar.activation(ro[:], B[7][:], ACT.Ln, bias=eps[:, 0:1], scale=1.0 / P).then_inc(s.o_ln, 1)
            act.wait_ge(s.o_ln, h + 1)
            nc.scalar.activation(ro[:], ro[:], ACT.Exp, scale=-0.5).then_inc(s.o_r, 1)

        def on_dve(dve, h):
            dve.wait_ge(s.o_r, h + 1)
            nc.vector.scalar_tensor_tensor(oc[:, h, :], oc[:, h, :], col("onorm"), ro[:], ALU.mult,
                                           ALU.mult).then_inc(s.on_done, 1)

        def yb_dve(dve, h):
            dve.wait_ge(s.sz_done, h + 1)
            dve.wait_ge(s.on_done, h + 1)
            nc.vector.tensor_tensor(oc[:, h, :], oc[:, h, :], sig[:], ALU.mult).then_inc(s.yb_f, 1)

        def yb_act(act, h):
            act.wait_ge(s.yb_f, h + 1)
            nc.scalar.activation(yb_hi[:, h, :], oc[:, h, :], ACT.Copy).then_inc(s.yb_hid, 1)

        def yb_lo_dve(dve, h):
            dve.wait_ge(s.yb_hid, h + 1)
            nc.vector.tensor_tensor(yb_lo[:, h, :], oc[:, h, :], yb_hi[:, h, :].bitcast(f32),
                                    ALU.subtract).then_inc(s.yb_lod, 1)

        def mu_pe(pe):
            pe.wait_ge(s.cf_tap, TAPS)
            pe.wait_ge(s.wt_done, NH)
            pe.wait_ge(s.v_done, NC * NH)
            for i in range(CA):
                mm = nc.tensor.matmul(B[6][:], cm(ONES), tc[:, i, :], start=(i == 0), stop=(i == CA - 1))
            mm.then_inc(s.mu_mm, 1)

        def var_pe(pe):
            pe.wait_ge(s.o_ln, NH)
            for i in range(CA):
                pe.wait_ge(s.csq_done, i + 1)
                mm = nc.tensor.matmul(B[7][:], cm(ONES), sqb[:, i % 2, :], start=(i == 0), stop=(i == CA - 1))
                mm.then_inc(s.var_mm, 1)

        def sq_act(act):
            for i in range(CA):
                act.wait_ge(s.xc_done, i + 1)
                if i >= 2:
                    act.wait_ge(s.var_mm, i - 1)
                nc.scalar.activation(sqb[:, i % 2, :], tc[:, i, :], ACT.Square).then_inc(s.csq_done, 1)

        def var_act(act):
            act.preload_act_table_set("natural_log_exp_and_others")
            act.wait_ge(s.var_mm, CA)
            nc.scalar.activation(rkq[:, 0, :], B[7][:], ACT.Ln, bias=eps[:, 1:2], scale=1.0 / (CA * P)).then_inc(s.c_ln, 1)
            act.wait_ge(s.c_ln, 1)
            nc.scalar.activation(rkq[:, 0, :], rkq[:, 0, :], ACT.Exp, scale=-0.5).then_inc(s.c_r, 1)

        def xc_dve(dve):
            dve.wait_ge(s.mu_mm, 1)
            for i in range(CA):
                nc.vector.scalar_tensor_tensor(tc[:, i, :], B[6][:], -1.0 / (CA * P), tc[:, i, :], ALU.mult,
                                               ALU.add).then_inc(s.xc_done, 1)

        def cn_dve(dve):
            dve.wait_ge(s.c_r, 1)
            for i in range(CA):
                nc.vector.scalar_tensor_tensor(tc[:, i, :], tc[:, i, :], col("lnw", i), rkq[:, 0, :], ALU.mult,
                                               ALU.mult).then_inc(s.cn_done, 1)

        def ya_act(act):
            for i in range(CA):
                act.wait_ge(s.cn_done, i + 1)
                nc.scalar.activation(tc[:, i, :], tc[:, i, :], ACT.Silu, bias=col("lnb", i)).then_inc(s.ya_f, 1)
            for i in range(CA):
                act.wait_ge(s.ya_f, i + 1)
                nc.scalar.activation(ya_hi[:, i, :], tc[:, i, :], ACT.Copy).then_inc(s.ya_hid, 1)

        def ya_dve(dve):
            for i in range(CA):
                dve.wait_ge(s.ya_hid, i + 1)
                nc.vector.tensor_tensor(ya_lo[:, i, :], tc[:, i, :], ya_hi[:, i, :].bitcast(f32),
                                        ALU.subtract).then_inc(s.ya_lod, 1)

        def out0_pe(pe):
            def half_block(j):
                n, a0 = j % KT, 0 if j >= KT else CA
                b = BO0 + j
                w_wait(pe, b)
                if j == 0:
                    pe.wait_ge(s.a_free, NB0)
                if j == 6:
                    pe.wait_ge(s.xc_done, CA)
                if j == 7:
                    pe.wait_ge(s.c_ln, 1)
                for k in range(CA):
                    if j == 0:
                        pe.wait_ge(s.yb_lod, k + 1)
                    if j == KT:
                        pe.wait_ge(s.ya_lod, k + 1)
                    ahi, alo = (ya_hi, ya_lo) if j >= KT else (yb_hi, yb_lo)
                    mm = mm3(B[n][:], w_hi[:, b % RING, k * P:(k + 1) * P], w_lo[:, b % RING, k * P:(k + 1) * P],
                             ahi[:, k, :], alo[:, k, :], j < KT and k == 0, j >= KT and k == CA - 1)
                mm.then_inc(s.block_done, 1)
            mu_pe(pe)
            for j in range(3):
                half_block(j)
            var_pe(pe)
            for j in range(3, 2 * KT):
                half_block(j)

        def out0_act(act):
            split_act(act, BO0 + 3)
            sq_act(act)
            split_act(act, BO0 + 4)
            split_act(act, BO0 + 5)
            var_act(act)
            for j in range(3, 6):
                split_act(act, BO0 + j + 3)
            ya_act(act)
            for j in range(6, 8):
                split_act(act, BO0 + j + 3)
            for n in range(KT):
                split_act(act, BO0 + KT + n + 3)
                rnorm_act(act, 1, n, False)

        def out0_dve(dve):
            xc_dve(dve)
            for j in range(3):
                split_dve(dve, BO0 + j + 3)
            cn_dve(dve)
            for j in range(3, 6):
                split_dve(dve, BO0 + j + 3)
            ya_dve(dve)
            for j in range(6, 8):
                split_dve(dve, BO0 + j + 3)
            for n in range(KT):
                dve.wait_ge(s.block_done, BO0 + KT + n + 1)
                nc.vector.tensor_tensor(x[:, n, :], x[:, n, :], B[n][:], ALU.add).then_inc(s.x_new, 1)
                split_dve(dve, BO0 + KT + n + 3)
                rnorm_lo(dve, 1, n)

        def window(g):
            return ((g - 12) % 3, (g - 12) // 3) if g >= 12 else (None, None)

        def a_pe(pe):
            for g in range(NB0):
                w_wait(pe, g)
                if g >= 2:
                    pe.wait_ge(s.a_free, g - 1)
                bank = B[g % 2]
                mc = 8 if g == 0 else P

                def part(k0, k1):
                    mm = gemm(bank, g, k0, k1, h_hi, h_lo, k0 == 0, k1 == KT, mc)
                    if k1 == KT:
                        mm.then_inc(s.block_done, 1)
                w, h = window(g)
                if g == 0:
                    for k in range(KT):
                        pe.wait_ge(s.h_lo_done, k + 1)
                        part(k, k + 1)
                    pe.wait_ge(s.const_in, 16)
                    stat_pe(pe, 0, B[7])
                elif w == 0:
                    now, last = h < NH, h > 0
                    if now:
                        l2_pe(pe, h)
                    if last:
                        wt_pe(pe, h - 1)
                    part(0, 1)
                    if now:
                        dn_pe(pe, h)
                    for c in range(NC):
                        part(2 * c + 1, 2 * c + 2)
                        if c == 1 and now:
                            kk_pe(pe, h)
                        if last:
                            seq_v_pe(pe, h - 1, c)
                        if c < NC - 1:
                            part(2 * c + 2, 2 * c + 3)
                        if last:
                            seq_o_pe(pe, h - 1, c)
                elif w == 1:
                    inv_t_pe(pe, h, 0)
                    part(0, 1)
                    qk_pe(pe, h)
                    inv_xy_pe(pe, h, 0)
                    dt_pe(pe, h)
                    part(1, 2)
                    inv_t_pe(pe, h, 1)
                    if h:
                        on_pe(pe, h - 1)
                    part(2, 3)
                    inv_xy_pe(pe, h, 1)
                    gb_pe(pe, h)
                    part(3, 4)
                    inv_t_pe(pe, h, 2)
                    part(4, 5)
                    inv_xy_pe(pe, h, 2)
                    kt_pe(pe, h)
                    part(5, 6)
                    vt0_pe(pe, h)
                    part(6, 8)
                elif w == 2:
                    for l in range(3, LEVELS):
                        inv_t_pe(pe, h, l)
                        part(2 * l - 6, 2 * l - 5)
                        inv_xy_pe(pe, h, l)
                        part(2 * l - 5, 2 * l - 4)
                else:
                    part(0, KT)
                if g == 2:
                    ab_pe(pe)
            on_pe(pe, NH - 1)

        def split_act(act, b):
            if b < BEND:
                w_hi_of(act, b, nblk(b))

        def split_dve(dve, b):
            if b < BEND:
                w_lo_of(dve, b, nblk(b))

        def a_act(act):
            act.wait_ge(s.par_in, 16)
            act.wait_ge(s.ones_set, 1)
            for k in range(KT):
                norm_act_in(act, k)
                if k < RING:
                    split_act(act, k)
            stat_act(act, 0, B[7])
            for g in range(NB0):
                w, h = window(g)
                if w == 0:
                    if h < NH:
                        l2_act(act, h)
                    post_act0(act, g - 1)
                    if h:
                        wt_act(act, h - 1)
                        seq_act(act, h - 1, 0)
                    split_act(act, g + 2)
                    if h < NH:
                        dn_act(act, h)
                    if h:
                        for c in range(1, NC):
                            seq_act(act, h - 1, c)
                    post_act1(act, g - 1)
                    if h:
                        on_act(act, h - 1)
                elif w == 1:
                    post_act0(act, g - 1)
                    dt_act(act, h)
                    split_act(act, g + 2)
                    if h:
                        on_act2(act, h - 1)
                    gb_act(act, h)
                    kt_act(act, h)
                    vt0_act(act, h)
                    post_act1(act, g - 1)
                elif w == 2:
                    post_act0(act, g - 1)
                    split_act(act, g + 2)
                    post_act1(act, g - 1)
                elif g >= 1:
                    split_act(act, g + 2)
                    post_act0(act, g - 1)
                    post_act1(act, g - 1)
                if g == 3:
                    ab_act(act)
                if g >= 1 and ORDER[g - 1][0] == "z":
                    yb_act(act, ORDER[g - 1][1])
            split_act(act, NB0 + 2)
            on_act2(act, NH - 1)
            post_act0(act, NB0 - 1)
            yb_act(act, NH - 1)

        def norm_act_in(act, k):
            act.wait_ge(s.x_in0 if k < 4 else s.x_in1, 16)
            nc.scalar.activation(h_hi[:, k, :], x[:, k, :], ACT.Copy, scale=col("norm", k)).then_inc(s.h_hi_done, 1)
            if k >= 2:
                act.wait_ge(s.ssq_done, k - 1)
            nc.scalar.activation(sq2[:, k % 2, :], x[:, k, :], ACT.Square).then_inc(s.sq_done, 1)

        def a_dve(dve):
            for a in (hb[:, :, 0:C31 - 1], cb[:, 0:3]):
                nc.vector.memset(a, 0.0).then_inc(s.halo_set, 1)
            dve.wait_ge(s.x_in0, 16)
            dve.wait_ge(s.x_in1, 16)
            dve.wait_ge(s.par_in, 16)
            dve.wait_ge(s.halo_set, 2)
            for k in range(KT):
                norm_lo(dve, 0, k)
                if k < RING:
                    split_dve(dve, k)
            dve.wait_ge(s.const_in, 16)
            for g in range(NB0):
                w, h = window(g)
                if w is None and g >= 1:
                    split_dve(dve, g + 2)
                    post_evac(dve, g - 1)
                    kind = ORDER[g - 1][0]
                    if kind == "v":
                        taps(dve, EARLY[g] // 2)
                        glu(dve, g - 1)
                        taps(dve, EARLY[g] - EARLY[g] // 2)
                    elif kind in "kqu":
                        for j in range(1, 4):
                            taps(dve, EARLY[g] // 3)
                            short_tap(dve, g - 1, j)
                    else:
                        taps(dve, EARLY[g])
                elif w == 0:
                    post_evac(dve, g - 1)
                    taps(dve, 1)
                    if h < NH:
                        kn_dve(dve, h)
                        qn_dve(dve, h)
                    short_tap(dve, g - 1, 1)
                    if h:
                        seq_dve(dve, h - 1, 0)
                    split_dve(dve, g + 2)
                    if h < NH:
                        a1_dve(dve, h)
                    short_tap(dve, g - 1, 2)
                    if h:
                        seq_dve(dve, h - 1, 1)
                    if h < NH:
                        a2_dve(dve, h)
                    short_tap(dve, g - 1, 3)
                    taps(dve, 1)
                    if h:
                        seq_dve(dve, h - 1, 2)
                    taps(dve, TAPS0)
                elif w == 1:
                    inv_t_dve(dve, h, 0)
                    post_evac(dve, g - 1)
                    inv_xy_dve(dve, h, 0)
                    qkd_dve(dve, h)
                    taps(dve, TAPS1)
                    inv_t_dve(dve, h, 1)
                    split_dve(dve, g + 2)
                    short_tap(dve, g - 1, 1)
                    inv_xy_dve(dve, h, 1)
                    short_tap(dve, g - 1, 2)
                    taps(dve, TAPS1 - 1)
                    inv_t_dve(dve, h, 2)
                    qd_dve(dve, h)
                    short_tap(dve, g - 1, 3)
                    taps(dve, TAPS1 - 1)
                    inv_xy_dve(dve, h, 2)
                    if h:
                        on_dve(dve, h - 1)
                    taps(dve, TAPS1)
                elif w == 2:
                    inv_t_dve(dve, h, 3)
                    post_evac(dve, g - 1)
                    taps(dve, 1)
                    inv_xy_dve(dve, h, 3)
                    short_tap(dve, g - 1, 1)
                    for l in range(4, LEVELS):
                        inv_t_dve(dve, h, l)
                        if l == 4:
                            split_dve(dve, g + 2)
                        else:
                            taps(dve, TAPS2)
                        inv_xy_dve(dve, h, l)
                        if l < 6:
                            short_tap(dve, g - 1, l - 2)
                if g == 3:
                    ab_dve(dve)
                if g >= 1 and ORDER[g - 1][0] == "z":
                    yb_dve(dve, ORDER[g - 1][1])
                    yb_lo_dve(dve, ORDER[g - 1][1])
            taps(dve, TAPS)
            split_dve(dve, NB0 + 2)
            post_evac(dve, NB0 - 1)
            on_dve(dve, NH - 1)
            yb_dve(dve, NH - 1)
            yb_lo_dve(dve, NH - 1)

        def a_pool(pool):
            for l in range(2):
                t2_zero_pool(pool, 0, l)
            norm_pool(pool, 0)
            pool.wait_ge(s.sg_g, 1)
            gu_pool(pool, 0)
            for h in range(NH):
                for l in range(LEVELS):
                    if LEVELS * h + l >= 2:
                        t2_zero_pool(pool, h, l)
                    if l == 2:
                        qkd_pool(pool, h)
                    if l == 4 and h < NH - 1:
                        gu_pool(pool, h + 1)

        def resid_dve(dve, r, n, b_last, it=None):
            if it is None:
                dve.wait_ge(s.block_done, b_last + 1)
                xt = x[:, n, :]
            else:
                i, mt, mb = it
                dve.wait_ge(s.block_done, i * mb + (b_last + 1))
                xt = x[:, bass.ds(i * mt + n, 1), :].rearrange("p o t -> p (o t)")
            nc.vector.tensor_tensor(xt, xt, B[6 + n % 2][:], ALU.add).then_inc(s.x_new, 1)

        def rnorm_act(act, r, n, last, it=None):
            i, mt = (None, 0) if it is None else it[:2]
            xn = KT * (r - 1) + n
            c = KT * r + n
            g = lambda a: a[:, n, :] if it is None else a[:, bass.ds(i * mt + n, 1), :].rearrange("p o t -> p (o t)")
            at = lambda v: v if it is None else i * mt + v
            act.wait_ge(s.ssq_done, at(c - 1))
            act.wait_ge(s.x_new, at(xn + 1))
            if not last:
                w = col("norm", KT * r + n) if it is None else par[:, bass.ds(i * mt + (PAR["norm"] + KT * r + n), 1)]
                nc.scalar.activation(g(h_hi), g(x), ACT.Copy, scale=w).then_inc(s.h_hi_done, 1)
            nc.scalar.activation(sq2[:, n % 2, :], g(x), ACT.Square).then_inc(s.sq_done, 1)

        def rnorm_lo(dve, r, n, it=None):
            i, mt = (None, 0) if it is None else it[:2]
            c = KT * r + n
            g = lambda a: a[:, n, :] if it is None else a[:, bass.ds(i * mt + n, 1), :].rearrange("p o t -> p (o t)")
            w = col("norm", KT * r + n) if it is None else par[:, bass.ds(i * mt + (PAR["norm"] + KT * r + n), 1)]
            dve.wait_ge(s.h_hi_done, c + 1 if it is None else i * mt + (c + 1))
            nc.vector.scalar_tensor_tensor(g(h_lo), g(x), w, g(h_hi).bitcast(f32), ALU.mult,
                                           ALU.subtract).then_inc(s.h_lo_done, 1)

        def out_pe(pe, r, b0, act_tile, ready):
            for n in range(KT):
                w_wait(pe, b0 + n)
                if 8 * (r - 1) + n >= 2:
                    pe.wait_ge(s.x_new, 8 * (r - 1) + n - 1)
                for j, k in enumerate(ready["order"]):
                    if n == 0:
                        ready["wait"](pe, k)
                    ahi, alo = act_tile(k)
                    mm = mm3(B[6 + n % 2][:], w_hi[:, (b0 + n) % RING, k * P:(k + 1) * P],
                             w_lo[:, (b0 + n) % RING, k * P:(k + 1) * P], ahi, alo, j == 0, j == KT - 1)
                mm.then_inc(s.block_done, 1)

        def out_act(act, r, b0):
            for n in range(KT):
                split_act(act, b0 + n + 3)
                rnorm_act(act, r, n, False)

        def out_dve(dve, r, b0):
            for n in range(KT):
                resid_dve(dve, r, n, b0 + n)
                split_dve(dve, b0 + n + 3)
                rnorm_lo(dve, r, n)


        PB = 3

        def at(v, it, m):
            return v if it is None else it * m + v

        def up_pe(pe, L, b0, j, it):
            for q in range(2):
                g = 2 * j + q
                w_wait(pe, b0 + g, it, 2 * PB)
                G_ = 2 * FT * L + g
                if it is not None or g >= 6:
                    pe.wait_ge(s.up_free, at(G_ - 5, it, 2 * PB))
                if j == 0 and it is None:
                    for k in range(KT):
                        if q == 0:
                            pe.wait_ge(s.h_lo_done, KT * (2 * L + 1) + k + 1)
                            mm = gemm(B[g % 6], b0 + g, k, k + 1, h_hi, h_lo, k == 0, k == KT - 1)
                    if q == 1:
                        mm = gemm(B[g % 6], b0 + g, 0, KT, h_hi, h_lo, True, True)
                else:
                    mm = gemm(B[g % 6], b0 + g, 0, KT, h_hi, h_lo, True, True)
                mm.then_inc(s.block_done, 1)
                if j == 0 and it is None and q == 0:
                    stat_pe(pe, 2 * L + 1, B[7])

        def fcol(L, j, it, q, tap):
            o = PAR["fc%d" % L] + (2 * j + q) * 3 + tap
            return par[:, o:o + 1] if it is None else par[:, bass.ds(it * (6 * PB) + o, 1)]

        def up_act(act, L, b0, j, it, tail):
            for q in range(2):
                g = 2 * j + q
                if not tail:
                    w_hi_of(act, b0 + g + 3, D, it, 2 * PB)
                else:
                    split_act(act, b0 + g + 3)
                G_ = 2 * FT * L + g
                u, t = (ug, tg) if q == 0 else (uv, tv)
                act.wait_ge(s.up_free, at(G_ + 1, it, 2 * PB))
                nc.scalar.activation(t[:, j % 3, :], u[:, 0:T], ACT.Copy, scale=fcol(L, j, it, q, 0)).then_inc(s.tap0, 1)
            J = FT * L + j
            act.wait_ge(s.tap1, at(4 * J + 2, it, 4 * PB))
            nc.scalar.activation(tg[:, j % 3, :], tg[:, j % 3, :], ACT.Silu).then_inc(s.silu_f, 1)
            act.wait_ge(s.prod, at(J + 1, it, PB))
            dst = p_hi[:, j, :] if it is None else p_hi[:, bass.ds(it * PB + j, 1), :].rearrange("p o t -> p (o t)")
            nc.scalar.activation(dst, tv[:, j % 3, :], ACT.Copy).then_inc(s.prod_hi, 1)

        def up_taps(dve, L, j, it, q):
            J = FT * L + j
            u, t = (ug, tg) if q == 0 else (uv, tv)
            n = 4 * J + 2 * q
            dve.wait_ge(s.tap0, at(2 * J + q + 1, it, 2 * PB))
            nc.vector.scalar_tensor_tensor(t[:, j % 3, :], u[:, 1:T + 1], fcol(L, j, it, q, 1), t[:, j % 3, :],
                                           ALU.mult, ALU.add).then_inc(s.tap1, 1)
            dve.wait_ge(s.tap1, at(n + 1, it, 4 * PB))
            nc.vector.scalar_tensor_tensor(t[:, j % 3, :], u[:, 2:T + 2], fcol(L, j, it, q, 2), t[:, j % 3, :],
                                           ALU.mult, ALU.add).then_inc(s.tap1, 1)

        def up_evac(dve, L, b0, j, it, q):
            g = 2 * j + q
            u = ug if q == 0 else uv
            dve.wait_ge(s.block_done, at(b0 + g + 1, it, 2 * PB))
            nc.vector.tensor_tensor(u[:, 2:], B[g % 6][:], rms[:], ALU.mult).then_inc(s.up_free, 1)

        def up_plo(dve, L, j, it):
            J = FT * L + j
            dve.wait_ge(s.prod_hi, at(J + 1, it, PB))
            g = lambda a: a[:, j, :] if it is None else a[:, bass.ds(it * PB + j, 1), :].rearrange("p o t -> p (o t)")
            nc.vector.tensor_tensor(g(p_lo), tv[:, j % 3, :], g(p_hi).bitcast(f32), ALU.subtract).then_inc(s.prod_lo, 1)

        def up_dve(dve, L, b0, j, it, tail):
            J = FT * L + j
            up_evac(dve, L, b0, j, it, 0)
            if not (j == 0 and it is None):
                up_plo(dve, L, j - 1, it)
            if tail:
                split_dve(dve, b0 + 2 * j + 3)
            else:
                w_lo_of(dve, b0 + 2 * j + 3, D, it, 2 * PB)
            up_taps(dve, L, j, it, 0)
            up_evac(dve, L, b0, j, it, 1)
            if tail:
                split_dve(dve, b0 + 2 * j + 4)
            else:
                w_lo_of(dve, b0 + 2 * j + 4, D, it, 2 * PB)
            up_taps(dve, L, j, it, 1)
            dve.wait_ge(s.silu_f, at(J + 1, it, PB))
            dve.wait_ge(s.tap1, at(4 * J + 4, it, 4 * PB))
            nc.vector.tensor_tensor(tv[:, j % 3, :], tg[:, j % 3, :], tv[:, j % 3, :], ALU.mult).then_inc(s.prod, 1)

        UP_FIRST = 1 + PB
        UP_ITERS = (FT - UP_FIRST) // PB - 1

        def up(eng, fn, L, b0):
            for j in range(UP_FIRST):
                fn(eng, L, b0, j, None)
            with eng.Fori(0, UP_ITERS) as it:
                for j in range(UP_FIRST, UP_FIRST + PB):
                    fn(eng, L, b0, j, it)
            for j in range(FT - PB, FT):
                fn(eng, L, b0, j, None)

        def down_pe(pe, L, r, b0, n, it):
            b = b0 + 3 * n
            for q, kts in enumerate(DOWN):
                w_wait(pe, b + q, it, 6)
                k0 = sum(DOWN[:q])
                pe.wait_ge(s.prod_lo, FT * L + k0 + kts)
                if q == 0:
                    pe.wait_ge(s.x_new, at(8 * (r - 1) + n - 1, it, 2))
                mm = gemm(B[6 + n % 2], b + q, 0, kts, p_hi, p_lo, q == 0, q == 2, a0=k0)
                mm.then_inc(s.block_done, 1)

        def down_act(act, L, r, b0, n, it):
            b = b0 + 3 * n
            for q in range(3):
                if it is None:
                    split_act(act, b + q + 3)
                else:
                    w_hi_of(act, b + q + 3, DOWN[q] * P, it, 6)
            rnorm_act(act, r, n, r == 4, None if it is None else (it, 2))

        def down_dve(dve, L, r, b0, n, it):
            b = b0 + 3 * n
            for q in range(3):
                if q == 2:
                    resid_dve(dve, r, n, b + 2, None if it is None else (it, 2, 6))
                if it is None:
                    split_dve(dve, b + q + 3)
                else:
                    w_lo_of(dve, b + q + 3, DOWN[q] * P, it, 6)
            if r != 4:
                rnorm_lo(dve, r, n, None if it is None else (it, 2))

        def down(eng, fn, L, r, b0):
            with eng.Fori(0, KT // 2 - 1) as it:
                for n in range(2):
                    fn(eng, L, r, b0, n, it)
            for n in range(KT - 2, KT):
                fn(eng, L, r, b0, n, None)

        PLACE = {0: (0, 0), 1: (1, 0), 3: (1, 384), 2: (2, 0)}
        BASE = (0, 512, 1024)
        WID = (512, 512, 256)

        def kcols(kb):
            bank, c0 = PLACE[kb]
            return BASE[bank] + c0, T - P * kb

        def proj_pe(pe, p, kind):
            b = BQ + 3 * p + kind
            bank = B[6 if kind == 0 else 7 if kind == 1 else 7]
            w_wait(pe, b)
            if kind == 0:
                if p == 0:
                    pe.wait_ge(s.x_new, 2 * KT - 1)
                if p:
                    pe.wait_ge(s.v_lod, p)
            elif kind == 1:
                if p >= 2:
                    pe.wait_ge(s.y1_lod, p - 1)
            else:
                pe.wait_ge(s.k_f, p + 1)
            if kind == 0 and p == 0:
                for k in range(KT):
                    pe.wait_ge(s.h_lo_done, KT * 2 + k + 1)
                    mm = gemm(bank, b, k, k + 1, h_hi, h_lo, k == 0, k == KT - 1)
            else:
                mm = gemm(bank, b, 0, KT, h_hi, h_lo, True, True)
            mm.then_inc(s.block_done, 1)

        def vt_pe(pe, p):
            pe.wait_ge(s.v_f, p + 1)
            pe.wait_ge(s.q_f, p + 1)
            for c in range(NC):
                mm = nc.tensor.transpose(B[6][:, c * P:(c + 1) * P], vT[:, c * P:(c + 1) * P], cm(IDENT))
            mm.then_inc(s.vt2_mm, 1)

        def proj_dve(dve, p, kind):
            b = BQ + 3 * p + kind
            dve.wait_ge(s.block_done, b + 1)
            if kind == 0:
                if p:
                    dve.wait_ge(s.k_lod, p)
                nc.vector.scalar_tensor_tensor(pf[:], B[6][:], 0.125, rms[:], ALU.mult, ALU.mult).then_inc(s.q_f, 1)
                dve.wait_ge(s.q_hid, p + 1)
                nc.vector.tensor_tensor(q_lo[:, p % 2, :], pf[:], q_hi[:, p % 2, :].bitcast(f32), ALU.subtract).then_inc(s.q_lod, 1)
            elif kind == 1:
                dve.wait_ge(s.q_lod, p + 1)
                nc.vector.tensor_tensor(pf[:], B[7][:], rms[:], ALU.mult).then_inc(s.k_f, 1)
                dve.wait_ge(s.k_hid, p + 1)
                nc.vector.tensor_tensor(k_lo[:, p % 2, :], pf[:], k_hi[:, p % 2, :].bitcast(f32), ALU.subtract).then_inc(s.k_lod, 1)
            else:
                if p:
                    dve.wait_ge(s.vt2_mm, p)
                nc.vector.tensor_tensor(vT[:], B[7][:], rms[:], ALU.mult).then_inc(s.v_f, 1)

        def proj_act(act, p, kind):
            if kind == 0:
                act.wait_ge(s.q_f, p + 1)
                nc.scalar.activation(q_hi[:, p % 2, :], pf[:], ACT.Copy).then_inc(s.q_hid, 1)
            elif kind == 1:
                act.wait_ge(s.k_f, p + 1)
                nc.scalar.activation(k_hi[:, p % 2, :], pf[:], ACT.Copy).then_inc(s.k_hid, 1)

        def vpads(t, p, e):
            return t[:, p % 2, :, e, 64 * e:64 * e + 64]

        def vt_act(act, p):
            act.wait_ge(s.vt2_mm, p + 1)
            for e in range(2):
                nc.scalar.activation(vpads(v_hi, p, e), B[6][:].rearrange("p (c d) -> p c d", c=NC)[:, :, 64 * e:64 * e + 64],
                                     ACT.Copy).then_inc(s.v_hid, 1)

        def vt_dve(dve, p):
            for e in range(2):
                dve.wait_ge(s.v_hid, 2 * p + 2)
                mm = nc.vector.tensor_tensor(vpads(v_lo, p, e),
                                             B[6][:].rearrange("p (c d) -> p c d", c=NC)[:, :, 64 * e:64 * e + 64],
                                             vpads(v_hi, p, e).bitcast(f32), ALU.subtract)
            mm.then_inc(s.v_lod, 1)

        def z_pe(pe, p, e):
            u = 2 * p + e
            rows = slice(64 * e, 64 * e + 64)
            pe.wait_ge(s.k_lod, p + 1)
            if u >= 2:
                pe.wait_ge(s.att_done, 3 * (u - 1))
            if u == 0:
                pe.wait_ge(s.consts_r, 4)
            for bank, kbs in enumerate(((0,), (1, 3), (2,))):
                first = True
                for kb in kbs:
                    c0, w = PLACE[kb][1], T - P * kb
                    out = B[3 * e + bank]
                    kk, qq = slice(P * kb, P * kb + P), slice(P * kb, T)
                    for a, (kt, qt) in enumerate(((k_lo, q_hi), (k_hi, q_lo), (k_hi, q_hi))):
                        nc.tensor.matmul(out[:, c0:c0 + w], kt[rows, p % 2, kk], qt[rows, p % 2, qq],
                                         start=first, stop=False, skip_group_check=True)
                        first = False
                    mm = nc.tensor.matmul(out[:, c0:c0 + P], identr[:], negm[:], start=False, stop=(kb == kbs[-1]),
                                          skip_group_check=True)
                mm.then_inc(s.z_mm, 1)

        def cum_pe(pe, p, e):
            u = 2 * p + e
            pe.wait_ge(s.sp_lod, 3 * u + 3)
            for bank, kbs in enumerate(((0,), (1, 3), (2,))):
                for kb in kbs:
                    out, c0 = B[3 * e + bank], PLACE[kb][1]
                    for kb2 in range(kb, NC):
                        o, w = kcols(kb2)
                        d = c0 + P * (kb2 - kb)
                        for src in (s_lo, s_hi):
                            mm = nc.tensor.matmul(out[:, d:d + w], (ntri if kb2 == kb else nones)[:], src[:, e, o:o + w],
                                                  start=False, stop=False, skip_group_check=True)
                mm.then_inc(s.cum_mm, 1)

        def sp_act(act, p, e):
            u = 2 * p + e
            for bank in range(3):
                n = 3 * u + bank
                o, w = BASE[bank], WID[bank]
                act.wait_ge(s.z_mm, n + 1)
                if u >= 2:
                    act.wait_ge(s.att_lod, 3 * (u - 1))
                nc.scalar.activation(t_[:, e, o:o + w], B[3 * e + bank][:, 0:w], ACT.Abs).then_inc(s.za_done, 1)
            for bank in range(3):
                n = 3 * u + bank
                o, w = BASE[bank], WID[bank]
                act.wait_ge(s.za_done, n + 1)
                nc.scalar.activation(t_[:, e, o:o + w], t_[:, e, o:o + w], ACT.Exp, scale=-1.0).then_inc(s.ze_done, 1)
            for bank in range(3):
                n = 3 * u + bank
                o, w = BASE[bank], WID[bank]
                act.wait_ge(s.ze_done, n + 1)
                nc.scalar.activation(t_[:, e, o:o + w], t_[:, e, o:o + w], ACT.Ln, bias=1.0).then_inc(s.zl_done, 1)

        def sp2_dve(dve, p, e):
            u = 2 * p + e
            for bank in range(3):
                n = 3 * u + bank
                o, w = BASE[bank], WID[bank]
                dve.wait_ge(s.zl_done, n + 1)
                nc.vector.scalar_tensor_tensor(t_[:, e, o:o + w], B[3 * e + bank][:, 0:w], 0.0, t_[:, e, o:o + w],
                                               ALU.max, ALU.add).then_inc(s.sp_done, 1)

        def split_s_act(act, p, e, src_sem, dst_sem):
            u = 2 * p + e
            for bank in range(3):
                n = 3 * u + bank
                o, w = BASE[bank], WID[bank]
                act.wait_ge(src_sem, n + 1)
                nc.scalar.activation(s_hi[:, e, o:o + w], t_[:, e, o:o + w], ACT.Copy).then_inc(dst_sem, 1)

        def split_s_dve(dve, p, e, hi_sem, lo_sem):
            u = 2 * p + e
            for bank in range(3):
                n = 3 * u + bank
                o, w = BASE[bank], WID[bank]
                dve.wait_ge(hi_sem, n + 1)
                nc.vector.tensor_tensor(s_lo[:, e, o:o + w], t_[:, e, o:o + w], s_hi[:, e, o:o + w].bitcast(f32),
                                        ALU.subtract).then_inc(lo_sem, 1)

        def att_act(act, p, e):
            u = 2 * p + e
            for bank in range(3):
                o, w = BASE[bank], WID[bank]
                act.wait_ge(s.cum_mm, 3 * u + 3)
                nc.scalar.activation(t_[:, e, o:o + w], B[3 * e + bank][:, 0:w], ACT.Exp).then_inc(s.att_done, 1)

        def av_pe(pe, p):
            pe.wait_ge(s.v_lod, p + 1)
            pe.wait_ge(s.v_f, min(p + 1, PAIRS - 1) + 0)
            first = True
            for e in range(2):
                pe.wait_ge(s.att_lod, 3 * (2 * p + e) + 3)
                for kb in range(NC):
                    o, w = kcols(kb)
                    for vt, at_ in ((v_lo, s_hi), (v_hi, s_lo), (v_hi, s_hi)):
                        mm = nc.tensor.matmul(B[7][:, P * kb:T], vt[:, p % 2, kb, e, :], at_[:, e, o:o + w], start=first,
                                              stop=(e == 1 and kb == NC - 1 and at_ is s_hi and vt is v_hi),
                                              skip_group_check=True)
                        first = False
            mm.then_inc(s.av_mm, 1)

        def y1_act(act, p):
            act.wait_ge(s.av_mm, p + 1)
            nc.scalar.activation(y1_hi[:, p, :], B[7][:], ACT.Copy).then_inc(s.y1_hid, 1)

        def y1_dve(dve, p):
            dve.wait_ge(s.y1_hid, p + 1)
            nc.vector.tensor_tensor(y1_lo[:, p, :], B[7][:], y1_hi[:, p, :].bitcast(f32), ALU.subtract).then_inc(s.y1_lod, 1)

        def t_pe(pe):
            for kind in range(3):
                proj_pe(pe, 0, kind)
                if kind == 0:
                    stat_pe(pe, 2, B[5])
            vt_pe(pe, 0)
            for p in range(PAIRS):
                nxt = p + 1 < PAIRS
                z_pe(pe, p, 0)
                if nxt:
                    proj_pe(pe, p + 1, 0)
                z_pe(pe, p, 1)
                if p:
                    av_pe_wait(pe, p - 1)
                if nxt:
                    proj_pe(pe, p + 1, 1)
                cum_pe(pe, p, 0)
                if nxt:
                    proj_pe(pe, p + 1, 2)
                cum_pe(pe, p, 1)
                if nxt:
                    vt_pe(pe, p + 1)
            av_pe_wait(pe, PAIRS - 1)

        def av_pe_wait(pe, p):
            av_pe(pe, p)

        def t_act(act):
            for dst, i, sc in ((ntri, NTRI, 1.0), (nones, ONES, -1.0), (negm, NEG, 1.0), (identr, IDENT, 1.0)):
                nc.scalar.activation(dst[:], cm(i), ACT.Copy, scale=sc).then_inc(s.consts_r, 1)
            stat_act(act, 2, B[5])
            for kind in range(3):
                split_act(act, BQ + kind + 3)
                proj_act(act, 0, kind)
            vt_act(act, 0)
            for p in range(PAIRS):
                nxt = p + 1 < PAIRS
                if p:
                    split_s_act(act, p - 1, 1, s.att_done, s.att_hid)
                sp_act(act, p, 0)
                if nxt:
                    split_act(act, BQ + 3 * (p + 1) + 3)
                    proj_act(act, p + 1, 0)
                if p:
                    y1_act(act, p - 1)
                split_s_act(act, p, 0, s.sp_done, s.sp_hid)
                sp_act(act, p, 1)
                if nxt:
                    split_act(act, BQ + 3 * (p + 1) + 4)
                    proj_act(act, p + 1, 1)
                split_s_act(act, p, 1, s.sp_done, s.sp_hid)
                att_act(act, p, 0)
                split_s_act(act, p, 0, s.att_done, s.att_hid)
                if nxt:
                    split_act(act, BQ + 3 * (p + 1) + 5)
                    vt_act(act, p + 1)
                att_act(act, p, 1)
            split_s_act(act, PAIRS - 1, 1, s.att_done, s.att_hid)
            y1_act(act, PAIRS - 1)

        def t_dve(dve):
            dve.wait_ge(s.rms_done, 3)
            for kind in range(3):
                proj_dve(dve, 0, kind)
                split_dve(dve, BQ + kind + 3)
            vt_dve(dve, 0)
            for p in range(PAIRS):
                nxt = p + 1 < PAIRS
                if p:
                    split_s_dve(dve, p - 1, 1, s.att_hid, s.att_lod)
                sp2_dve(dve, p, 0)
                if nxt:
                    proj_dve(dve, p + 1, 0)
                    split_dve(dve, BQ + 3 * (p + 1) + 3)
                if p:
                    y1_dve(dve, p - 1)
                split_s_dve(dve, p, 0, s.sp_hid, s.sp_lod)
                sp2_dve(dve, p, 1)
                if nxt:
                    proj_dve(dve, p + 1, 1)
                    split_dve(dve, BQ + 3 * (p + 1) + 4)
                split_s_dve(dve, p, 1, s.sp_hid, s.sp_lod)
                split_s_dve(dve, p, 0, s.att_hid, s.att_lod)
                if nxt:
                    proj_dve(dve, p + 1, 2)
                    split_dve(dve, BQ + 3 * (p + 1) + 5)
                    vt_dve(dve, p + 1)
            split_s_dve(dve, PAIRS - 1, 1, s.att_hid, s.att_lod)
            y1_dve(dve, PAIRS - 1)

        block = ctx.enter_context(nc.Block())

        @block.sync
        def _(sp):
            sp.dma_start(x[:, 0:4, :], xT[:, 0:4, :]).then_inc(s.x_in0, 16)
            w_load(sp, w_ab, 0, 64)
            sp.dma_start(par[:], par_d).then_inc(s.par_in, 16)
            sp.dma_start(x[:, 4:8, :], xT[:, 4:8, :]).then_inc(s.x_in1, 16)
            for b in range(1, NB0):
                w_load(sp, w_in0[b - 1], b, D)
                if b == 2:
                    sp.dma_start(const[:], const_d).then_inc(s.const_in, 16)

            def out_loads(dram, b0):
                for n in range(KT):
                    w_load(sp, dram[n], b0 + n, D)

            def up_loads(dram, b0):
                for g in range(2):
                    w_load(sp, dram[g], b0 + g, D)
                with sp.Fori(0, (2 * FT - 2) // RING) as i:
                    for j in range(RING):
                        w_load(sp, dram[bass.ds(i * RING + (2 + j), 1)].rearrange("o p n -> (o p) n"), b0 + 2 + j, D, i, RING)

            def down_loads(dram, b0):
                with sp.Fori(0, KT) as i:
                    for q, kts in enumerate(DOWN):
                        k0 = sum(DOWN[:q]) * P
                        w_load(sp, dram[bass.ds(i, 1), :, k0:k0 + kts * P].rearrange("o p n -> (o p) n"), b0 + q, kts * P, i, 3)

            for j in range(NBO0):
                w_load(sp, w_out0[j], BO0 + j, D // 2)
            up_loads(w_up0, BU0)
            down_loads(w_dn0, BD0)
            for b in range(NBQ):
                w_load(sp, w_qkv[b], BQ + b, D)
            out_loads(w_out1, BO1)
            up_loads(w_up1, BU1)
            down_loads(w_dn1, BD1)
            for k in range(KT):
                sp.wait_ge(s.out_f, k + 1)
                sp.dma_start(outT[:, k, :], x[:, k, :]).then_inc(s.out_w, 16)
            sp.wait_ge(s.out_w, 16 * KT)


        @block.gpsimd
        def _(pool):
            nc.gpsimd.memset(eps[:, 0:1], 1e-6)
            nc.gpsimd.memset(eps[:, 1:2], 1e-5).then_inc(s.ones_set, 1)
            a_pool(pool)
            norm_pool(pool, 1)
            norm_pool(pool, 2)
            norm_pool(pool, 3)
            norm_pool(pool, 4)

        @block.scalar
        def _(act):
            a_act(act)
            out0_act(act)
            stat_act(act, 1, B[7])
            up(act, lambda e, L, b0, j, it: up_act(e, L, b0, j, it, it is None), 0, BU0)
            down(act, down_act, 0, 2, BD0)
            t_act(act)
            out_act(act, 3, BO1)
            stat_act(act, 3, B[7])
            up(act, lambda e, L, b0, j, it: up_act(e, L, b0, j, it, it is None), 1, BU1)
            down(act, down_act, 1, 4, BD1)
            stat_act(act, 4, B[7])

        @block.vector
        def _(dve):
            a_dve(dve)
            out0_dve(dve)

            def ffn_up(L, b0):
                dve.wait_ge(s.rms_done, 2 * L + 2)
                nc.vector.memset(ug[:, 0:2], 0.0).then_inc(s.halo_f, 1)
                nc.vector.memset(uv[:, 0:2], 0.0).then_inc(s.halo_f, 1)
                dve.wait_ge(s.halo_f, 2 * L + 2)
                up(dve, lambda e, L, b0, j, it: up_dve(e, L, b0, j, it, it is None), L, b0)
                up_plo(dve, L, FT - 1, None)
            ffn_up(0, BU0)
            down(dve, down_dve, 0, 2, BD0)
            for t in (v_hi, v_lo):
                nc.vector.memset(t[:].bitcast(f32), 0.0).then_inc(s.vp_zero, 1)
            dve.wait_ge(s.vp_zero, 2)
            t_dve(dve)
            out_dve(dve, 3, BO1)
            ffn_up(1, BU1)
            down(dve, down_dve, 1, 4, BD1)
            dve.wait_ge(s.rms_done, 5)
            for k in range(KT):
                nc.vector.scalar_tensor_tensor(x[:, k, :], x[:, k, :], col("norm", 4 * KT + k), rms[:], ALU.mult,
                                               ALU.mult).then_inc(s.out_f, 1)

        @block.tensor
        def _(pe):
            a_pe(pe)
            out0_pe(pe)
            up(pe, up_pe, 0, BU0)
            down(pe, down_pe, 0, 2, BD0)
            t_pe(pe)
            out_pe(pe, 3, BO1, lambda k: (y1_hi[:, k, :], y1_lo[:, k, :]),
                   {"order": tuple(range(KT)), "wait": lambda pe, k: pe.wait_ge(s.y1_lod, k + 1)})
            up(pe, up_pe, 1, BU1)
            down(pe, down_pe, 1, 4, BD1)
            stat_pe(pe, 4, B[7])


def _blocks(np, w, cols):
    k = w.shape[0] // P
    a = w.reshape(k, P, w.shape[1] // P, P) if w.shape[1] % P == 0 else None
    return np.ascontiguousarray(a[:, :, cols, :].transpose(2, 1, 0, 3).reshape(len(cols), P, k * P))


def _consts(np):
    i = np.arange(P)
    row, c = i[:, None], i[None, :]
    m = [row == c, row <= c, row > c, np.ones((P, P))]
    for l in range(LEVELS):
        b = 1 << l
        m.append((row // (2 * b) == c // (2 * b)) & ((row // b) % 2 == 0) & ((c // b) % 2 == 1))
    m.append(-1.0 * (row >= c))
    m.append(-(2.0 ** 100) * (row >= c))
    return np.ascontiguousarray(np.stack([np.asarray(a, np.float32) for a in m]).transpose(1, 0, 2))


def _arrays(np, inputs):
    g = {k: np.asarray(v) for k, v in inputs.items()}
    tile = lambda v: v.reshape(-1, P).T
    w0 = g["w_in0"][0]
    c = CA
    order = [t for i in range(CA) for t in (c + i, i)]
    for h in range(NH):
        order += [2 * c + NH + h, 2 * c + h, 2 * c + 2 * NH + h]
    order += [2 * c + 3 * NH + h for h in range(NH)]
    main = w0[:, :24 * P]
    w_ab = np.ascontiguousarray(w0[:, 24 * P:].reshape(KT, P, 8).transpose(1, 0, 2).reshape(P, 64))
    pairs = [t for j in range(FT) for t in (j, FT + j)]
    qkv = [t for p in range(PAIRS) for t in (p, PAIRS + p, 2 * PAIRS + p)]
    par = [tile(g["mix0_norm"][0]), tile(g["ffn_norm"][0]), tile(g["mix1_norm"][0]), tile(g["ffn_norm"][1]),
           tile(g["final_norm"]), tile(g["a_dw_b"][0]), tile(g["a_ln_w"][0]), tile(g["a_ln_b"][0]),
           tile(g["gdn_onorm_w"][0]),
           g["gdn_conv_w"][0].reshape(4, 12, P).transpose(2, 1, 0).reshape(P, 48),
           g["a_dw_w"][0].reshape(C31, CA, P).transpose(2, 1, 0).reshape(P, CA * C31)]
    for L in range(2):
        par.append(g["ffn_conv_w"][L].reshape(3, 2 * FT, P)[:, pairs, :].transpose(2, 1, 0).reshape(P, 6 * FT))
    par += [np.broadcast_to(g[n][0][None, :], (P, NH)) for n in ("gdn_dt_bias", "gdn_a_log")]
    down = lambda w: np.ascontiguousarray(w.reshape(FT, P, KT, P).transpose(2, 1, 0, 3).reshape(KT, P, FT * P))
    return {
        "xT": np.ascontiguousarray(g["x"][0].T.reshape(KT, P, T).transpose(1, 0, 2)),
        "w_ab": w_ab,
        "w_in0": _blocks(np, main, order),
        "w_out0": np.concatenate([_blocks(np, g["w_out0"][0][r], list(range(KT))) for r in (slice(CA * P, D), slice(0, CA * P))]),
        "w_up0": _blocks(np, g["w_up"][0], pairs),
        "w_dn0": down(g["w_down"][0]),
        "w_qkv": _blocks(np, g["w_qkv1"][0], qkv),
        "w_out1": _blocks(np, g["w_out1"][0], list(range(KT))),
        "w_up1": _blocks(np, g["w_up"][1], pairs),
        "w_dn1": down(g["w_down"][1]),
        "par": np.ascontiguousarray(np.concatenate(par, axis=1)),
        "const": _consts(np),
    }


def kernel(**inputs):
    import numpy as np
    import concourse.bacc as bacc
    from concourse import mybir as mb
    from concourse.bass_utils import run_bass_kernel_spmd
    arrays = {"in_" + n: a for n, a in _arrays(np, inputs).items()}
    nc = bacc.Bacc("TRN2", target_bir_lowering=False, num_devices=1)
    args = [nc.dram_tensor(n, a.shape, mb.dt.from_np(a.dtype), kind="ExternalInput").ap() for n, a in arrays.items()]
    args.append(nc.dram_tensor("outT", (P, KT, T), mb.dt.float32, kind="ExternalOutput").ap())
    trunk(nc, *args)
    r = run_bass_kernel_spmd(nc, [arrays], core_ids=[0])
    out = r.results[0]["outT"]
    return np.ascontiguousarray(out.transpose(1, 0, 2).reshape(D, T).T)[None]
```

```python
import concourse.bass as bass
from concourse import mybir
from contextlib import ExitStack
from collections import namedtuple

P = 128
T = 512
D = 1024
KT = D // P
FF = 2816
FT = FF // P
DOWN = (8, 8, 6)
C31 = 31
CA = 4
NH = 4
NC = T // P
LEVELS = 7
PAIRS = 8
NB0, NBO0, NBO1, NBU, NBD, NBQ = 25, 16, 8, 2 * FT, 24, 24
RING = 3

PAR = {}
_n = 0
for _name, _w in (("norm", 5 * KT), ("dwb", CA), ("lnw", CA), ("lnb", CA), ("onorm", 1), ("c4", 12 * 4),
                  ("c31", CA * C31), ("fc0", 2 * FT * 3), ("fc1", 2 * FT * 3), ("dtb", NH), ("alog", NH)):
    PAR[_name] = _n
    _n += _w
NPAR = _n
IDENT, UPPER, AFTER, ONES, LEV0, NTRI, NEG = 0, 1, 2, 3, 4, 11, 12
NCONST = 13


def trunk(nc, xT, w_ab, w_in0, w_out0, w_up0, w_dn0, w_qkv, w_out1, w_up1, w_dn1, par_d, const_d, outT):
    f32, f32r = mybir.dt.float32, mybir.dt.float32r
    ACT, ALU = mybir.ActivationFunctionType, mybir.AluOpType
    ctx = ExitStack()
    with ctx:
        def sb(name, shape, dt=f32, c=ctx):
            return c.enter_context(nc.sbuf_tensor(name, shape, dt))

        def sem(name):
            return ctx.enter_context(nc.semaphore(name))

        x = sb("x", [P, KT, T])
        h_hi, h_lo = sb("h_hi", [P, KT, T], f32r), sb("h_lo", [P, KT, T], f32r)
        stage = sb("stage", [P, RING, D])
        w_hi, w_lo = sb("w_hi", [P, RING, D], f32r), sb("w_lo", [P, RING, D], f32r)
        rms = sb("rms", [P, T])
        ssq = sb("ssq", [P, T])
        sq2 = sb("sq2", [P, 2, T])
        par = sb("par", [P, NPAR])
        const = sb("const", [P, NCONST, P])
        eps = sb("eps", [P, 4])
        za = ExitStack()
        yb_hi, yb_lo = sb("yb_hi", [P, NH, T], f32r, za), sb("yb_lo", [P, NH, T], f32r, za)
        ya_hi = sb("ya_hi", [P, CA, T], f32r, za)
        with ExitStack() as over:
            ya_lo = sb("ya_lo", [P, CA, T], f32r, over)
        hb = sb("hb", [P, CA, T + C31 - 1], f32, za)
        tc = sb("tc", [P, CA, T], f32, za)
        sig = sb("sig", [P, T], f32, za)
        cb = sb("cb", [P, T + 3], f32, za)
        sk, sq, sv = (sb(n, [P, T], f32, za) for n in ("sk", "sq", "sv"))
        sqb = sb("sqb", [P, 2, T], f32, za)
        rkq = sb("rkq", [P, 2, T], f32, za)
        kn, qn = sb("kn", [P, NC, P], f32, za), sb("qn", [P, NC, P], f32, za)
        gU, eDn, qd = (sb(n, [P, NC, P], f32, za) for n in ("gU", "eDn", "qd"))
        gU_hi, gU_lo = (sb(n, [P, NC, P], f32r, za) for n in ("gU_hi", "gU_lo"))
        after_r, ones_r = (sb(n, [P, P], f32r, za) for n in ("after_r", "ones_r"))
        qkd = sb("qkd", [P, 2, NC, P], f32, za)
        X, Y, ktail, kbg, vb, nWT = (sb(n, [P, NC, P], f32, za) for n in ("X", "Y", "ktail", "kbg", "vb", "nWT"))
        T2 = sb("T2", [P, NC, P], f32, za)
        vnew, S = sb("vnew", [P, P], f32, za), sb("S", [P, P], f32, za)
        oc, ro = sb("oc", [P, NH, T], f32, za), sb("ro", [P, T], f32, za)
        ab = sb("ab", [8, T], f32, za)
        sm = sb("sm", [P, 12, NC * NH], f32, za)
        za.close()
        zf = ExitStack()
        p_hi, p_lo = sb("p_hi", [P, FT, T], f32r, zf), sb("p_lo", [P, FT, T], f32r, zf)
        ug, uv = sb("ug", [P, T + 2], f32, zf), sb("uv", [P, T + 2], f32, zf)
        tg, tv = sb("tg", [P, 3, T], f32, zf), sb("tv", [P, 3, T], f32, zf)
        zf.close()
        zt = ExitStack()
        y1_hi, y1_lo = sb("y1_hi", [P, PAIRS, T], f32r, zt), sb("y1_lo", [P, PAIRS, T], f32r, zt)
        qs, ks = sb("qs", [P, 2, 2, T], f32r, zt), sb("ks", [P, 2, 2, T], f32r, zt)
        k_lo = sb("k_lo", [P, 2, T], f32r, zt)
        v_hl = sb("v_hl", [P, 2, NC, 2, P], f32r, zt)
        yt, yf = sb("yt", [P, 2, T], f32, zt), sb("yf", [P, T], f32, zt)
        pf = sb("pf", [P, T], f32, zt)
        vT = sb("vT", [P, T], f32, zt)
        AW = 1280
        t_ = sb("t_", [P, 2, AW], f32, zt)
        s_hi, s_lo = sb("s_hi", [P, 2, AW], f32r, zt), sb("s_lo", [P, 2, AW], f32r, zt)
        ntri, nones, identr = (sb(n, [P, P], f32r, zt) for n in ("ntri", "nones", "identr"))
        negm = sb("negm", [P, 2 * P], f32r, zt)
        zt.close()

        B = [ctx.enter_context(nc.psum_tensor(f"bank{i}", [P, T], f32)) for i in range(8)]

        names = (
            "norms_in par_in const_in out_w w_split_hi w_split_lo block_done x_new h_hi_done h_lo_done "
            "sq_done ssq_done stat_mm rms_ln rms_done ones_set halo_set a_free ab_t sg_beta sg_xa sg_abs "
            "sg_e sg_l sg_sp sg_ea sg_g sg_bg cols_mm cols_exp sig_done hb_done cf0 cf_tap c0_done ctap "
            "silu_done sqh_done kqss_mm kq_ln kq_r kn_done qn_done kt_mm vt_mm ktail_done kbg_done vb_done "
            "kk_mm qk_mm gu_done dn_mm dt_mm gb_mm edt_done egb_done a1_done a2_done qkd_done qkd_masked "
            "qd_done t_mm t2_done xt_mm x_done ym_mm y_done wt_mm wt_done v_mm v_done o_mm s_mm s_done "
            "oc_done osq_done oss_mm o_ln o_r on_done sz_done yb_f yb_hid yb_lod mu_mm xc_done csq_done "
            "var_mm c_ln c_r cn_done ya_f ya_hid ya_lod up_free tap0 tap1 silu_f prod prod_hi prod_lo halo_f "
            "consts_r q_f q_hid q_lod k_f k_hid k_lod v_f vt2_mm v_hid v_lod z_mm za_done ze_done zl_done "
            "sp_done sp_hid sp_lod cum_mm att_done att_hid att_lod av_mm y1_hid y1_lod y_sum yt_done out_f gu_f "
            "afr_done tsum_done qsum_done x_w k_twice "
        )
        s = namedtuple("Sems", names)(*(sem(n) for n in names.split()))
        x_in = [sem(f"x_in{k}") for k in range(KT)]
        w_in = [sem(f"w_in{i}") for i in range(RING)]

        def col(name, i=0):
            return par[:, PAR[name] + i:PAR[name] + i + 1]

        def cm(i):
            return const[:, i, :]

        def bc(ap):
            return ap.unsqueeze(1).to_broadcast([P, NC, P])

        def flat(a):
            return a[:].rearrange("p c t -> p (c t)")

        def r3(bank):
            return bank[:].rearrange("p (c t) -> p c t", c=NC)

        def tok(i, h):
            return sm[:, i, :].rearrange("p (c h) -> p c h", h=NH)[:, :, h:h + 1].to_broadcast([P, NC, P])

        def w_load(sp, dram, b, n, r=None, m=0):
            if r is None and b >= RING:
                sp.wait_ge(s.w_split_lo, b - RING + 1)
            if r is not None:
                sp.wait_ge(s.w_split_lo, r * m + (b - RING + 1))
            sp.dma_start(stage[:, b % RING, 0:n], dram).then_inc(w_in[b % RING], 16)

        def w_hi_of(act, b, n, r=None, m=0):
            if r is None:
                act.wait_ge(w_in[b % RING], 16 * (b // RING + 1))
                if b >= RING:
                    act.wait_ge(s.block_done, b - RING + 1)
            else:
                act.wait_ge(w_in[b % RING], r * (16 * m // RING) + 16 * (b // RING + 1))
                act.wait_ge(s.block_done, r * m + (b - RING + 1))
            nc.scalar.activation(w_hi[:, b % RING, 0:n], stage[:, b % RING, 0:n], ACT.Copy).then_inc(s.w_split_hi, 1)

        def w_lo_of(dve, b, n, r=None, m=0):
            dve.wait_ge(s.w_split_hi, (b + 1) if r is None else r * m + (b + 1))
            nc.vector.tensor_tensor(w_lo[:, b % RING, 0:n], stage[:, b % RING, 0:n],
                                    w_hi[:, b % RING, 0:n].bitcast(f32), ALU.subtract).then_inc(s.w_split_lo, 1)

        def mm3(out, whi, wlo, ahi, alo, start, stop):
            nc.tensor.matmul(out, wlo, ahi, start=start, stop=False, skip_group_check=True)
            nc.tensor.matmul(out, whi, alo, start=False, stop=False, skip_group_check=True)
            return nc.tensor.matmul(out, whi, ahi, start=False, stop=stop, skip_group_check=True)

        def w_wait(pe, b, r=None, m=0):
            pe.wait_ge(s.w_split_lo, (b + 1) if r is None else r * m + (b + 1))

        def gemm(bank, b, k0, k1, ahi, alo, first, last, mcols=P, a0=0):
            for k in range(k0, k1):
                mm = mm3(bank[0:mcols, :], w_hi[:, b % RING, k * mcols:(k + 1) * mcols],
                         w_lo[:, b % RING, k * mcols:(k + 1) * mcols], ahi[:, a0 + k, :], alo[:, a0 + k, :],
                         first and k == k0, last and k == k1 - 1)
            return mm

        def norm_lo(dve, n, k):
            dve.wait_ge(s.h_hi_done, KT * n + k + 1)
            nc.vector.scalar_tensor_tensor(h_lo[:, k, :], x[:, k, :], col("norm", KT * n + k), h_hi[:, k, :].bitcast(f32),
                                           ALU.mult, ALU.subtract).then_inc(s.h_lo_done, 1)

        def norm_pool(pool, n, tiles=KT):
            for k in range(tiles):
                c = KT * n + k
                pool.wait_ge(s.sq_done, c + 1)
                if k == 0:
                    if n:
                        pool.wait_ge(s.stat_mm, n)
                    nc.gpsimd.tensor_scalar(ssq[:], sq2[:, 0, :], 1.0, None, ALU.mult).then_inc(s.ssq_done, 1)
                else:
                    pool.wait_ge(s.ssq_done, c)
                    nc.gpsimd.tensor_tensor(ssq[:], ssq[:], sq2[:, k % 2, :], ALU.add).then_inc(s.ssq_done, 1)

        def stat_pe(pe, n, bank):
            pe.wait_ge(s.ssq_done, KT * (n + 1))
            nc.tensor.matmul(bank[:], cm(ONES), ssq[:], start=True, stop=True).then_inc(s.stat_mm, 1)

        def last_stat_pe(pe, n, bank):
            pe.wait_ge(s.ssq_done, KT * n + KT - 1)
            nc.tensor.matmul(bank[:], cm(ONES), ssq[:], start=True, stop=False)
            pe.wait_ge(s.sq_done, KT * (n + 1))
            nc.tensor.matmul(bank[:], cm(ONES), sq2[:, (KT - 1) % 2, :], start=False, stop=True).then_inc(s.stat_mm, 1)

        def stat_act(act, n, bank):
            if n < 4:
                act.preload_act_table_set("natural_log_exp_and_others")
            act.wait_ge(s.stat_mm, n + 1)
            nc.scalar.activation(rms[:], bank[:], ACT.Ln, bias=eps[:, 0:1], scale=1.0 / D).then_inc(s.rms_ln, 1)
            act.wait_ge(s.rms_ln, n + 1)
            nc.scalar.activation(rms[:], rms[:], ACT.Exp, scale=-0.5).then_inc(s.rms_done, 1)

        ORDER = [("ab", 0)] + [(c, i) for i in range(CA) for c in ("g", "v")] + \
                [(c, h) for h in range(NH) for c in ("k", "q", "u")] + [("z", h) for h in range(NH)]
        n_of = lambda g: 64 if g == 0 else D

        def nblk(b):
            if b == 0:
                return 64
            for size, kind in ((NB0, 0), (NBO0, 2), (NBU, 0), (NBD, 1), (NBQ + NBO1, 0), (NBU, 0), (NBD, 1)):
                if b < size:
                    return DOWN[b % 3] * P if kind == 1 else D // 2 if kind == 2 else D
                b -= size
            return 0
        BO0 = NB0
        BU0 = BO0 + NBO0
        BD0 = BU0 + NBU
        BQ = BD0 + NBD
        BO1 = BQ + NBQ
        BU1 = BO1 + NBO1
        BD1 = BU1 + NBU
        BEND = BD1 + NBD

        TAPS = CA * (C31 - 1)
        LEAD = 12
        even = [(i, j) for i in (0, 2) for j in range(1, C31)]
        odd = [(i, j) for i in (1, 3) for j in range(1, C31)]
        TAP = even[:LEAD]
        for a_, b_ in zip(odd, even[LEAD:]):
            TAP += [a_, b_]
        TAP += odd[len(even) - LEAD:]
        EARLY = (0, 0, 0, 0, 3, 4, 4, 5, 4, 4, 5, 1)
        TAPS0, TAPS1, TAPS2, TAPS3, TAPS4, TAPS5, TAPS6 = 6, 3, 3, 1, 2, 0, 1
        tap_next = [0]

        def taps(dve, n):
            for _ in range(min(n, TAPS - tap_next[0])):
                i, j = TAP[tap_next[0]]
                if j == 1:
                    dve.wait_ge(s.cf0, i + 1)
                else:
                    dve.wait_ge(s.cf_tap, TAP.index((i, j - 1)) + 1)
                nc.vector.scalar_tensor_tensor(tc[:, i, :], hb[:, i, j:j + T], col("c31", i * C31 + j), tc[:, i, :],
                                               ALU.mult, ALU.add).then_inc(s.cf_tap, 1)
                tap_next[0] += 1

        def group_bank(g):
            return B[g % 3 if g < 12 else g % 2]

        def post_evac(dve, g):
            kind, i = ORDER[g]
            bank = group_bank(g)
            dve.wait_ge(s.block_done, g + 1)
            if kind == "ab":
                dve.wait_ge(s.rms_done, 1)
                nc.vector.tensor_tensor(ab[:], bank[0:8, :], rms[0:8, :], ALU.mult).then_inc(s.a_free, 1)
            elif kind == "g":
                if i:
                    dve.wait_ge(s.hb_done, i)
                nc.vector.tensor_tensor(sig[:], bank[:], rms[:], ALU.mult).then_inc(s.a_free, 1)
            elif kind == "v":
                nc.vector.tensor_tensor(hb[:, i, C31 - 1:], bank[:], rms[:], ALU.mult).then_inc(s.a_free, 1)
            elif kind == "z":
                if i:
                    dve.wait_ge(s.yb_f, i)
                nc.vector.tensor_tensor(sig[:], bank[:], rms[:], ALU.mult).then_inc(s.a_free, 1)
            else:
                m = 3 * i + "kqu".index(kind)
                if m:
                    dve.wait_ge(s.ctap, 3 * m)
                nc.vector.tensor_tensor(cb[:, 3:], bank[:], rms[:], ALU.mult).then_inc(s.a_free, 1)

        def glu(dve, g):
            i = ORDER[g][1]
            dve.wait_ge(s.a_free, g + 1)
            dve.wait_ge(s.sig_done, i + 1)
            nc.vector.tensor_tensor(hb[:, i, C31 - 1:], hb[:, i, C31 - 1:], sig[:], ALU.mult).then_inc(s.hb_done, 1)

        def short_tap(dve, g, j):
            kind, i = ORDER[g]
            if kind not in "kqu":
                taps(dve, 1)
                return
            m = 3 * i + "kqu".index(kind)
            dst = (sk, sq, sv)["kqu".index(kind)]
            tile = {"k": NH, "q": 0, "u": 2 * NH}[kind] + i
            if j == 1:
                dve.wait_ge(s.c0_done, m + 1)
            else:
                dve.wait_ge(s.ctap, 3 * m + j - 1)
            nc.vector.scalar_tensor_tensor(dst[:], cb[:, j:j + T], col("c4", tile * 4 + j), dst[:],
                                           ALU.mult, ALU.add).then_inc(s.ctap, 1)

        def post_act0(act, g):
            kind, i = ORDER[g]
            if kind == "g":
                act.wait_ge(s.a_free, g + 1)
                nc.scalar.activation(sig[:], sig[:], ACT.Sigmoid).then_inc(s.sig_done, 1)
            elif kind == "v":
                act.wait_ge(s.hb_done, i + 1)
                nc.scalar.activation(tc[:, i, :], hb[:, i, 0:T], ACT.Identity, scale=col("c31", i * C31),
                                     bias=col("dwb", i)).then_inc(s.cf0, 1)
            elif kind in "kqu":
                m = 3 * i + "kqu".index(kind)
                dst = (sk, sq, sv)["kqu".index(kind)]
                tile = {"k": NH, "q": 0, "u": 2 * NH}[kind] + i
                act.wait_ge(s.a_free, g + 1)
                if i:
                    act.wait_ge((s.kn_done, s.qn_done, s.vt_mm)["kqu".index(kind)], i)
                nc.scalar.activation(dst[:], cb[:, 0:T], ACT.Copy, scale=col("c4", tile * 4)).then_inc(s.c0_done, 1)
            elif kind == "z":
                act.wait_ge(s.a_free, g + 1)
                nc.scalar.activation(sig[:], sig[:], ACT.Silu).then_inc(s.sz_done, 1)

        def post_act1(act, g):
            kind, i = ORDER[g]
            if kind not in "kqu":
                return
            m = 3 * i + "kqu".index(kind)
            dst = (sk, sq, sv)["kqu".index(kind)]
            act.wait_ge(s.ctap, 3 * m + 3)
            nc.scalar.activation(dst[:], dst[:], ACT.Silu).then_inc(s.silu_done, 1)
            if kind != "u":
                n = 2 * i + (kind == "q")
                act.wait_ge(s.silu_done, m + 1)
                if n >= 2:
                    act.wait_ge(s.kqss_mm, n - 1)
                nc.scalar.activation(sqb[:, n % 2, :], dst[:], ACT.Square).then_inc(s.sqh_done, 1)

        def ab_pe(pe):
            pe.wait_ge(s.const_in, 16)
            pe.wait_ge(s.a_free, 1)
            for c in range(NC):
                mm = nc.tensor.transpose(B[3][:, c * 8:(c + 1) * 8], ab[:, c * P:(c + 1) * P], const[0:8, IDENT, 0:8])
            mm.then_inc(s.ab_t, 1)

        def cols_pe(pe):
            pe.wait_ge(s.sg_g, 1)
            for i, m in enumerate((UPPER, AFTER, ONES)):
                mm = nc.tensor.matmul(B[3][:, 16 * i:16 * i + 16], cm(m), sm[:, 4, :], start=(i == 0), stop=(i == 2),
                                      skip_group_check=True)
            mm.then_inc(s.cols_mm, 1)

        def ab_act(act):
            pa = B[3][:, 0:32].rearrange("p (c k) -> p c k", k=8)
            v = lambda i: sm[:, i, :].rearrange("p (c h) -> p c h", h=NH)
            act.wait_ge(s.sg_xa, 1)
            nc.scalar.activation(v(0), pa[:, :, NH:2 * NH], ACT.Sigmoid).then_inc(s.sg_beta, 1)
            act.preload_act_table_set("natural_log_exp_and_others")
            act.wait_ge(s.sg_abs, 1)
            nc.scalar.activation(sm[:, 2, :], sm[:, 2, :], ACT.Exp).then_inc(s.sg_e, 1)
            act.wait_ge(s.sg_e, 1)
            nc.scalar.activation(sm[:, 3, :], sm[:, 2, :], ACT.Ln, bias=1.0).then_inc(s.sg_l, 1)
            nc.scalar.activation(sm[:, 9, 0:NH], par[:, PAR["alog"]:PAR["alog"] + NH], ACT.Exp).then_inc(s.sg_ea, 1)

        def cols_act(act):
            act.wait_ge(s.const_in, 16)
            for dst, i in ((after_r, AFTER), (ones_r, ONES)):
                nc.scalar.activation(dst[:], cm(i), ACT.Copy).then_inc(s.afr_done, 1)
            act.wait_ge(s.cols_mm, 1)
            nc.scalar.activation(sm[:, 5:8, :].rearrange("p a b -> p (a b)"), B[3][:, 0:48], ACT.Exp).then_inc(s.cols_exp, 1)

        def ab_dve(dve):
            pa = B[3][:, 0:32].rearrange("p (c k) -> p c k", k=8)
            v = lambda i: sm[:, i, :].rearrange("p (c h) -> p c h", h=NH)
            hbc = lambda ap: ap.unsqueeze(1).to_broadcast([P, NC, NH])
            dve.wait_ge(s.ab_t, 1)
            nc.vector.tensor_tensor(v(1), pa[:, :, 0:NH], hbc(par[:, PAR["dtb"]:PAR["dtb"] + NH]), ALU.add).then_inc(s.sg_xa, 1)
            dve.wait_ge(s.sg_xa, 1)
            nc.vector.scalar_tensor_tensor(sm[:, 2, :], sm[:, 1, :], -1.0, sm[:, 1, :], ALU.mult, ALU.min).then_inc(s.sg_abs, 1)
            dve.wait_ge(s.sg_l, 1)
            nc.vector.scalar_tensor_tensor(sm[:, 10, :], sm[:, 1, :], 0.0, sm[:, 3, :], ALU.max, ALU.add).then_inc(s.sg_sp, 1)
            dve.wait_ge(s.sg_ea, 1)
            dve.wait_ge(s.sg_sp, 1)
            nc.vector.scalar_tensor_tensor(v(4), v(10), -1.0, hbc(sm[:, 9, 0:NH]), ALU.mult, ALU.mult).then_inc(s.sg_g, 1)

        def cols_dve(dve):
            dve.wait_ge(s.cols_exp, 1)
            nc.vector.tensor_tensor(sm[:, 8, :], sm[:, 0, :], sm[:, 5, :], ALU.mult).then_inc(s.sg_bg, 1)

        def l2_pe(pe, h):
            if h:
                pe.wait_ge(s.y_done, LEVELS * h)
            for j in range(2):
                pe.wait_ge(s.sqh_done, 2 * h + j + 1)
                nc.tensor.matmul(B[3 + j][:], cm(ONES), sqb[:, j, :], start=True, stop=True).then_inc(s.kqss_mm, 1)

        def l2_act(act, h):
            act.preload_act_table_set("natural_log_exp_and_others")
            for j in range(2):
                act.wait_ge(s.kqss_mm, 2 * h + j + 1)
                nc.scalar.activation(rkq[:, j, :], B[3 + j][:], ACT.Ln, bias=eps[:, 0:1]).then_inc(s.kq_ln, 1)
            for j in range(2):
                act.wait_ge(s.kq_ln, 2 * h + j + 1)
                nc.scalar.activation(rkq[:, j, :], rkq[:, j, :], ACT.Exp, scale=-0.5).then_inc(s.kq_r, 1)

        def kn_dve(dve, h):
            dve.wait_ge(s.kq_r, 2 * h + 1)
            if h:
                dve.wait_ge(s.kt_mm, h)
            nc.vector.tensor_tensor(flat(kn), sk[:], rkq[:, 0, :], ALU.mult).then_inc(s.kn_done, 1)

        def qn_dve(dve, h):
            dve.wait_ge(s.kq_r, 2 * h + 2)
            nc.vector.scalar_tensor_tensor(flat(qn), sq[:], P ** -0.5, rkq[:, 1, :], ALU.mult, ALU.mult).then_inc(s.qn_done, 1)

        def gu_pool(pool, h):
            if h:
                pool.wait_ge(s.gu_done, 2 * h)
                pool.wait_ge(s.gb_mm, h)
            nc.gpsimd.tensor_tensor(gU[:], bc(cm(UPPER)), tok(4, h), ALU.mult).then_inc(s.gu_f, 1)
            pool.wait_ge(s.gu_f, h + 1)
            nc.gpsimd.tensor_scalar(gU_hi[:], gU[:], 1.0, None, ALU.mult).then_inc(s.gu_done, 1)
            pool.wait_ge(s.gu_done, 2 * h + 1)
            nc.gpsimd.tensor_tensor(gU_lo[:], gU[:], gU_hi[:].bitcast(f32), ALU.subtract).then_inc(s.gu_done, 1)

        def dt_pe(pe, h):
            pe.wait_ge(s.gu_done, 2 * h + 2)
            nc.tensor.matmul(B[5][:], after_r[:], flat(gU_lo), start=True, stop=False)
            nc.tensor.matmul(B[5][:], after_r[:], flat(gU_hi), start=False, stop=True).then_inc(s.dt_mm, 1)

        def dt_act(act, h):
            act.wait_ge(s.dt_mm, h + 1)
            nc.scalar.activation(qkd[:, h % 2].rearrange("p c t -> p (c t)"), B[5][:], ACT.Exp).then_inc(s.edt_done, 1)

        def dn_pe(pe, h):
            pe.wait_ge(s.edt_done, h + 1)
            for c in range(NC):
                mm = nc.tensor.transpose(B[5][:, c * P:(c + 1) * P], qkd[:, h % 2, c, :], cm(IDENT))
            mm.then_inc(s.dn_mm, 1)

        def kk_pe(pe, h):
            pe.wait_ge(s.kn_done, h + 1)
            pe.wait_ge(s.kq_ln, 2 * h + 1)
            for c in range(NC):
                mm = nc.tensor.matmul(B[3][:, c * P:(c + 1) * P], kn[:, c, :], kn[:, c, :], start=True, stop=True)
            mm.then_inc(s.kk_mm, 1)

        def a1_dve(dve, h):
            dve.wait_ge(s.kk_mm, h + 1)
            dve.wait_ge(s.dn_mm, h + 1)
            nc.vector.tensor_tensor(eDn[:], r3(B[3]), tok(0, h), ALU.mult).then_inc(s.a1_done, 1)

        def a2_dve(dve, h):
            dve.wait_ge(s.a1_done, h + 1)
            nc.vector.tensor_tensor(eDn[:], r3(B[5]), eDn[:], ALU.mult).then_inc(s.a2_done, 1)

        def qk_pe(pe, h):
            pe.wait_ge(s.qn_done, h + 1)
            if h:
                pe.wait_ge(s.kbg_done, h)
            for c in range(NC):
                mm = nc.tensor.matmul(B[2][:, c * P:(c + 1) * P], kn[:, c, :], qn[:, c, :], start=True, stop=True)
            mm.then_inc(s.qk_mm, 1)

        def kt_pe(pe, h):
            pe.wait_ge(s.qkd_done, h + 1)
            for c in range(NC):
                mm = nc.tensor.transpose(B[2][:, c * P:(c + 1) * P], kn[:, c, :], cm(IDENT))
            mm.then_inc(s.kt_mm, 1)

        def gb_pe(pe, h):
            if h:
                pe.wait_ge(s.v_done, NC * h)
            nc.tensor.matmul(B[6][:], ones_r[:], flat(gU_lo), start=True, stop=False)
            nc.tensor.matmul(B[6][:], ones_r[:], flat(gU_hi), start=False, stop=True).then_inc(s.gb_mm, 1)

        def vt0_pe(pe, h):
            pe.wait_ge(s.silu_done, 3 * h + 3)
            pe.wait_ge(s.egb_done, h + 1)
            for c in range(NC):
                mm = nc.tensor.transpose(B[6][:, c * P:(c + 1) * P], sv[:, c * P:(c + 1) * P], cm(IDENT))
            mm.then_inc(s.vt_mm, 1)

        def gb_act(act, h):
            act.preload_act_table_set("natural_log_exp_and_others")
            act.wait_ge(s.gb_mm, h + 1)
            nc.scalar.activation(flat(qd), B[6][:], ACT.Exp).then_inc(s.egb_done, 1)

        def scaled_act(dst, bank, i, h, done):
            for c in range(NC):
                a = nc.scalar.activation(dst[:, c, :], bank[:, c * P:(c + 1) * P], ACT.Copy,
                                         scale=sm[:, i, NH * c + h:NH * c + h + 1])
            a.then_inc(done, 1)

        def kt_act(act, h):
            act.wait_ge(s.kt_mm, h + 1)
            scaled_act(ktail, B[2], 6, h, s.ktail_done)
            scaled_act(kbg, B[2], 8, h, s.kbg_done)

        def vt0_act(act, h):
            act.wait_ge(s.vt_mm, h + 1)
            scaled_act(vb, B[6], 0, h, s.vb_done)

        def qkd_dve(dve, h):
            dve.wait_ge(s.qk_mm, h + 1)
            dve.wait_ge(s.edt_done, h + 1)
            nc.vector.tensor_tensor(qkd[:, h % 2], r3(B[2]), qkd[:, h % 2], ALU.mult).then_inc(s.qkd_done, 1)

        def qkd_pool(pool, h):
            pool.wait_ge(s.qkd_done, h + 1)
            nc.gpsimd.affine_select(out=qkd[:, h % 2], in_=qkd[:, h % 2], compare_op=ALU.is_ge, fill=0.0, base=0,
                                    pattern=[[0, NC], [1, P]], channel_multiplier=-1).then_inc(s.qkd_masked, 1)

        def qd_dve(dve, h):
            dve.wait_ge(s.egb_done, h + 1)
            nc.vector.tensor_tensor(qd[:], qd[:], qn[:], ALU.mult).then_inc(s.qd_done, 1)

        HP = P // 2

        def odd_cols(a, l):
            return a.rearrange("p (g two b) -> p g two b", two=2, b=1 << l)[:, :, 1, :]

        def odd_all(a, l):
            return a.rearrange("p c (g two b) -> p c g two b", two=2, b=1 << l)[:, :, :, 1, :]

        def packed(a, l):
            return a.rearrange("p (c g b) -> p c g b", c=NC, b=1 << l)

        T2p = flat(T2)[:, 0:NC * HP]

        def inv_t_pe(pe, h, l):
            n = LEVELS * h + l
            if l == 0:
                pe.wait_ge(s.a2_done, h + 1)
                for c in range(NC):
                    mm = nc.tensor.transpose(B[3][:, c * P:(c + 1) * P], eDn[:, c, :], cm(IDENT))
                mm.then_inc(s.t_mm, 1)
                return
            pe.wait_ge(s.y_done, n)
            for c in range(NC):
                mm = nc.tensor.transpose(B[4][:, c * P:(c + 1) * P], Y[:, c, :], cm(IDENT))
            mm.then_inc(s.xt_mm, 1)
            for c in range(NC):
                mm = nc.tensor.matmul(B[3][:, c * HP:(c + 1) * HP], eDn[:, c, :], odd_cols(Y[:, c, :], l), start=True, stop=True)
            mm.then_inc(s.t_mm, 1)

        def inv_y_pe(pe, h, l):
            pe.wait_ge(s.t2_done, LEVELS * h + l + 1)
            pe.wait_ge(s.x_done, (LEVELS - 1) * h + l)
            for c in range(NC):
                mm = nc.tensor.matmul(B[5][:, c * HP:(c + 1) * HP], X[:, c, :], T2p[:, c * HP:(c + 1) * HP], start=True, stop=True)
            mm.then_inc(s.ym_mm, 1)

        def inv_x_act(act, h, l):
            act.wait_ge(s.xt_mm, (LEVELS - 1) * h + l)
            nc.scalar.activation(flat(X), B[4][:], ACT.Copy).then_inc(s.x_done, 1)

        def inv_t_dve(dve, h, l):
            n = LEVELS * h + l
            dve.wait_ge(s.t_mm, n + 1)
            if l == 0:
                nc.vector.tensor_tensor(T2[:], r3(B[3]), bc(cm(LEV0)), ALU.mult).then_inc(s.t2_done, 1)
                return
            nc.vector.tensor_tensor(packed(T2p, l), packed(B[3][:, 0:NC * HP], l),
                                    odd_cols(cm(LEV0 + l), l).unsqueeze(1).to_broadcast([P, NC, HP >> l, 1 << l]),
                                    ALU.mult).then_inc(s.t2_done, 1)

        def inv_y_dve(dve, h, l):
            n = LEVELS * h + l
            if l == 0:
                dve.wait_ge(s.t2_done, n + 1)
                if h:
                    dve.wait_ge(s.o_mm, h)
                nc.vector.tensor_tensor(Y[:], bc(cm(IDENT)), T2[:], ALU.subtract).then_inc(s.y_done, 1)
                return
            dve.wait_ge(s.ym_mm, (LEVELS - 1) * h + l)
            dve.wait_ge(s.y_done, n)
            nc.vector.tensor_tensor(odd_all(Y, l), odd_all(Y, l), packed(B[5][:, 0:NC * HP], l), ALU.subtract).then_inc(s.y_done, 1)

        def wt_pe(pe, h):
            pe.wait_ge(s.y_done, LEVELS * (h + 1))
            pe.wait_ge(s.kbg_done, h + 1)
            pe.wait_ge(s.vb_done, h + 1)
            for c in range(NC):
                mm = nc.tensor.matmul(B[6][:, c * P:(c + 1) * P], kbg[:, c, :], Y[:, c, :], start=True, stop=True)
            mm.then_inc(s.wt_mm, 1)

        def wt_act(act, h):
            act.wait_ge(s.wt_mm, h + 1)
            nc.scalar.activation(nWT[:].rearrange("p c t -> p (c t)"), B[6][:], ACT.Copy, scale=-1.0).then_inc(s.wt_done, 1)

        def seq_v_pe(pe, h, c):
            if c == 0:
                pe.wait_ge(s.wt_done, h + 1)
            else:
                pe.wait_ge(s.s_done, (NC - 1) * h + c)
            mm = nc.tensor.matmul(B[6][:, 0:P], Y[:, c, :], vb[:, c, :], start=True, stop=(c == 0))
            if c:
                mm = nc.tensor.matmul(B[6][:, 0:P], nWT[:, c, :], S[:], start=False, stop=True)
            mm.then_inc(s.v_mm, 1)

        def seq_o_pe(pe, h, c):
            if c == 0:
                pe.wait_ge(s.qkd_masked, h + 1)
                pe.wait_ge(s.qd_done, h + 1)
                if h:
                    pe.wait_ge(s.o_ln, h)
            else:
                nc.tensor.matmul(B[7][:, c * P:(c + 1) * P], S[:], qd[:, c, :], start=False, stop=False,
                                 skip_group_check=True)
            pe.wait_ge(s.v_done, NC * h + c + 1)
            mm = nc.tensor.matmul(B[7][:, c * P:(c + 1) * P], vnew[:], qkd[:, h % 2, c, :], start=(c == 0), stop=True,
                                  skip_group_check=True)
            if c == NC - 1:
                mm.then_inc(s.o_mm, 1)
            else:
                nc.tensor.matmul(B[6][:, P:2 * P], ktail[:, c, :], vnew[:], start=True, stop=True).then_inc(s.s_mm, 1)

        def seq_act(act, h, c):
            act.wait_ge(s.v_mm, NC * h + c + 1)
            nc.scalar.activation(vnew[:], B[6][:, 0:P], ACT.Copy).then_inc(s.v_done, 1)

        def seq_dve(dve, h, c):
            n = (NC - 1) * h + c
            dve.wait_ge(s.s_mm, n + 1)
            if c == 0:
                nc.vector.tensor_copy(S[:], B[6][:, P:2 * P]).then_inc(s.s_done, 1)
            else:
                dve.wait_ge(s.s_done, n)
                nc.vector.scalar_tensor_tensor(S[:], S[:], sm[:, 7, NH * c + h:NH * c + h + 1], B[6][:, P:2 * P],
                                               ALU.mult, ALU.add).then_inc(s.s_done, 1)

        def on_pe(pe, h):
            pe.wait_ge(s.osq_done, h + 1)
            nc.tensor.matmul(B[7][:], cm(ONES), ro[:], start=True, stop=True).then_inc(s.oss_mm, 1)

        def on_act(act, h):
            act.wait_ge(s.o_mm, h + 1)
            nc.scalar.activation(oc[:, h, :], B[7][:], ACT.Copy).then_inc(s.oc_done, 1)
            if h:
                act.wait_ge(s.on_done, h)
            act.wait_ge(s.oc_done, h + 1)
            nc.scalar.activation(ro[:], oc[:, h, :], ACT.Square).then_inc(s.osq_done, 1)

        def on_act2(act, h):
            if h == NH - 1:
                act.preload_act_table_set("natural_log_exp_and_others")
            act.wait_ge(s.oss_mm, h + 1)
            nc.scalar.activation(ro[:], B[7][:], ACT.Ln, bias=eps[:, 0:1], scale=1.0 / P).then_inc(s.o_ln, 1)
            act.wait_ge(s.o_ln, h + 1)
            nc.scalar.activation(ro[:], ro[:], ACT.Exp, scale=-0.5).then_inc(s.o_r, 1)

        def on_dve(dve, h):
            dve.wait_ge(s.o_r, h + 1)
            nc.vector.scalar_tensor_tensor(oc[:, h, :], oc[:, h, :], col("onorm"), ro[:], ALU.mult,
                                           ALU.mult).then_inc(s.on_done, 1)

        def yb_dve(dve, h):
            dve.wait_ge(s.sz_done, h + 1)
            dve.wait_ge(s.on_done, h + 1)
            nc.vector.tensor_tensor(oc[:, h, :], oc[:, h, :], sig[:], ALU.mult).then_inc(s.yb_f, 1)

        def yb_act(act, h):
            act.wait_ge(s.yb_f, h + 1)
            nc.scalar.activation(yb_hi[:, h, :], oc[:, h, :], ACT.Copy).then_inc(s.yb_hid, 1)

        def yb_lo_dve(dve, h):
            dve.wait_ge(s.yb_hid, h + 1)
            nc.vector.tensor_tensor(yb_lo[:, h, :], oc[:, h, :], yb_hi[:, h, :].bitcast(f32),
                                    ALU.subtract).then_inc(s.yb_lod, 1)

        def ln_pool(pool):
            end_of = lambda i: TAP.index((i, C31 - 1)) + 1
            pool.wait_ge(s.c0_done, 3 * NH)
            pool.wait_ge(s.ctap, 9 * NH)
            pool.wait_ge(s.cf_tap, max(end_of(0), end_of(2)))
            nc.gpsimd.tensor_tensor(cb[:, 0:T], tc[:, 0, :], tc[:, 2, :], ALU.add).then_inc(s.tsum_done, 1)
            for n, i in enumerate((1, 3)):
                pool.wait_ge(s.cf_tap, end_of(i))
                pool.wait_ge(s.tsum_done, n + 1)
                nc.gpsimd.tensor_tensor(cb[:, 0:T], cb[:, 0:T], tc[:, i, :], ALU.add).then_inc(s.tsum_done, 1)

        def mu_pe(pe):
            pe.wait_ge(s.tsum_done, CA - 1)
            pe.wait_ge(s.wt_done, NH)
            pe.wait_ge(s.v_done, NC * NH)
            nc.tensor.matmul(B[6][:], cm(ONES), cb[:, 0:T], start=True, stop=True).then_inc(s.mu_mm, 1)

        def var_pe(pe):
            pe.wait_ge(s.o_ln, NH)
            pe.wait_ge(s.qsum_done, CA - 1)
            nc.tensor.matmul(B[7][:], cm(ONES), sk[:], start=True, stop=True).then_inc(s.var_mm, 1)

        def sq_act(act, tiles):
            for i in tiles:
                act.wait_ge(s.xc_done, i + 1)
                if i >= 2:
                    act.wait_ge(s.qsum_done, 1)
                nc.scalar.activation(sqb[:, i % 2, :], tc[:, i, :], ACT.Square).then_inc(s.csq_done, 1)

        def var_act(act):
            act.preload_act_table_set("natural_log_exp_and_others")
            act.wait_ge(s.var_mm, 1)
            nc.scalar.activation(rkq[:, 0, :], B[7][:], ACT.Ln, bias=eps[:, 1:2], scale=1.0 / (CA * P)).then_inc(s.c_ln, 1)
            act.wait_ge(s.c_ln, 1)
            nc.scalar.activation(rkq[:, 0, :], rkq[:, 0, :], ACT.Exp, scale=-0.5).then_inc(s.c_r, 1)

        def xc_dve(dve, tiles):
            dve.wait_ge(s.mu_mm, 1)
            for i in tiles:
                nc.vector.scalar_tensor_tensor(tc[:, i, :], B[6][:], -1.0 / (CA * P), tc[:, i, :], ALU.mult,
                                               ALU.add).then_inc(s.xc_done, 1)

        def qsum_dve(dve, i):
            dve.wait_ge(s.csq_done, i + 1)
            if i == 1:
                nc.vector.tensor_tensor(sk[:], sqb[:, 0, :], sqb[:, 1, :], ALU.add).then_inc(s.qsum_done, 1)
            else:
                dve.wait_ge(s.qsum_done, i - 1)
                nc.vector.tensor_tensor(sk[:], sk[:], sqb[:, i % 2, :], ALU.add).then_inc(s.qsum_done, 1)

        def cn_dve(dve):
            dve.wait_ge(s.c_r, 1)
            for i in range(CA):
                nc.vector.scalar_tensor_tensor(tc[:, i, :], tc[:, i, :], col("lnw", i), rkq[:, 0, :], ALU.mult,
                                               ALU.mult).then_inc(s.cn_done, 1)

        def ya_act(act):
            def silu(i):
                act.wait_ge(s.cn_done, i + 1)
                nc.scalar.activation(tc[:, i, :], tc[:, i, :], ACT.Silu, bias=col("lnb", i)).then_inc(s.ya_f, 1)
            silu(0)
            for i in range(CA):
                if i + 1 < CA:
                    silu(i + 1)
                act.wait_ge(s.ya_f, i + 1)
                nc.scalar.activation(ya_hi[:, i, :], tc[:, i, :], ACT.Copy).then_inc(s.ya_hid, 1)
                if i == 1:
                    split_act(act, BO0 + 7)

        def ya_dve(dve):
            for i in range(CA):
                dve.wait_ge(s.ya_hid, i + 1)
                nc.vector.tensor_tensor(ya_lo[:, i, :], tc[:, i, :], ya_hi[:, i, :].bitcast(f32),
                                        ALU.subtract).then_inc(s.ya_lod, 1)
                if i == 1:
                    split_dve(dve, BO0 + 7)

        OUT0 = (2, 3, 4, 5, 1, 0, 6, 7)

        def out0_part(pe, j, k0, k1):
            n, half = j % KT, j // KT
            b = BO0 + j
            w_wait(pe, b)
            if j == 4:
                pe.wait_ge(s.a_free, NB0)
            if j == 6:
                pe.wait_ge(s.xc_done, CA)
            if j == 7:
                pe.wait_ge(s.c_ln, 1)
            for k in range(k0, k1):
                if half == 0:
                    pe.wait_ge(s.yb_lod, k + 1)
                else:
                    pe.wait_ge(s.ya_lod, k + 1)
                ahi, alo = (ya_hi, ya_lo) if half else (yb_hi, yb_lo)
                mm = mm3(B[OUT0[n]][:], w_hi[:, b % RING, k * P:(k + 1) * P], w_lo[:, b % RING, k * P:(k + 1) * P],
                         ahi[:, k, :], alo[:, k, :], half == 0 and k == 0, half == 1 and k == CA - 1)
            if k1 == CA:
                mm.then_inc(s.block_done, 1)

        def out0_pe(pe):
            out0_part(pe, 0, 0, NH - 1)
            on_pe(pe, NH - 1)
            out0_part(pe, 1, 0, NH - 1)
            out0_part(pe, 2, 0, NH - 1)
            mu_pe(pe)
            for j in range(3):
                out0_part(pe, j, NH - 1, NH)
            out0_part(pe, 3, 0, CA)
            var_pe(pe)
            for j in range(4, 2 * KT):
                out0_part(pe, j, 0, CA)

        def out0_act(act):
            split_act(act, BO0 + 3)
            sq_act(act, (0,))
            split_act(act, BO0 + 4)
            sq_act(act, (1, 2, 3))
            split_act(act, BO0 + 5)
            var_act(act)
            split_act(act, BO0 + 6)
            ya_act(act)
            for j in range(5, 8):
                split_act(act, BO0 + j + 3)
            for n in range(KT):
                split_act(act, BO0 + KT + n + 3)
                rnorm_act(act, 1, n, False)

        def out0_dve(dve):
            xc_dve(dve, (0, 1))
            split_dve(dve, BO0 + 3)
            xc_dve(dve, (2, 3))
            split_dve(dve, BO0 + 4)
            qsum_dve(dve, 1)
            qsum_dve(dve, 2)
            qsum_dve(dve, 3)
            split_dve(dve, BO0 + 5)
            cn_dve(dve)
            split_dve(dve, BO0 + 6)
            ya_dve(dve)
            for j in range(5, 8):
                split_dve(dve, BO0 + j + 3)
            for n in range(KT):
                dve.wait_ge(s.block_done, BO0 + KT + n + 1)
                nc.vector.tensor_tensor(x[:, n, :], x[:, n, :], B[OUT0[n]][:], ALU.add).then_inc(s.x_new, 1)
                split_dve(dve, BO0 + KT + n + 3)
                rnorm_lo(dve, 1, n)

        def window(g):
            return ((g - 12) % 3, (g - 12) // 3) if g >= 12 else (None, None)

        def a_pe(pe):
            for g in range(NB0):
                w_wait(pe, g)
                if g >= 3:
                    pe.wait_ge(s.a_free, g - 2 if g < 12 else g - 1)
                bank = group_bank(g)
                mc = 8 if g == 0 else P

                def part(k0, k1):
                    mm = gemm(bank, g, k0, k1, h_hi, h_lo, k0 == 0, k1 == KT, mc)
                    if k1 == KT:
                        mm.then_inc(s.block_done, 1)
                w, h = window(g)
                if g == 0:
                    for k in range(KT):
                        pe.wait_ge(s.h_lo_done, k + 1)
                        part(k, k + 1)
                elif w == 0:
                    if h == 0:
                        pe.wait_ge(s.afr_done, 2)
                        dt_pe(pe, h)
                        part(0, 3)
                        l2_pe(pe, h)
                        part(3, 6)
                        dn_pe(pe, h)
                        kk_pe(pe, h)
                        part(6, 8)
                        continue
                    now = h < NH
                    if now:
                        l2_pe(pe, h)
                    wt_pe(pe, h - 1)
                    part(0, 1)
                    if now:
                        dt_pe(pe, h)
                    for c in range(NC):
                        part(2 * c + 1, 2 * c + 2)
                        if c == 1 and now:
                            dn_pe(pe, h)
                            kk_pe(pe, h)
                        seq_v_pe(pe, h - 1, c)
                        if c < NC - 1:
                            part(2 * c + 2, 2 * c + 3)
                        seq_o_pe(pe, h - 1, c)
                elif w == 1:
                    inv_t_pe(pe, h, 0)
                    part(0, 1)
                    qk_pe(pe, h)
                    gb_pe(pe, h)
                    part(1, 2)
                    inv_t_pe(pe, h, 1)
                    if h:
                        on_pe(pe, h - 1)
                    part(2, 3)
                    inv_y_pe(pe, h, 1)
                    part(3, 4)
                    inv_t_pe(pe, h, 2)
                    part(4, 5)
                    inv_y_pe(pe, h, 2)
                    kt_pe(pe, h)
                    part(5, 6)
                    vt0_pe(pe, h)
                    part(6, 8)
                elif w == 2:
                    for l in range(3, LEVELS):
                        inv_t_pe(pe, h, l)
                        part(2 * l - 6, 2 * l - 5)
                        inv_y_pe(pe, h, l)
                        part(2 * l - 5, 2 * l - 4)
                else:
                    part(0, KT)
                if g == 1:
                    pe.wait_ge(s.const_in, 16)
                    stat_pe(pe, 0, B[7])
                if g == 3:
                    ab_pe(pe)
                if g == 5:
                    cols_pe(pe)
        def split_act(act, b):
            if b < BEND:
                w_hi_of(act, b, nblk(b))

        def split_dve(dve, b):
            if b < BEND:
                w_lo_of(dve, b, nblk(b))

        def a_act(act):
            act.wait_ge(s.norms_in, 16)
            for k in range(KT):
                norm0_hi(act, k)
                if k in (1, 4, 7):
                    split_act(act, (1, 4, 7).index(k))
                if k >= 2:
                    norm0_sq(act, k - 2)
            norm0_sq(act, KT - 2)
            norm0_sq(act, KT - 1)
            act.wait_ge(s.ones_set, 1)
            act.wait_ge(s.par_in, 16)
            stat_act(act, 0, B[7])
            for g in range(NB0):
                w, h = window(g)
                if w == 0:
                    if h < NH:
                        l2_act(act, h)
                    if h:
                        wt_act(act, h - 1)
                    post_act0(act, g - 1)
                    if h:
                        seq_act(act, h - 1, 0)
                    split_act(act, g + 2)
                    if h < NH:
                        dt_act(act, h)
                    if h:
                        for c in range(1, NC):
                            seq_act(act, h - 1, c)
                    post_act1(act, g - 1)
                    if h:
                        on_act(act, h - 1)
                elif w == 1:
                    gb_act(act, h)
                    if h < NH - 1:
                        post_act0(act, g - 1)
                    inv_x_act(act, h, 1)
                    split_act(act, g + 2)
                    if h:
                        on_act2(act, h - 1)
                    inv_x_act(act, h, 2)
                    kt_act(act, h)
                    vt0_act(act, h)
                    inv_x_act(act, h, 3)
                    if h == NH - 1:
                        post_act0(act, g - 1)
                    post_act1(act, g - 1)
                elif w == 2:
                    post_act0(act, g - 1)
                    split_act(act, g + 2)
                    inv_x_act(act, h, 4)
                    inv_x_act(act, h, 5)
                    inv_x_act(act, h, 6)
                    post_act1(act, g - 1)
                elif g >= 1:
                    split_act(act, g + 2)
                    post_act0(act, g - 1)
                    post_act1(act, g - 1)
                if g == 3:
                    ab_act(act)
                if g == 6:
                    cols_act(act)
                if g >= 1 and ORDER[g - 1][0] == "z":
                    yb_act(act, ORDER[g - 1][1])
            split_act(act, NB0 + 2)
            on_act2(act, NH - 1)
            post_act0(act, NB0 - 1)
            yb_act(act, NH - 1)

        def norm0_hi(act, k):
            act.wait_ge(x_in[k], 16)
            nc.scalar.activation(h_hi[:, k, :], x[:, k, :], ACT.Copy, scale=col("norm", k)).then_inc(s.h_hi_done, 1)

        def norm0_sq(act, k):
            if k >= 2:
                act.wait_ge(s.ssq_done, k - 1)
            nc.scalar.activation(sq2[:, k % 2, :], x[:, k, :], ACT.Square).then_inc(s.sq_done, 1)

        def a_dve(dve):
            for a in (hb[:, :, 0:C31 - 1], cb[:, 0:3]):
                nc.vector.memset(a, 0.0).then_inc(s.halo_set, 1)
            dve.wait_ge(s.norms_in, 16)
            dve.wait_ge(s.halo_set, 2)
            for k in range(KT):
                dve.wait_ge(x_in[k], 16)
                norm_lo(dve, 0, k)
                if k in (1, 4, 7):
                    split_dve(dve, (1, 4, 7).index(k))
            dve.wait_ge(s.par_in, 16)
            dve.wait_ge(s.const_in, 16)
            for g in range(NB0):
                w, h = window(g)
                if w is None and g >= 1:
                    split_dve(dve, g + 2)
                    post_evac(dve, g - 1)
                    kind = ORDER[g - 1][0]
                    if kind == "v":
                        taps(dve, EARLY[g] // 2)
                        glu(dve, g - 1)
                        taps(dve, EARLY[g] - EARLY[g] // 2)
                    elif kind in "kqu":
                        for j in range(1, 4):
                            taps(dve, EARLY[g] // 3)
                            short_tap(dve, g - 1, j)
                    else:
                        taps(dve, EARLY[g])
                elif w == 0:
                    post_evac(dve, g - 1)
                    taps(dve, 1)
                    if h < NH:
                        kn_dve(dve, h)
                        qn_dve(dve, h)
                    short_tap(dve, g - 1, 1)
                    if h:
                        seq_dve(dve, h - 1, 0)
                    split_dve(dve, g + 2)
                    if h < NH:
                        a1_dve(dve, h)
                    short_tap(dve, g - 1, 2)
                    if h:
                        seq_dve(dve, h - 1, 1)
                    if h < NH:
                        a2_dve(dve, h)
                    short_tap(dve, g - 1, 3)
                    taps(dve, 1)
                    if h:
                        seq_dve(dve, h - 1, 2)
                    taps(dve, TAPS0 if h else TAPS6)
                elif w == 1:
                    inv_t_dve(dve, h, 0)
                    inv_y_dve(dve, h, 0)
                    post_evac(dve, g - 1)
                    taps(dve, TAPS1)
                    inv_t_dve(dve, h, 1)
                    qkd_dve(dve, h)
                    inv_y_dve(dve, h, 1)
                    split_dve(dve, g + 2)
                    short_tap(dve, g - 1, 1)
                    inv_t_dve(dve, h, 2)
                    taps(dve, 1)
                    short_tap(dve, g - 1, 2)
                    inv_y_dve(dve, h, 2)
                    qd_dve(dve, h)
                    short_tap(dve, g - 1, 3)
                    taps(dve, TAPS2)
                elif w == 2:
                    inv_t_dve(dve, h, 3)
                    inv_y_dve(dve, h, 3)
                    if h == NH - 1:
                        yb_dve(dve, 0)
                        yb_lo_dve(dve, 0)
                    post_evac(dve, g - 1)
                    if h:
                        on_dve(dve, h - 1)
                    short_tap(dve, g - 1, 1)
                    inv_t_dve(dve, h, 4)
                    split_dve(dve, g + 2)
                    inv_y_dve(dve, h, 4)
                    short_tap(dve, g - 1, 2)
                    taps(dve, TAPS3)
                    inv_t_dve(dve, h, 5)
                    taps(dve, TAPS4)
                    inv_y_dve(dve, h, 5)
                    short_tap(dve, g - 1, 3)
                    taps(dve, TAPS3)
                    inv_t_dve(dve, h, 6)
                    taps(dve, TAPS4)
                    inv_y_dve(dve, h, 6)
                    taps(dve, TAPS5)
                if g == 3:
                    ab_dve(dve)
                if g == 7:
                    cols_dve(dve)
                if g >= 1 and ORDER[g - 1] in (("z", 1), ("z", 2)):
                    yb_dve(dve, ORDER[g - 1][1])
                    yb_lo_dve(dve, ORDER[g - 1][1])
            post_evac(dve, NB0 - 1)
            split_dve(dve, NB0 + 2)
            taps(dve, TAPS)
            on_dve(dve, NH - 1)
            yb_dve(dve, NH - 1)
            yb_lo_dve(dve, NH - 1)

        def a_pool(pool):
            norm_pool(pool, 0)
            pool.wait_ge(s.sg_g, 1)
            gu_pool(pool, 0)
            for h in range(NH):
                qkd_pool(pool, h)
                if h < NH - 1:
                    gu_pool(pool, h + 1)
            ln_pool(pool)

        def resid_dve(dve, r, n, b_last, it=None):
            if it is None:
                dve.wait_ge(s.block_done, b_last + 1)
                xt = x[:, n, :]
            else:
                i, mt, mb = it
                dve.wait_ge(s.block_done, i * mb + (b_last + 1))
                xt = x[:, bass.ds(i * mt + n, 1), :].rearrange("p o t -> p (o t)")
            nc.vector.tensor_tensor(xt, xt, B[6 + n % 2][:], ALU.add).then_inc(s.x_new, 1)

        def rnorm_act(act, r, n, last, it=None):
            i, mt = (None, 0) if it is None else it[:2]
            xn = KT * (r - 1) + n
            c = KT * r + n
            g = lambda a: a[:, n, :] if it is None else a[:, bass.ds(i * mt + n, 1), :].rearrange("p o t -> p (o t)")
            at = lambda v: v if it is None else i * mt + v
            act.wait_ge(s.ssq_done, at(c - 1))
            act.wait_ge(s.x_new, at(xn + 1))
            if not last:
                w = col("norm", KT * r + n) if it is None else par[:, bass.ds(i * mt + (PAR["norm"] + KT * r + n), 1)]
                nc.scalar.activation(g(h_hi), g(x), ACT.Copy, scale=w).then_inc(s.h_hi_done, 1)
            nc.scalar.activation(sq2[:, n % 2, :], g(x), ACT.Square).then_inc(s.sq_done, 1)
            if last:
                w = col("norm", KT * r + n) if it is None else par[:, bass.ds(i * mt + (PAR["norm"] + KT * r + n), 1)]
                act.wait_ge(s.sq_done, at(c + 1))
                nc.scalar.activation(g(x), g(x), ACT.Copy, scale=w).then_inc(s.x_w, 1)

        def rnorm_lo(dve, r, n, it=None):
            i, mt = (None, 0) if it is None else it[:2]
            c = KT * r + n
            g = lambda a: a[:, n, :] if it is None else a[:, bass.ds(i * mt + n, 1), :].rearrange("p o t -> p (o t)")
            w = col("norm", KT * r + n) if it is None else par[:, bass.ds(i * mt + (PAR["norm"] + KT * r + n), 1)]
            dve.wait_ge(s.h_hi_done, c + 1 if it is None else i * mt + (c + 1))
            nc.vector.scalar_tensor_tensor(g(h_lo), g(x), w, g(h_hi).bitcast(f32), ALU.mult,
                                           ALU.subtract).then_inc(s.h_lo_done, 1)

        OUT1 = (7, 0, 1, 6, 3, 4, 5, 2)

        def out1_part(pe, n, k0, k1):
            w_wait(pe, BO1 + n)
            for k in range(k0, k1):
                pe.wait_ge(s.y1_lod, k + 1)
                mm = mm3(B[OUT1[n]][:], w_hi[:, (BO1 + n) % RING, k * P:(k + 1) * P],
                         w_lo[:, (BO1 + n) % RING, k * P:(k + 1) * P], y1_hi[:, k, :], y1_lo[:, k, :], k == 0, k == KT - 1)
            if k1 == KT:
                mm.then_inc(s.block_done, 1)

        def out1_pe(pe):
            for n in range(3):
                out1_part(pe, n, KT - 1, KT)
            for n in range(3, KT):
                out1_part(pe, n, 0, KT)

        def out1_act(act):
            for n in range(KT):
                split_act(act, BO1 + n + 3)
                rnorm_act(act, 3, n, False)

        def out1_dve(dve):
            for n in range(KT):
                split_dve(dve, BO1 + n + 3)
                dve.wait_ge(s.block_done, BO1 + n + 1)
                nc.vector.tensor_tensor(x[:, n, :], x[:, n, :], B[OUT1[n]][:], ALU.add).then_inc(s.x_new, 1)
                rnorm_lo(dve, 3, n)


        PB = 3

        def at(v, it, m):
            return v if it is None else it * m + v

        def up_pe(pe, L, b0, j, it):
            for q in range(2):
                g = 2 * j + q
                w_wait(pe, b0 + g, it, 2 * PB)
                G_ = 2 * FT * L + g
                if it is not None or g >= 6:
                    pe.wait_ge(s.up_free, at(G_ - 5, it, 2 * PB))
                if j == 0 and it is None:
                    for k in range(KT):
                        if q == 0:
                            pe.wait_ge(s.h_lo_done, KT * (2 * L + 1) + k + 1)
                            mm = gemm(B[g % 6], b0 + g, k, k + 1, h_hi, h_lo, k == 0, k == KT - 1)
                    if q == 1:
                        mm = gemm(B[g % 6], b0 + g, 0, KT, h_hi, h_lo, True, True)
                else:
                    mm = gemm(B[g % 6], b0 + g, 0, KT, h_hi, h_lo, True, True)
                mm.then_inc(s.block_done, 1)
                if j == 0 and it is None and q == 0:
                    stat_pe(pe, 2 * L + 1, B[7])

        def fcol(L, j, it, q, tap):
            o = PAR["fc%d" % L] + (2 * j + q) * 3 + tap
            return par[:, o:o + 1] if it is None else par[:, bass.ds(it * (6 * PB) + o, 1)]

        def up_act(act, L, b0, j, it, tail):
            for q in range(2):
                g = 2 * j + q
                if not tail:
                    w_hi_of(act, b0 + g + 3, D, it, 2 * PB)
                else:
                    split_act(act, b0 + g + 3)
                G_ = 2 * FT * L + g
                u, t = (ug, tg) if q == 0 else (uv, tv)
                act.wait_ge(s.up_free, at(G_ + 1, it, 2 * PB))
                nc.scalar.activation(t[:, j % 3, :], u[:, 0:T], ACT.Copy, scale=fcol(L, j, it, q, 0)).then_inc(s.tap0, 1)
            J = FT * L + j
            act.wait_ge(s.tap1, at(4 * J + 2, it, 4 * PB))
            nc.scalar.activation(tg[:, j % 3, :], tg[:, j % 3, :], ACT.Silu).then_inc(s.silu_f, 1)
            act.wait_ge(s.prod, at(J + 1, it, PB))
            dst = p_hi[:, j, :] if it is None else p_hi[:, bass.ds(it * PB + j, 1), :].rearrange("p o t -> p (o t)")
            nc.scalar.activation(dst, tv[:, j % 3, :], ACT.Copy).then_inc(s.prod_hi, 1)

        def up_taps(dve, L, j, it, q):
            J = FT * L + j
            u, t = (ug, tg) if q == 0 else (uv, tv)
            n = 4 * J + 2 * q
            dve.wait_ge(s.tap0, at(2 * J + q + 1, it, 2 * PB))
            nc.vector.scalar_tensor_tensor(t[:, j % 3, :], u[:, 1:T + 1], fcol(L, j, it, q, 1), t[:, j % 3, :],
                                           ALU.mult, ALU.add).then_inc(s.tap1, 1)
            dve.wait_ge(s.tap1, at(n + 1, it, 4 * PB))
            nc.vector.scalar_tensor_tensor(t[:, j % 3, :], u[:, 2:T + 2], fcol(L, j, it, q, 2), t[:, j % 3, :],
                                           ALU.mult, ALU.add).then_inc(s.tap1, 1)

        def up_evac(dve, L, b0, j, it, q):
            g = 2 * j + q
            u = ug if q == 0 else uv
            dve.wait_ge(s.block_done, at(b0 + g + 1, it, 2 * PB))
            nc.vector.tensor_tensor(u[:, 2:], B[g % 6][:], rms[:], ALU.mult).then_inc(s.up_free, 1)

        def up_plo(dve, L, j, it):
            J = FT * L + j
            dve.wait_ge(s.prod_hi, at(J + 1, it, PB))
            g = lambda a: a[:, j, :] if it is None else a[:, bass.ds(it * PB + j, 1), :].rearrange("p o t -> p (o t)")
            nc.vector.tensor_tensor(g(p_lo), tv[:, j % 3, :], g(p_hi).bitcast(f32), ALU.subtract).then_inc(s.prod_lo, 1)

        def up_dve(dve, L, b0, j, it, tail):
            J = FT * L + j
            up_evac(dve, L, b0, j, it, 0)
            if not (j == 0 and it is None):
                up_plo(dve, L, j - 1, it)
            if tail:
                split_dve(dve, b0 + 2 * j + 3)
            else:
                w_lo_of(dve, b0 + 2 * j + 3, D, it, 2 * PB)
            up_taps(dve, L, j, it, 0)
            up_evac(dve, L, b0, j, it, 1)
            if tail:
                split_dve(dve, b0 + 2 * j + 4)
            else:
                w_lo_of(dve, b0 + 2 * j + 4, D, it, 2 * PB)
            up_taps(dve, L, j, it, 1)
            dve.wait_ge(s.silu_f, at(J + 1, it, PB))
            dve.wait_ge(s.tap1, at(4 * J + 4, it, 4 * PB))
            nc.vector.tensor_tensor(tv[:, j % 3, :], tg[:, j % 3, :], tv[:, j % 3, :], ALU.mult).then_inc(s.prod, 1)

        UP_FIRST = 1 + PB
        UP_ITERS = (FT - UP_FIRST) // PB - 1

        def up(eng, fn, L, b0):
            for j in range(UP_FIRST):
                fn(eng, L, b0, j, None)
            with eng.Fori(0, UP_ITERS) as it:
                for j in range(UP_FIRST, UP_FIRST + PB):
                    fn(eng, L, b0, j, it)
            for j in range(FT - PB, FT):
                fn(eng, L, b0, j, None)

        def down_pe(pe, L, r, b0, n, it):
            b = b0 + 3 * n
            for q, kts in enumerate(DOWN):
                w_wait(pe, b + q, it, 6)
                k0 = sum(DOWN[:q])
                pe.wait_ge(s.prod_lo, FT * L + k0 + kts)
                if q == 0:
                    pe.wait_ge(s.x_new, at(8 * (r - 1) + n - 1, it, 2))
                mm = gemm(B[6 + n % 2], b + q, 0, kts, p_hi, p_lo, q == 0, q == 2, a0=k0)
                mm.then_inc(s.block_done, 1)

        def down_act(act, L, r, b0, n, it):
            b = b0 + 3 * n
            for q in range(3):
                if it is None:
                    split_act(act, b + q + 3)
                else:
                    w_hi_of(act, b + q + 3, DOWN[q] * P, it, 6)
            rnorm_act(act, r, n, r == 4, None if it is None else (it, 2))

        def down_dve(dve, L, r, b0, n, it):
            b = b0 + 3 * n
            for q in range(3):
                if q == 2:
                    resid_dve(dve, r, n, b + 2, None if it is None else (it, 2, 6))
                if it is None:
                    split_dve(dve, b + q + 3)
                else:
                    w_lo_of(dve, b + q + 3, DOWN[q] * P, it, 6)
            if r != 4:
                rnorm_lo(dve, r, n, None if it is None else (it, 2))

        def down(eng, fn, L, r, b0):
            with eng.Fori(0, KT // 2 - 1) as it:
                for n in range(2):
                    fn(eng, L, r, b0, n, it)
            for n in range(KT - 2, KT):
                fn(eng, L, r, b0, n, None)

        PLACE = {0: (0, 0), 3: (1, 0), 1: (1, 128), 2: (2, 0)}
        BASE = (0, 512, 1024)
        WID = (512, 512, 256)

        def kcols(kb):
            bank, c0 = PLACE[kb]
            return BASE[bank] + c0, T - P * kb

        def own(e):
            return slice(64 * e, 64 * e + 64)

        def other(e):
            return own(1 - e)

        def proj_pe(pe, p, kind):
            b = BQ + 3 * p + kind
            bank = B[7 if kind == 1 else 6]
            w_wait(pe, b)
            if kind == 0:
                if p == 0:
                    pe.wait_ge(s.x_new, 2 * KT - 1)
                else:
                    pe.wait_ge(s.v_f, p)
            elif kind == 1:
                if p == 0:
                    pe.wait_ge(s.x_new, 2 * KT)
                else:
                    pe.wait_ge(s.v_lod, p)
                if p >= 2:
                    pe.wait_ge(s.y_sum, 2 * (p - 2) + 1)
            else:
                pe.wait_ge(s.q_f, p + 1)
                if p >= 2:
                    pe.wait_ge(s.y_sum, 2 * (p - 2) + 2)
            if kind == 0 and p == 0:
                for k in range(KT):
                    pe.wait_ge(s.h_lo_done, KT * 2 + k + 1)
                    mm = gemm(bank, b, k, k + 1, h_hi, h_lo, k == 0, k == KT - 1)
            else:
                mm = gemm(bank, b, 0, KT, h_hi, h_lo, True, True)
            mm.then_inc(s.block_done, 1)

        def vt_pe(pe, p):
            pe.wait_ge(s.v_f, p + 1)
            pe.wait_ge(s.k_f, p + 1)
            for c in range(NC):
                mm = nc.tensor.transpose(B[7][:, c * P:(c + 1) * P], vT[:, c * P:(c + 1) * P], cm(IDENT))
            mm.then_inc(s.vt2_mm, 1)

        def proj_dve(dve, p, kind):
            b = BQ + 3 * p + kind
            dve.wait_ge(s.block_done, b + 1)
            if kind == 0:
                if p:
                    dve.wait_ge(s.k_lod, p)
                    dve.wait_ge(s.k_twice, p)
                nc.vector.scalar_tensor_tensor(pf[:], B[6][:], 0.125, rms[:], ALU.mult, ALU.mult).then_inc(s.q_f, 1)
                dve.wait_ge(s.q_hid, p + 1)
                for e in range(2):
                    op = nc.vector.tensor_tensor(qs[other(e), p % 2, e, :], pf[own(e), :], qs[own(e), p % 2, e, :].bitcast(f32),
                                                 ALU.subtract)
                op.then_inc(s.q_lod, 1)
            elif kind == 1:
                dve.wait_ge(s.q_lod, p + 1)
                nc.vector.tensor_tensor(pf[:], B[7][:], rms[:], ALU.mult).then_inc(s.k_f, 1)
                dve.wait_ge(s.k_hid, p + 1)
                for e in range(2):
                    op = nc.vector.tensor_tensor(k_lo[own(e), p % 2, :], pf[own(e), :], ks[own(e), p % 2, e, :].bitcast(f32),
                                                 ALU.subtract)
                op.then_inc(s.k_lod, 1)
            else:
                if p:
                    dve.wait_ge(s.vt2_mm, p)
                nc.vector.tensor_tensor(vT[:], B[6][:], rms[:], ALU.mult).then_inc(s.v_f, 1)

        def proj_act(act, p, kind):
            if kind == 0:
                act.wait_ge(s.q_f, p + 1)
                for e in range(2):
                    op = nc.scalar.activation(qs[own(e), p % 2, e, :], pf[own(e), :], ACT.Copy)
                op.then_inc(s.q_hid, 1)
            elif kind == 1:
                act.wait_ge(s.k_f, p + 1)
                for e in range(2):
                    op = nc.scalar.activation(ks[own(e), p % 2, e, :], pf[own(e), :], ACT.Copy)
                op.then_inc(s.k_hid, 1)

        def k_twice_pool(pool, p):
            pool.wait_ge(s.k_hid, p + 1)
            for e in range(2):
                op = nc.gpsimd.tensor_scalar(ks[other(e), p % 2, e, :], pf[own(e), :], 1.0, None, ALU.mult)
            op.then_inc(s.k_twice, 1)

        def v_part(p, e, lo):
            return v_hl[:, p % 2, :, e, 64 * lo:64 * lo + 64]

        def v_bank(e):
            return B[7][:].rearrange("p (c d) -> p c d", c=NC)[:, :, 64 * e:64 * e + 64]

        def vt_act(act, p):
            act.wait_ge(s.vt2_mm, p + 1)
            for e in range(2):
                nc.scalar.activation(v_part(p, e, 0), v_bank(e), ACT.Copy).then_inc(s.v_hid, 1)

        def vt_dve(dve, p):
            for e in range(2):
                dve.wait_ge(s.v_hid, 2 * p + 2)
                op = nc.vector.tensor_tensor(v_part(p, e, 1), v_bank(e), v_part(p, e, 0).bitcast(f32), ALU.subtract)
            op.then_inc(s.v_lod, 1)

        def z_pe(pe, p, e):
            u = 2 * p + e
            pe.wait_ge(s.k_lod, p + 1)
            pe.wait_ge(s.k_twice, p + 1)
            if u >= 2:
                pe.wait_ge(s.att_done, 3 * (u - 1))
            if u == 0:
                pe.wait_ge(s.consts_r, 5)
            for bank, kbs in enumerate(((0,), (3, 1), (2,))):
                first = True
                for kb in kbs:
                    c0, w = PLACE[kb][1], T - P * kb
                    out = B[3 * e + bank]
                    kk, qq = slice(P * kb, P * kb + P), slice(P * kb, T)
                    nc.tensor.matmul(out[:, c0:c0 + w], k_lo[own(e), p % 2, kk], qs[own(e), p % 2, e, qq],
                                     start=first, stop=False, skip_group_check=True)
                    nc.tensor.matmul(out[:, c0:c0 + w], ks[:, p % 2, e, kk], qs[:, p % 2, e, qq],
                                     start=False, stop=False, skip_group_check=True)
                    first = False
                n = P * len(kbs)
                nc.tensor.matmul(out[:, 0:n], identr[:], negm[:, 0:n], start=False, stop=True,
                                 skip_group_check=True).then_inc(s.z_mm, 1)

        def cum_pe(pe, p, e):
            u = 2 * p + e
            pe.wait_ge(s.sp_lod, 3 * u + 3)
            for bank, kbs in enumerate(((0,), (3, 1), (2,))):
                for kb in kbs:
                    out, c0 = B[3 * e + bank], PLACE[kb][1]
                    for kb2 in range(kb, NC):
                        o, w = kcols(kb2)
                        d = c0 + P * (kb2 - kb)
                        for src in (s_lo, s_hi):
                            mm = nc.tensor.matmul(out[:, d:d + w], (ntri if kb2 == kb else nones)[:], src[:, e, o:o + w],
                                                  start=False, stop=False, skip_group_check=True)
                mm.then_inc(s.cum_mm, 1)

        def sp_act(act, p, e):
            u = 2 * p + e
            for bank in range(3):
                n = 3 * u + bank
                o, w = BASE[bank], WID[bank]
                act.wait_ge(s.z_mm, n + 1)
                if u >= 2:
                    act.wait_ge(s.att_lod, 3 * (u - 1))
                nc.scalar.activation(t_[:, e, o:o + w], B[3 * e + bank][:, 0:w], ACT.Abs).then_inc(s.za_done, 1)
            for bank in range(3):
                n = 3 * u + bank
                o, w = BASE[bank], WID[bank]
                act.wait_ge(s.za_done, n + 1)
                nc.scalar.activation(t_[:, e, o:o + w], t_[:, e, o:o + w], ACT.Exp, scale=-1.0).then_inc(s.ze_done, 1)
            for bank in range(3):
                n = 3 * u + bank
                o, w = BASE[bank], WID[bank]
                act.wait_ge(s.ze_done, n + 1)
                nc.scalar.activation(t_[:, e, o:o + w], t_[:, e, o:o + w], ACT.Ln, bias=1.0).then_inc(s.zl_done, 1)

        def sp2_dve(dve, p, e):
            u = 2 * p + e
            for bank in range(3):
                n = 3 * u + bank
                o, w = BASE[bank], WID[bank]
                dve.wait_ge(s.zl_done, n + 1)
                nc.vector.scalar_tensor_tensor(t_[:, e, o:o + w], B[3 * e + bank][:, 0:w], 0.0, t_[:, e, o:o + w],
                                               ALU.max, ALU.add).then_inc(s.sp_done, 1)

        def split_s_act(act, p, e, src_sem, dst_sem):
            u = 2 * p + e
            for bank in range(3):
                n = 3 * u + bank
                o, w = BASE[bank], WID[bank]
                act.wait_ge(src_sem, n + 1)
                nc.scalar.activation(s_hi[:, e, o:o + w], t_[:, e, o:o + w], ACT.Copy).then_inc(dst_sem, 1)

        def split_s_dve(dve, p, e, hi_sem, lo_sem):
            u = 2 * p + e
            for bank in range(3):
                n = 3 * u + bank
                o, w = BASE[bank], WID[bank]
                dve.wait_ge(hi_sem, n + 1)
                nc.vector.tensor_tensor(s_lo[:, e, o:o + w], t_[:, e, o:o + w], s_hi[:, e, o:o + w].bitcast(f32),
                                        ALU.subtract).then_inc(lo_sem, 1)

        def att_act(act, p, e):
            u = 2 * p + e
            for bank in range(3):
                o, w = BASE[bank], WID[bank]
                act.wait_ge(s.cum_mm, 3 * u + 3)
                nc.scalar.activation(t_[:, e, o:o + w], B[3 * e + bank][:, 0:w], ACT.Exp).then_inc(s.att_done, 1)

        def av_bank(p, e):
            return B[((7, 6), (6, 2))[p == PAIRS - 1][e]]

        def av_pe(pe, p, e):
            pe.wait_ge(s.v_lod, min(p + 2, PAIRS))
            pe.wait_ge(s.att_lod, 3 * (2 * p + e) + 3)
            if e == 0 and p == PAIRS - 1:
                pe.wait_ge(s.y_sum, 2 * p)
            if e == 1:
                pe.wait_ge(s.q_f, min(p + 3, PAIRS))
            for kb in range(NC):
                o, w = kcols(kb)
                nc.tensor.matmul(av_bank(p, e)[:, P * kb:T], v_hl[:, p % 2, kb, e, :], s_hi[:, e, o:o + w], start=(kb == 0),
                                 stop=False, skip_group_check=True)
                mm = nc.tensor.matmul(av_bank(p, e)[0:64, P * kb:T], v_hl[:, p % 2, kb, e, 0:64], s_lo[:, e, o:o + w],
                                      start=False, stop=(kb == NC - 1), skip_group_check=True)
            mm.then_inc(s.av_mm, 1)

        def y_sum_act(act, p, e):
            act.wait_ge(s.av_mm, 2 * p + e + 1)
            if p:
                act.wait_ge(s.y_sum, 2 * p + e - 1)
            nc.scalar.activation(yt[0:64, e, :], av_bank(p, e)[64:128, :], ACT.Copy).then_inc(s.yt_done, 1)

        def y_sum_dve(dve, p, e):
            if p:
                dve.wait_ge(s.y1_lod, p)
            dve.wait_ge(s.yt_done, 2 * p + e + 1)
            nc.vector.tensor_tensor(yf[own(e), :], av_bank(p, e)[0:64, :], yt[0:64, e, :], ALU.add).then_inc(s.y_sum, 1)

        def y1_act(act, p):
            act.wait_ge(s.y_sum, 2 * p + 2)
            nc.scalar.activation(y1_hi[:, p, :], yf[:], ACT.Copy).then_inc(s.y1_hid, 1)

        def y1_dve(dve, p):
            dve.wait_ge(s.y1_hid, p + 1)
            nc.vector.tensor_tensor(y1_lo[:, p, :], yf[:], y1_hi[:, p, :].bitcast(f32), ALU.subtract).then_inc(s.y1_lod, 1)

        def t_pe(pe):
            for kind in range(3):
                proj_pe(pe, 0, kind)
                if kind == 0:
                    stat_pe(pe, 2, B[5])
            vt_pe(pe, 0)
            for p in range(PAIRS - 1):
                z_pe(pe, p, 0)
                if p:
                    av_pe(pe, p - 1, 0)
                proj_pe(pe, p + 1, 0)
                z_pe(pe, p, 1)
                if p:
                    av_pe(pe, p - 1, 1)
                proj_pe(pe, p + 1, 1)
                cum_pe(pe, p, 0)
                proj_pe(pe, p + 1, 2)
                cum_pe(pe, p, 1)
                vt_pe(pe, p + 1)
            p = PAIRS - 1
            z_pe(pe, p, 0)
            av_pe(pe, p - 1, 0)
            z_pe(pe, p, 1)
            av_pe(pe, p - 1, 1)
            pe.wait_ge(s.y_sum, 2 * p - 1)
            out1_part(pe, 0, 0, PAIRS - 2)
            cum_pe(pe, p, 0)
            out1_part(pe, 0, PAIRS - 2, PAIRS - 1)
            cum_pe(pe, p, 1)
            pe.wait_ge(s.att_done, 3 * (2 * p + 1))
            out1_part(pe, 1, 0, PAIRS - 1)
            av_pe(pe, p, 0)
            av_pe(pe, p, 1)
            out1_part(pe, 2, 0, PAIRS - 1)

        def t_act(act):
            for dst, i, sc in ((ntri[:], NTRI, 1.0), (nones[:], ONES, -1.0), (negm[:, 0:P], NEG, 1.0), (negm[:, P:], NEG, 1.0),
                               (identr[:], IDENT, 1.0)):
                nc.scalar.activation(dst, cm(i), ACT.Copy, scale=sc).then_inc(s.consts_r, 1)
            stat_act(act, 2, B[5])
            for kind in range(3):
                split_act(act, BQ + kind + 3)
                proj_act(act, 0, kind)
            vt_act(act, 0)
            for p in range(PAIRS):
                nxt = p + 1 < PAIRS
                if p:
                    split_s_act(act, p - 1, 1, s.att_done, s.att_hid)
                sp_act(act, p, 0)
                if p:
                    y_sum_act(act, p - 1, 0)
                if nxt:
                    split_act(act, BQ + 3 * (p + 1) + 3)
                    proj_act(act, p + 1, 0)
                if p:
                    y_sum_act(act, p - 1, 1)
                split_s_act(act, p, 0, s.sp_done, s.sp_hid)
                if p:
                    y1_act(act, p - 1)
                sp_act(act, p, 1)
                if nxt:
                    proj_act(act, p + 1, 1)
                split_s_act(act, p, 1, s.sp_done, s.sp_hid)
                if nxt:
                    split_act(act, BQ + 3 * (p + 1) + 4)
                att_act(act, p, 0)
                split_s_act(act, p, 0, s.att_done, s.att_hid)
                if nxt:
                    split_act(act, BQ + 3 * (p + 1) + 5)
                    vt_act(act, p + 1)
                att_act(act, p, 1)
            split_s_act(act, PAIRS - 1, 1, s.att_done, s.att_hid)
            y_sum_act(act, PAIRS - 1, 0)
            y_sum_act(act, PAIRS - 1, 1)
            y1_act(act, PAIRS - 1)

        def t_dve(dve):
            dve.wait_ge(s.rms_done, 3)
            for kind in range(3):
                proj_dve(dve, 0, kind)
                split_dve(dve, BQ + kind + 3)
            vt_dve(dve, 0)
            for p in range(PAIRS):
                nxt = p + 1 < PAIRS
                if p:
                    split_s_dve(dve, p - 1, 1, s.att_hid, s.att_lod)
                sp2_dve(dve, p, 0)
                if p:
                    y_sum_dve(dve, p - 1, 0)
                if nxt:
                    proj_dve(dve, p + 1, 0)
                    split_dve(dve, BQ + 3 * (p + 1) + 3)
                if p:
                    y_sum_dve(dve, p - 1, 1)
                split_s_dve(dve, p, 0, s.sp_hid, s.sp_lod)
                if p:
                    y1_dve(dve, p - 1)
                sp2_dve(dve, p, 1)
                if nxt:
                    proj_dve(dve, p + 1, 1)
                split_s_dve(dve, p, 1, s.sp_hid, s.sp_lod)
                if nxt:
                    split_dve(dve, BQ + 3 * (p + 1) + 4)
                    proj_dve(dve, p + 1, 2)
                split_s_dve(dve, p, 0, s.att_hid, s.att_lod)
                if nxt:
                    split_dve(dve, BQ + 3 * (p + 1) + 5)
                    vt_dve(dve, p + 1)
            split_s_dve(dve, PAIRS - 1, 1, s.att_hid, s.att_lod)
            y_sum_dve(dve, PAIRS - 1, 0)
            y_sum_dve(dve, PAIRS - 1, 1)
            y1_dve(dve, PAIRS - 1)

        block = ctx.enter_context(nc.Block())

        @block.sync
        def _(sp):
            NORMS = 5 * KT
            sp.dma_start(par[:, 0:NORMS], par_d[:, 0:NORMS]).then_inc(s.norms_in, 16)
            for k in range(KT):
                sp.dma_start(x[:, k, :], xT[:, k, :]).then_inc(x_in[k], 16)
                if k == 0:
                    w_load(sp, w_ab, 0, 64)
                if k == 3:
                    w_load(sp, w_in0[0], 1, D)
            w_load(sp, w_in0[1], 2, D)
            sp.dma_start(par[:, NORMS:], par_d[:, NORMS:]).then_inc(s.par_in, 16)
            sp.dma_start(const[:], const_d).then_inc(s.const_in, 16)
            for b in range(3, NB0):
                w_load(sp, w_in0[b - 1], b, D)

            def out_loads(dram, b0):
                for n in range(KT):
                    w_load(sp, dram[n], b0 + n, D)

            def up_loads(dram, b0):
                for g in range(2):
                    w_load(sp, dram[g], b0 + g, D)
                with sp.Fori(0, (2 * FT - 2) // RING) as i:
                    for j in range(RING):
                        w_load(sp, dram[bass.ds(i * RING + (2 + j), 1)].rearrange("o p n -> (o p) n"), b0 + 2 + j, D, i, RING)

            def down_loads(dram, b0):
                with sp.Fori(0, KT) as i:
                    for q, kts in enumerate(DOWN):
                        k0 = sum(DOWN[:q]) * P
                        w_load(sp, dram[bass.ds(i, 1), :, k0:k0 + kts * P].rearrange("o p n -> (o p) n"), b0 + q, kts * P, i, 3)

            for j in range(NBO0):
                w_load(sp, w_out0[j], BO0 + j, D // 2)
            up_loads(w_up0, BU0)
            down_loads(w_dn0, BD0)
            for b in range(NBQ):
                w_load(sp, w_qkv[b], BQ + b, D)
            out_loads(w_out1, BO1)
            up_loads(w_up1, BU1)
            down_loads(w_dn1, BD1)
            for k in range(KT):
                sp.wait_ge(s.out_f, k + 1)
                sp.dma_start(outT[:, k, :], x[:, k, :]).then_inc(s.out_w, 16)
            sp.wait_ge(s.out_w, 16 * KT)


        @block.gpsimd
        def _(pool):
            nc.gpsimd.memset(eps[:, 0:1], 1e-6)
            nc.gpsimd.memset(eps[:, 1:2], 1e-5).then_inc(s.ones_set, 1)
            a_pool(pool)
            norm_pool(pool, 1)
            norm_pool(pool, 2)
            for p in range(PAIRS):
                k_twice_pool(pool, p)
            norm_pool(pool, 3)
            norm_pool(pool, 4, KT - 1)

        @block.scalar
        def _(act):
            a_act(act)
            out0_act(act)
            stat_act(act, 1, B[7])
            up(act, lambda e, L, b0, j, it: up_act(e, L, b0, j, it, it is None), 0, BU0)
            down(act, down_act, 0, 2, BD0)
            t_act(act)
            out1_act(act)
            stat_act(act, 3, B[7])
            up(act, lambda e, L, b0, j, it: up_act(e, L, b0, j, it, it is None), 1, BU1)
            act.preload_act_table_set("natural_log_exp_and_others")
            down(act, down_act, 1, 4, BD1)
            stat_act(act, 4, B[5])

        @block.vector
        def _(dve):
            a_dve(dve)
            out0_dve(dve)

            def ffn_up(L, b0):
                dve.wait_ge(s.rms_done, 2 * L + 2)
                nc.vector.memset(ug[:, 0:2], 0.0).then_inc(s.halo_f, 1)
                nc.vector.memset(uv[:, 0:2], 0.0).then_inc(s.halo_f, 1)
                dve.wait_ge(s.halo_f, 2 * L + 2)
                up(dve, lambda e, L, b0, j, it: up_dve(e, L, b0, j, it, it is None), L, b0)
                up_plo(dve, L, FT - 1, None)
            ffn_up(0, BU0)
            down(dve, down_dve, 0, 2, BD0)
            t_dve(dve)
            out1_dve(dve)
            ffn_up(1, BU1)
            down(dve, down_dve, 1, 4, BD1)
            dve.wait_ge(s.rms_done, 5)
            dve.wait_ge(s.x_w, KT)
            for k in range(KT):
                nc.vector.tensor_tensor(x[:, k, :], x[:, k, :], rms[:], ALU.mult).then_inc(s.out_f, 1)

        @block.tensor
        def _(pe):
            a_pe(pe)
            out0_pe(pe)
            up(pe, up_pe, 0, BU0)
            down(pe, down_pe, 0, 2, BD0)
            t_pe(pe)
            out1_pe(pe)
            up(pe, up_pe, 1, BU1)
            down(pe, down_pe, 1, 4, BD1)
            last_stat_pe(pe, 4, B[5])


def _blocks(np, w, cols):
    k = w.shape[0] // P
    a = w.reshape(k, P, w.shape[1] // P, P) if w.shape[1] % P == 0 else None
    return np.ascontiguousarray(a[:, :, cols, :].transpose(2, 1, 0, 3).reshape(len(cols), P, k * P))


def _consts(np):
    i = np.arange(P)
    row, c = i[:, None], i[None, :]
    m = [row == c, row <= c, row > c, np.ones((P, P))]
    for l in range(LEVELS):
        b = 1 << l
        m.append((row // (2 * b) == c // (2 * b)) & ((row // b) % 2 == 0) & ((c // b) % 2 == 1))
    m.append(-1.0 * (row >= c))
    m.append(-(2.0 ** 100) * (row >= c))
    return np.ascontiguousarray(np.stack([np.asarray(a, np.float32) for a in m]).transpose(1, 0, 2))


def _arrays(np, inputs):
    g = {k: np.asarray(v) for k, v in inputs.items()}
    tile = lambda v: v.reshape(-1, P).T
    w0 = g["w_in0"][0]
    c = CA
    order = [t for i in range(CA) for t in (c + i, i)]
    for h in range(NH):
        order += [2 * c + NH + h, 2 * c + h, 2 * c + 2 * NH + h]
    order += [2 * c + 3 * NH + h for h in range(NH)]
    main = w0[:, :24 * P]
    w_ab = np.ascontiguousarray(w0[:, 24 * P:].reshape(KT, P, 8).transpose(1, 0, 2).reshape(P, 64))
    pairs = [t for j in range(FT) for t in (j, FT + j)]
    qkv = [t for p in range(PAIRS) for t in (p, PAIRS + p, 2 * PAIRS + p)]
    par = [tile(g["mix0_norm"][0]), tile(g["ffn_norm"][0]), tile(g["mix1_norm"][0]), tile(g["ffn_norm"][1]),
           tile(g["final_norm"]), tile(g["a_dw_b"][0]), tile(g["a_ln_w"][0]), tile(g["a_ln_b"][0]),
           tile(g["gdn_onorm_w"][0]),
           g["gdn_conv_w"][0].reshape(4, 12, P).transpose(2, 1, 0).reshape(P, 48),
           g["a_dw_w"][0].reshape(C31, CA, P).transpose(2, 1, 0).reshape(P, CA * C31)]
    for L in range(2):
        par.append(g["ffn_conv_w"][L].reshape(3, 2 * FT, P)[:, pairs, :].transpose(2, 1, 0).reshape(P, 6 * FT))
    par += [np.broadcast_to(g[n][0][None, :], (P, NH)) for n in ("gdn_dt_bias", "gdn_a_log")]
    down = lambda w: np.ascontiguousarray(w.reshape(FT, P, KT, P).transpose(2, 1, 0, 3).reshape(KT, P, FT * P))
    return {
        "xT": np.ascontiguousarray(g["x"][0].T.reshape(KT, P, T).transpose(1, 0, 2)),
        "w_ab": w_ab,
        "w_in0": _blocks(np, main, order),
        "w_out0": np.concatenate([_blocks(np, g["w_out0"][0][r], list(range(KT))) for r in (slice(CA * P, D), slice(0, CA * P))]),
        "w_up0": _blocks(np, g["w_up"][0], pairs),
        "w_dn0": down(g["w_down"][0]),
        "w_qkv": _blocks(np, g["w_qkv1"][0], qkv),
        "w_out1": _blocks(np, g["w_out1"][0], list(range(KT))),
        "w_up1": _blocks(np, g["w_up"][1], pairs),
        "w_dn1": down(g["w_down"][1]),
        "par": np.ascontiguousarray(np.concatenate(par, axis=1)),
        "const": _consts(np),
    }


def kernel(**inputs):
    import numpy as np
    import concourse.bacc as bacc
    from concourse import mybir as mb
    from concourse.bass_utils import run_bass_kernel_spmd
    arrays = {"in_" + n: a for n, a in _arrays(np, inputs).items()}
    nc = bacc.Bacc("TRN2", target_bir_lowering=False, num_devices=1)
    args = [nc.dram_tensor(n, a.shape, mb.dt.from_np(a.dtype), kind="ExternalInput").ap() for n, a in arrays.items()]
    args.append(nc.dram_tensor("outT", (P, KT, T), mb.dt.float32, kind="ExternalOutput").ap())
    trunk(nc, *args)
    r = run_bass_kernel_spmd(nc, [arrays], core_ids=[0])
    out = r.results[0]["outT"]
    return np.ascontiguousarray(out.transpose(1, 0, 2).reshape(D, T).T)[None]
```
